# Optimizing a Trainium2 kernel written in Bass

```python
import jax, jax.numpy as jnp
from jax import lax
import numpy as np
import math
import jax
import jax.numpy as jnp

D_MODEL = 1024
BATCH = 1
SEQ = 512
DEPTH = 2

N_MIXERS = 2
N_A = (DEPTH + 1) // 2
N_B = DEPTH // 2
D_FF = 2816
LRU_WIDTH = D_MODEL
LRU_HEADS = 16
LRU_HEAD_DIM = LRU_WIDTH // LRU_HEADS
LRU_C = 8.0
CONV_WIDTH = 4
SG_WIDTH = D_MODEL
SG_HEADS = 8
SG_HEAD_DIM = SG_WIDTH // SG_HEADS
CHUNK = 128
NORM_EPS = 1e-6


def rms_norm(x, g):
    xf = x.astype(jnp.float32)
    y = xf * lax.rsqrt(jnp.mean(xf * xf, axis=-1, keepdims=True) + NORM_EPS)
    return (y * g.astype(jnp.float32)).astype(x.dtype)

def swiglu(x, w_in, w_out):
    g, u = jnp.split(x @ w_in, 2, axis=-1)
    return (jax.nn.silu(g) * u) @ w_out

def causal_depthwise_conv(x, w, b):
    k_width = w.shape[0]
    s = x.shape[1]
    xp = jnp.pad(x, ((0, 0), (k_width - 1, 0), (0, 0)))
    out = b + xp[:, 0:s] * w[0]
    for k in range(1, k_width):
        out = out + xp[:, k:k + s] * w[k]
    return out

def block_diag_linear(x, w, b):
    bsz, s, _ = x.shape
    h, dh, _ = w.shape
    xh = x.reshape(bsz, s, h, dh)
    return (jnp.einsum('bshi,hij->bshj', xh, w) + b).reshape(bsz, s, h * dh)

def rg_lru(x, w_a, b_a, w_x, b_x, lam):
    f32 = jnp.float32
    xf = x.astype(f32)
    gate_a = jax.nn.sigmoid(block_diag_linear(xf, w_a.astype(f32), b_a.astype(f32)))
    gate_x = jax.nn.sigmoid(block_diag_linear(xf, w_x.astype(f32), b_x.astype(f32)))
    log_a = -LRU_C * gate_a * jax.nn.softplus(-lam.astype(f32))
    a = jnp.exp(log_a)
    mult = jnp.sqrt(-jnp.expm1(2.0 * log_a))
    bx = xf * gate_x * mult

    def combine(left, right):
        a_l, b_l = left
        a_r, b_r = right
        return a_l * a_r, a_r * b_l + b_r

    _, h = lax.associative_scan(combine, (a, bx), axis=1)
    return h.astype(x.dtype)

def recurrent_mixer(x, w_in, conv_w, conv_b, gate_a_w, gate_a_b, gate_x_w, gate_x_b, lam, w_out):
    y, r = jnp.split(x @ w_in, 2, axis=-1)
    y = jax.nn.gelu(y)
    r = causal_depthwise_conv(r, conv_w, conv_b)
    h = rg_lru(r, gate_a_w, gate_a_b, gate_x_w, gate_x_b, lam)
    return (y * h) @ w_out

def spatial_gating_mixer(x, w_in, v_norm, w_s, b_s, w_out):
    bsz, s, _ = x.shape
    u, v = jnp.split(jax.nn.gelu(x @ w_in), 2, axis=-1)
    v = rms_norm(v, v_norm)
    h, p, _ = w_s.shape
    c = v.shape[-1] // h
    vc = v.reshape(bsz, s // p, p, h, c)
    causal = jnp.tril(jnp.ones((p, p), dtype=bool))
    ws = jnp.where(causal[None], w_s, jnp.zeros_like(w_s))
    sg = jnp.einsum('hpq,bnqhc->bnphc', ws, vc) + b_s.T[:, :, None]
    sg = sg.reshape(bsz, s, h * c)
    return (u * sg) @ w_out

def first_inputs(seed: int = 0) -> dict:
    key = jax.random.key(seed)
    ks = jax.random.split(key, 32)
    f32 = jnp.float32

    def nrm(k, shape, fan_in):
        return jax.random.normal(k, shape, f32) * (fan_in ** -0.5)

    def gain(k, shape):
        return 1.0 + 0.05 * jax.random.normal(k, shape, f32)

    def small(k, shape):
        return 0.01 * jax.random.normal(k, shape, f32)

    x = jax.random.normal(ks[0], (BATCH, SEQ, D_MODEL), f32)

    a0 = jax.random.uniform(ks[14], (N_A, LRU_WIDTH), f32, 0.9, 0.999)
    p0 = a0 ** (1.0 / LRU_C)
    rec_lambda = jnp.log(p0) - jnp.log1p(-p0)

    return {
        "x": x,
        "ffn1_norm": gain(ks[1], (DEPTH, D_MODEL)),
        "ffn1_w_in": nrm(ks[2], (DEPTH, D_MODEL, 2 * D_FF), D_MODEL),
        "ffn1_w_out": nrm(ks[3], (DEPTH, D_FF, D_MODEL), D_FF),
        "mix_norm": gain(ks[4], (DEPTH, D_MODEL)),
        "ffn2_norm": gain(ks[5], (DEPTH, D_MODEL)),
        "ffn2_w_in": nrm(ks[6], (DEPTH, D_MODEL, 2 * D_FF), D_MODEL),
        "ffn2_w_out": nrm(ks[7], (DEPTH, D_FF, D_MODEL), D_FF),
        "rec_w_in": nrm(ks[8], (N_A, D_MODEL, 2 * LRU_WIDTH), D_MODEL),
        "rec_conv_w": nrm(ks[9], (N_A, CONV_WIDTH, LRU_WIDTH), CONV_WIDTH),
        "rec_conv_b": small(ks[10], (N_A, LRU_WIDTH)),
        "rec_gate_a_w": nrm(ks[11], (N_A, LRU_HEADS, LRU_HEAD_DIM, LRU_HEAD_DIM), LRU_HEAD_DIM),
        "rec_gate_a_b": small(ks[12], (N_A, LRU_HEADS, LRU_HEAD_DIM)),
        "rec_gate_x_w": nrm(ks[13], (N_A, LRU_HEADS, LRU_HEAD_DIM, LRU_HEAD_DIM), LRU_HEAD_DIM),
        "rec_gate_x_b": small(ks[15], (N_A, LRU_HEADS, LRU_HEAD_DIM)),
        "rec_lambda": rec_lambda,
        "rec_w_out": nrm(ks[16], (N_A, LRU_WIDTH, D_MODEL), LRU_WIDTH),
        "sg_w_in": nrm(ks[17], (N_B, D_MODEL, 2 * SG_WIDTH), D_MODEL),
        "sg_v_norm": gain(ks[18], (N_B, SG_WIDTH)),
        "sg_w_s": nrm(ks[19], (N_B, SG_HEADS, CHUNK, CHUNK), CHUNK),
        "sg_b_s": 1.0 + 0.1 * jax.random.normal(ks[20], (N_B, SG_HEADS, CHUNK), f32),
        "sg_w_out": nrm(ks[21], (N_B, SG_WIDTH, D_MODEL), SG_WIDTH),
        "final_norm": gain(ks[22], (D_MODEL,)),
    }

def first_block(x, ffn1_norm, ffn1_w_in, ffn1_w_out, mix_norm, ffn2_norm, ffn2_w_in, ffn2_w_out,
              rec_w_in, rec_conv_w, rec_conv_b, rec_gate_a_w, rec_gate_a_b, rec_gate_x_w, rec_gate_x_b,
              rec_lambda, rec_w_out, sg_w_in, sg_v_norm, sg_w_s, sg_b_s, sg_w_out, final_norm):
    h = x
    for i in range(DEPTH):
        h = h + 0.5 * swiglu(rms_norm(h, ffn1_norm[i]), ffn1_w_in[i], ffn1_w_out[i])
        hn = rms_norm(h, mix_norm[i])
        j = i // N_MIXERS
        if i % N_MIXERS == 0:
            m = recurrent_mixer(hn, rec_w_in[j], rec_conv_w[j], rec_conv_b[j], rec_gate_a_w[j], rec_gate_a_b[j],
                                rec_gate_x_w[j], rec_gate_x_b[j], rec_lambda[j], rec_w_out[j])
        else:
            m = spatial_gating_mixer(hn, sg_w_in[j], sg_v_norm[j], sg_w_s[j], sg_b_s[j], sg_w_out[j])
        h = h + m
        h = h + 0.5 * swiglu(rms_norm(h, ffn2_norm[i]), ffn2_w_in[i], ffn2_w_out[i])
    return rms_norm(h, final_norm)


DEPTH_2 = 1

N_MEM = 256
BRANCH_W = D_MODEL // 2
N_BRANCH = 3
MIX_W = N_BRANCH * BRANCH_W

FOX_HD = 64
FOX_HEADS = BRANCH_W // FOX_HD
FOX_W = FOX_HEADS * FOX_HD
Q_BLOCK = 128
FOX_FBIAS_OFFSET = 3.0

S5_W = BRANCH_W
S5_GROUP = 16
S5_GROUPS = S5_W // S5_GROUP
S5_STATE = 64

HG_DK = 128
HG_DV = 128
HG_HEADS = BRANCH_W // HG_DV
HG_W = HG_HEADS * HG_DV
HG_CHUNK = 64

X_HEADS = 4
X_HD = D_MODEL // X_HEADS

D_FF_2 = ((8 * D_MODEL + 3 * 256 - 1) // (3 * 256)) * 256

IN_SIZES = (FOX_W, FOX_W, FOX_W, FOX_HEADS, S5_W, HG_HEADS * HG_DK, HG_HEADS * HG_DK, HG_W, HG_W, N_BRANCH * D_MODEL)
IN_COLS = sum(IN_SIZES)
EPS = 1e-6


def rmsnorm(x, g):
    xf = x.astype(jnp.float32)
    y = xf * lax.rsqrt(jnp.mean(xf * xf, axis=-1, keepdims=True) + EPS)
    return (y * g.astype(jnp.float32)).astype(x.dtype)

def _split_points(sizes):
    pts, acc = [], 0
    for s in sizes[:-1]:
        acc += s
        pts.append(acc)
    return pts

def fox_attention(q, k, v, log_f):
    bsz, seq, n_h, hd = q.shape
    n_blk = seq // Q_BLOCK
    c = jnp.cumsum(log_f, axis=1)
    c_keys = c.transpose(0, 2, 1)[:, :, None, :]
    q_blocks = q.reshape(bsz, n_blk, Q_BLOCK, n_h, hd).transpose(1, 0, 2, 3, 4)
    c_blocks = c.reshape(bsz, n_blk, Q_BLOCK, n_h).transpose(1, 0, 3, 2)
    k_pos = jnp.arange(seq)
    scale = hd ** -0.5

    def block(args):
        qi, ci, bi = args
        s = jnp.einsum('bqhd,bkhd->bhqk', qi, k, preferred_element_type=jnp.float32) * scale
        s = s + ci[..., None] - c_keys
        q_pos = bi * Q_BLOCK + jnp.arange(Q_BLOCK)
        s = jnp.where(k_pos[None, :] <= q_pos[:, None], s, -jnp.inf)
        p = jax.nn.softmax(s, axis=-1).astype(v.dtype)
        return jnp.einsum('bhqk,bkhd->bqhd', p, v)

    out = lax.map(block, (q_blocks, c_blocks, jnp.arange(n_blk)))
    return out.transpose(1, 0, 2, 3, 4).reshape(bsz, seq, n_h, hd)

def _complex_linear_combine(e1, e2):
    a1r, a1i, b1r, b1i = e1
    a2r, a2i, b2r, b2i = e2
    return (a1r * a2r - a1i * a2i,
            a1r * a2i + a1i * a2r,
            a2r * b1r - a2i * b1i + b2r,
            a2r * b1i + a2i * b1r + b2i)

def s5_mixer(u, a_re, a_im, b_re, b_im, c_re, c_im, d_skip, log_dt, w_glu, b_glu):
    bsz, seq, _ = u.shape
    f32 = jnp.float32
    uf = u.astype(f32)
    ug = uf.reshape(bsz, seq, S5_GROUPS, S5_GROUP)
    dt = jnp.exp(log_dt.astype(f32))[:, None]
    ar, ai = a_re.astype(f32), a_im.astype(f32)
    mag = jnp.exp(dt * ar)
    abar_r, abar_i = mag * jnp.cos(dt * ai), mag * jnp.sin(dt * ai)
    inv_den = 1.0 / (ar * ar + ai * ai)
    nr, ni = abar_r - 1.0, abar_i
    coef_r = (nr * ar + ni * ai) * inv_den
    coef_i = (ni * ar - nr * ai) * inv_den
    br, bi = b_re.astype(f32), b_im.astype(f32)
    bbar_r = coef_r[..., None] * br - coef_i[..., None] * bi
    bbar_i = coef_r[..., None] * bi + coef_i[..., None] * br
    drive_r = jnp.einsum('bsgh,gph->bsgp', ug, bbar_r)
    drive_i = jnp.einsum('bsgh,gph->bsgp', ug, bbar_i)
    a_shape = (1, seq, S5_GROUPS, S5_STATE)
    elems = (jnp.broadcast_to(abar_r, a_shape), jnp.broadcast_to(abar_i, a_shape), drive_r, drive_i)
    _, _, h_r, h_i = lax.associative_scan(_complex_linear_combine, elems, axis=1)
    y = (jnp.einsum('bsgp,ghp->bsgh', h_r, c_re.astype(f32))
         - jnp.einsum('bsgp,ghp->bsgh', h_i, c_im.astype(f32)))
    y = y.reshape(bsz, seq, S5_W) + d_skip.astype(f32) * uf
    z = jax.nn.gelu(y)
    out = z * jax.nn.sigmoid(z @ w_glu.astype(f32) + b_glu.astype(f32))
    return out.astype(u.dtype)

def hgrn2_mixer(q, f_logit, i_in, g_out, lb, o_gain):
    bsz, seq = q.shape[0], q.shape[1]
    f32 = jnp.float32
    n_chunks = seq // HG_CHUNK
    z = f_logit.astype(f32)
    log_f = jnp.logaddexp(jnp.log(lb), jnp.log1p(-lb) + jax.nn.log_sigmoid(z))
    key = (1.0 - lb) * jax.nn.sigmoid(-z)
    qf = jax.nn.silu(q.astype(f32))
    vf = i_in.astype(f32)

    def chunks(t):
        return t.reshape(bsz, n_chunks, HG_CHUNK, HG_HEADS, t.shape[-1]).transpose(1, 0, 3, 2, 4)

    causal = jnp.tril(jnp.ones((HG_CHUNK, HG_CHUNK), dtype=bool))[None, None, :, :, None]

    def step(state, xs):
        qc, kc, vc, lfc = xs
        b = jnp.cumsum(lfc, axis=2)
        o_inter = jnp.einsum('bhtk,bhkv->bhtv', qc * jnp.exp(b), state)
        rel = jnp.where(causal, b[:, :, :, None, :] - b[:, :, None, :, :], -jnp.inf)
        scores = jnp.einsum('bhtsk,bhsk->bhts', qc[:, :, :, None, :] * jnp.exp(rel), kc)
        o_intra = jnp.einsum('bhts,bhsv->bhtv', scores, vc)
        b_last = b[:, :, -1:, :]
        new_state = (jnp.exp(b_last[:, :, 0, :])[..., None] * state
                     + jnp.einsum('bhsk,bhsv->bhkv', kc * jnp.exp(b_last - b), vc))
        return new_state, o_inter + o_intra

    init = jnp.zeros((bsz, HG_HEADS, HG_DK, HG_DV), f32)
    _, o = lax.scan(step, init, (chunks(qf), chunks(key), chunks(vf), chunks(log_f)))
    o = o.transpose(1, 0, 3, 2, 4).reshape(bsz, seq, HG_HEADS, HG_DV)
    o = rmsnorm(o, o_gain) * jax.nn.silu(g_out.astype(f32))
    return o.reshape(bsz, seq, HG_W).astype(q.dtype)

def cross_attention(h, m, wq, wk, wv, wo, gq, gk):
    bsz, seq, _ = h.shape
    n_mem = m.shape[1]
    q = rmsnorm((h @ wq).reshape(bsz, seq, X_HEADS, X_HD), gq)
    k = rmsnorm((m @ wk).reshape(bsz, n_mem, X_HEADS, X_HD), gk)
    v = (m @ wv).reshape(bsz, n_mem, X_HEADS, X_HD)
    s = jnp.einsum('bshd,bmhd->bhsm', q, k, preferred_element_type=jnp.float32) * (X_HD ** -0.5)
    p = jax.nn.softmax(s, axis=-1).astype(v.dtype)
    o = jnp.einsum('bhsm,bmhd->bshd', p, v).reshape(bsz, seq, X_HEADS * X_HD)
    return o @ wo

def swiglu_2(h, w_gu, w_d):
    a, b = jnp.split(h @ w_gu, 2, axis=-1)
    return (jax.nn.silu(a) * b) @ w_d

def second_inputs(seed: int = 0) -> dict:
    key = jax.random.key(seed)
    keys = jax.random.split(key, 40)
    counter = [0]
    f32 = jnp.float32

    def nxt():
        k = keys[counter[0]]
        counter[0] += 1
        return k

    def nrm(shape, scale):
        return jax.random.normal(nxt(), shape, f32) * scale

    def gain(shape):
        return 1.0 + nrm(shape, 0.02)

    L, D = DEPTH_2, D_MODEL
    G, P, GS = S5_GROUPS, S5_STATE, S5_GROUP
    return {
        'x': nrm((BATCH, SEQ, D), 1.0),
        'mem': nrm((BATCH, N_MEM, D), 1.0),
        'norm_mix': gain((L, D)),
        'w_in': nrm((L, D, IN_COLS), D ** -0.5),
        'fox_fbias': FOX_FBIAS_OFFSET + nrm((L, FOX_HEADS), 0.5),
        'fox_qnorm': gain((L, FOX_HD)),
        'fox_knorm': gain((L, FOX_HD)),
        's5_a_re': -0.5 + nrm((L, G, P), 0.01),
        's5_a_im': math.pi * jnp.arange(P, dtype=f32)[None, None, :] + nrm((L, G, P), 0.01),
        's5_b_re': nrm((L, G, P, GS), (2 * GS) ** -0.5),
        's5_b_im': nrm((L, G, P, GS), (2 * GS) ** -0.5),
        's5_c_re': nrm((L, G, GS, P), (2 * P) ** -0.5),
        's5_c_im': nrm((L, G, GS, P), (2 * P) ** -0.5),
        's5_d': nrm((L, S5_W), 1.0),
        's5_log_dt': jax.random.uniform(nxt(), (L, G), f32, math.log(1e-3), math.log(1e-1)),
        's5_w_glu': nrm((L, S5_W, S5_W), S5_W ** -0.5),
        's5_b_glu': nrm((L, S5_W), 0.01),
        'hg_lb': nrm((L, HG_HEADS * HG_DK), 0.1),
        'hg_onorm': gain((L, HG_DV)),
        'w_branch': nrm((L, MIX_W, D), BRANCH_W ** -0.5),
        'w_out': nrm((L, D, D), D ** -0.5),
        'norm_x': gain((L, D)),
        'norm_mem': gain((L, D)),
        'xq': nrm((L, D, D), D ** -0.5),
        'xk': nrm((L, D, D), D ** -0.5),
        'xv': nrm((L, D, D), D ** -0.5),
        'xo': nrm((L, D, D), D ** -0.5),
        'x_qnorm': gain((L, X_HD)),
        'x_knorm': gain((L, X_HD)),
        'norm_ffn': gain((L, D)),
        'w_gate_up': nrm((L, D, 2 * D_FF_2), D ** -0.5),
        'w_down': nrm((L, D_FF_2, D), D_FF_2 ** -0.5),
    }

def second_block(x, mem, norm_mix, w_in, fox_fbias, fox_qnorm, fox_knorm, s5_a_re, s5_a_im,
              s5_b_re, s5_b_im, s5_c_re, s5_c_im, s5_d, s5_log_dt, s5_w_glu, s5_b_glu,
              hg_lb, hg_onorm, w_branch, w_out, norm_x, norm_mem, xq, xk, xv, xo,
              x_qnorm, x_knorm, norm_ffn, w_gate_up, w_down):
    bsz, seq, _ = x.shape
    split_pts = _split_points(IN_SIZES)
    lb_all = jnp.cumsum(jax.nn.softmax(hg_lb.astype(jnp.float32), axis=0), axis=0)
    lb_all = lb_all - lb_all[0:1]
    for l in range(DEPTH_2):
        h = rmsnorm(x, norm_mix[l])
        proj = h @ w_in[l]
        fq, fk, fv, ff, su, hq, hf, hi, hg, gl = jnp.split(proj, split_pts, axis=-1)
        q = rmsnorm(fq.reshape(bsz, seq, FOX_HEADS, FOX_HD), fox_qnorm[l])
        k = rmsnorm(fk.reshape(bsz, seq, FOX_HEADS, FOX_HD), fox_knorm[l])
        v = fv.reshape(bsz, seq, FOX_HEADS, FOX_HD)
        log_f = jax.nn.log_sigmoid((ff + fox_fbias[l]).astype(jnp.float32))
        y_fox = fox_attention(q, k, v, log_f).reshape(bsz, seq, FOX_W)
        y_s5 = s5_mixer(su, s5_a_re[l], s5_a_im[l], s5_b_re[l], s5_b_im[l], s5_c_re[l], s5_c_im[l],
                        s5_d[l], s5_log_dt[l], s5_w_glu[l], s5_b_glu[l])
        y_hg = hgrn2_mixer(hq.reshape(bsz, seq, HG_HEADS, HG_DK), hf.reshape(bsz, seq, HG_HEADS, HG_DK),
                           hi.reshape(bsz, seq, HG_HEADS, HG_DV), hg.reshape(bsz, seq, HG_HEADS, HG_DV),
                           lb_all[l].reshape(HG_HEADS, HG_DK), hg_onorm[l])
        gates = jax.nn.sigmoid(gl).reshape(bsz, seq, N_BRANCH, D_MODEL)
        wb = w_branch[l]
        merged = (gates[:, :, 0] * (y_fox @ wb[:BRANCH_W])
                  + gates[:, :, 1] * (y_s5 @ wb[BRANCH_W:2 * BRANCH_W])
                  + gates[:, :, 2] * (y_hg @ wb[2 * BRANCH_W:]))
        x = x + merged @ w_out[l]
        x = x + cross_attention(rmsnorm(x, norm_x[l]), rmsnorm(mem, norm_mem[l]),
                                xq[l], xk[l], xv[l], xo[l], x_qnorm[l], x_knorm[l])
        x = x + swiglu_2(rmsnorm(x, norm_ffn[l]), w_gate_up[l], w_down[l])
    return x


def setup_inputs(seed=0):
    out = dict(first_inputs(seed))
    for name, value in second_inputs(seed + 1).items():
        if name != "x":
            out[name + "_2"] = value
    return out


def reference(
    x, ffn1_norm, ffn1_w_in, ffn1_w_out, mix_norm, ffn2_norm, ffn2_w_in, ffn2_w_out, rec_w_in,
    rec_conv_w, rec_conv_b, rec_gate_a_w, rec_gate_a_b, rec_gate_x_w, rec_gate_x_b, rec_lambda,
    rec_w_out, sg_w_in, sg_v_norm, sg_w_s, sg_b_s, sg_w_out, final_norm, mem_2, norm_mix_2,
    w_in_2, fox_fbias_2, fox_qnorm_2, fox_knorm_2, s5_a_re_2, s5_a_im_2, s5_b_re_2, s5_b_im_2,
    s5_c_re_2, s5_c_im_2, s5_d_2, s5_log_dt_2, s5_w_glu_2, s5_b_glu_2, hg_lb_2, hg_onorm_2,
    w_branch_2, w_out_2, norm_x_2, norm_mem_2, xq_2, xk_2, xv_2, xo_2, x_qnorm_2, x_knorm_2,
    norm_ffn_2, w_gate_up_2, w_down_2,
):
    x = first_block(
        x, ffn1_norm, ffn1_w_in, ffn1_w_out, mix_norm, ffn2_norm, ffn2_w_in, ffn2_w_out,
        rec_w_in, rec_conv_w, rec_conv_b, rec_gate_a_w, rec_gate_a_b, rec_gate_x_w,
        rec_gate_x_b, rec_lambda, rec_w_out, sg_w_in, sg_v_norm, sg_w_s, sg_b_s, sg_w_out,
        final_norm,
    )
    return second_block(
        x, mem_2, norm_mix_2, w_in_2, fox_fbias_2, fox_qnorm_2, fox_knorm_2, s5_a_re_2,
        s5_a_im_2, s5_b_re_2, s5_b_im_2, s5_c_re_2, s5_c_im_2, s5_d_2, s5_log_dt_2, s5_w_glu_2,
        s5_b_glu_2, hg_lb_2, hg_onorm_2, w_branch_2, w_out_2, norm_x_2, norm_mem_2, xq_2, xk_2,
        xv_2, xo_2, x_qnorm_2, x_knorm_2, norm_ffn_2, w_gate_up_2, w_down_2,
    )


_drawn_inputs = setup_inputs


def setup_inputs(seed=0):
    import zlib

    import numpy as np

    out = dict(_drawn_inputs(seed))
    spreads = {}
    factors = {'rec_gate_a_b': 8.0,
     'rec_gate_x_b': 8.0,
     'sg_v_norm': 3.046,
     'norm_mix_2': 4.662,
     'fox_qnorm_2': 8.0,
     'fox_knorm_2': 8.0,
     's5_a_re_2': 64.0,
     's5_a_im_2': 39.04,
     's5_b_re_2': 53.048,
     's5_b_im_2': 54.656,
     's5_c_re_2': 52.592,
     's5_c_im_2': 55.256,
     's5_log_dt_2': 43.128,
     's5_b_glu_2': 64.0,
     'hg_onorm_2': 8.0,
     'norm_x_2': 8.0,
     'norm_mem_2': 8.0,
     'x_qnorm_2': 8.0,
     'x_knorm_2': 8.0,
     'norm_ffn_2': 15.226}
    for name, (base, spread) in spreads.items():
        noise = np.random.default_rng([zlib.crc32(name.encode()), seed]).standard_normal(out[name].shape)
        drawn = base * np.exp(spread * noise) if base else spread * noise
        out[name] = jnp.asarray(drawn.astype(out[name].dtype))
    for name, factor in factors.items():
        out[name] = (out[name] * factor).astype(out[name].dtype)
    return out
```

```python
from contextlib import ExitStack

import numpy as np

import concourse.bass as bass
from concourse import mybir

P = 128
T = 512
D = 1024
KD = D // P
FF = 2816
KF = FF // P
NMEM = 256
EPS = 1e-6
RING = 4
UNIT = 8 * P
AHEAD = 3
ROUND = 12582912.0
TWO_PI = (6.28125, 0.0019350051879882812, 3.0199159819e-07)
PI_BELOW = 3.1415925
TURN = 6.283185
FINAL = 6
F32 = mybir.dt.float32
F32R = mybir.dt.float32r
U8 = mybir.dt.uint8
ACT = mybir.ActivationFunctionType
ALU = mybir.AluOpType
AX = mybir.AxisListType

PARAMS = {}
_at = 0
for _name, _n in (("ffn1_norm", 2 * KD), ("ffn2_norm", 2 * KD), ("mix_norm", 2 * KD), ("final_norm", KD),
                  ("norm_mix_2", KD), ("norm_x_2", KD), ("norm_mem_2", KD), ("norm_ffn_2", KD),
                  ("rec_conv_w", 4 * KD), ("rec_conv_b", KD), ("rec_gate_a_b", KD), ("rec_gate_x_b", KD),
                  ("rec_lambda", KD), ("sg_v_norm", KD), ("s5_d_2", 4), ("s5_b_glu_2", 4), ("hg_onorm_2", 1),
                  ("x_qnorm_2", 2), ("x_knorm_2", 2), ("fox_qnorm_2", 1), ("fox_knorm_2", 1),
                  ("s5_a_re_2", 16), ("s5_a_im_2", 16), ("s5_log_dt_2", 16)):
    PARAMS[_name] = _at
    _at += _n
NPAR = _at


class Layer:

    def __init__(self, name, src, widths, bodies, results, base, rbase):
        self.name, self.src, self.widths, self.bodies = name, src, widths, bodies
        self.per = len(widths)
        self.n = self.per * bodies
        self.results, self.base, self.rbase = results, base, rbase
        assert self.per % RING == 0 and self.base % RING == 0 and self.rbase % RING == 0


class Chain:

    def __init__(self, sem):
        self.sem, self.n = sem, 0

    def __call__(self, eng, ins):
        self.n += 1
        ins.then_inc(self.sem, 1)
        eng.wait_ge(self.sem, self.n)


def each_body(eng, n, body):
    if n == 1:
        body(0)
    else:
        with eng.Fori(0, n) as b:
            body(b)


LAST = {"ffn0": "down0", "rec": "rec_out", "ffn1": "down1", "ffn2": "down2", "sgu": "sg_out", "ffn3": "down3", "first": "down3", "yfox": "s5_in", "ys5": "s5_glu", "yhg": "merge1", "mix": "w_out", "xattn": "xo"}


def build(nc, io, stop=None):
    ctx = ExitStack()
    layers = {}
    order = []

    def layer(name, dram, widths, bodies, results, cols=None):
        base = order[-1].base + order[-1].n if order else 0
        rbase = order[-1].rbase + order[-1].results if order else 0

        def src(b, i):
            if cols is None:
                return io[dram][bass.ds((b * len(widths) + i) * P, P), 0:widths[i]]
            row, c0, c1 = cols(i)
            rows = len(widths) // (KF * P // UNIT + 1)
            return io[dram][bass.ds((b * rows + row) * P, P), c0:c1]
        order.append(Layer(name, src, widths, bodies, results, base, rbase))
        layers[name] = order[-1]

    DOWN_W = [UNIT, UNIT, KF * P - 2 * UNIT]

    def ffn_layers(i):
        layer(f"up{i}", f"w_up{i}", [UNIT] * 4, 11, 44)
        layer(f"down{i}", f"w_down{i}", DOWN_W * 4, 2, 8,
              cols=lambda j: (j // 3, (j % 3) * UNIT, min((j % 3 + 1) * UNIT, KF * P)))

    def column_layer(name, n, widths=(UNIT,) * 4, results=None):
        layer(name, name, list(widths), n // len(widths), n if results is None else results)

    ffn_layers(0)
    column_layer("rec_r", 8)
    column_layer("rec_y", 8)
    column_layer("rec_out", 8)
    ffn_layers(1)
    ffn_layers(2)
    column_layer("sg_v", 8)
    column_layer("sg_u", 8)
    column_layer("sg_out", 8)
    ffn_layers(3)
    column_layer("fox_qk", 8)
    column_layer("fox_v", 4)
    column_layer("s5_in", 4)
    column_layer("hg_qfg", 12)
    column_layer("hg_v", 4)
    column_layer("s5_glu", 4, (UNIT // 2,) * 4)
    column_layer("merge0", 12, (UNIT,) * 12, 16)
    column_layer("merge1", 12, (UNIT,) * 12, 16)
    column_layer("merge2", 12, (UNIT,) * 12, 16)
    column_layer("xk", 8)
    column_layer("xv", 8, results=4)
    column_layer("w_out", 8)
    column_layer("xq", 8)
    column_layer("xo", 8)
    ffn_layers(4)
    if stop in LAST:
        while order[-1].name != LAST[stop]:
            del layers[order.pop().name]

    base = -(-nc.sbuf_base // 64) * 64
    cursor = [base]

    def place(name, shape, dt=F32, at=None):
        size = int(np.prod(shape[1:])) * mybir.dt.size(dt)
        off = cursor[0] if at is None else at
        t = nc.alloc_sbuf_tensor_at(name, list(shape), dt, offset=off)
        if at is None:
            cursor[0] += -(-size // 32) * 32
        return t

    x = place("x_res", [P, KD, T])
    xg_hi = place("xg_hi", [P, KD, T], F32R)
    xg_lo = place("xg_lo", [P, KD, T], F32R)
    w_stage = place("w_stage", [P, RING, UNIT])
    w_hi = place("w_hi", [P, RING, UNIT], F32R)
    w_lo = place("w_lo", [P, RING, UNIT], F32R)
    ubuf = place("ubuf", [P, T])
    gbuf = place("gbuf", [P, T])
    sq = place("sq", [P, 2, T])
    ss = place("ss", [P, T])
    rstd = place("rstd", [P, T])
    par = place("par", [P, NPAR])
    ones = place("ones", [P, P])
    eps = place("eps", [P, 1])
    rcol = place("rcol", [P, 4])
    c8 = place("c8", [P, 2, KD])
    ident = place("ident", [P, P])
    aux = cursor[0]
    cursor[0] += 8192
    work = cursor[0]
    h_hi = place("h_hi", [P, KF, T], F32R)
    h_lo = place("h_lo", [P, KF, T], F32R)
    KB = 1024

    gate_w = place("gate_w", [P, 2, KD, P], at=aux)
    r_pad = place("r_pad", [P, KD, T + 3], at=work)
    y_rec = place("y_rec", [P, KD, T], at=work)
    conv = place("conv", [P, KD, T], at=work + 17 * KB)
    ga = place("ga", [P, KD, T], at=work + 33 * KB)
    gx = place("gx", [P, KD, T], at=work + 49 * KB)
    hs = place("hs", [P, KD, T], at=work + 65 * KB)
    yh_hi = place("yh_hi", [P, KD, T], F32R, at=work + 17 * KB)
    yh_lo = place("yh_lo", [P, KD, T], F32R, at=work + 49 * KB)

    ws_raw = place("ws_raw", [P, KD, P], at=aux)
    bsb = place("bsb", [P, KD, P], at=aux + 4 * KB)
    vt = place("vt", [P, 4, D], at=work)
    ug = place("ug", [P, KD, T], at=work + 16 * KB)
    sgy_hi = place("sgy_hi", [P, KD, T], F32R, at=work + 32 * KB)
    sgy_lo = place("sgy_lo", [P, KD, T], F32R, at=work + 48 * KB)
    ws = place("ws", [P, KD, P], at=work + 64 * KB)
    tri = place("tri", [P, P], U8, at=work + 68 * KB)
    tri_f = place("tri_f", [P, P], at=work + 69 * KB)
    vss = place("vss", [P, 3, 8], at=work + 68 * KB + 128)

    bank = [ctx.enter_context(nc.psum_tensor(f"bank{i}", [P, T], F32)) for i in range(8)]

    R = work + 48 * KB
    y0_hi = place("y0_hi", [P, 4, T], F32R, at=work)
    y0_lo = place("y0_lo", [P, 4, T], F32R, at=work + 8 * KB)
    y1_hi = place("y1_hi", [P, 4, T], F32R, at=work + 16 * KB)
    y1_lo = place("y1_lo", [P, 4, T], F32R, at=work + 24 * KB)
    merged = place("merged", [P, KD, T], at=work + 32 * KB)
    qk = place("qk", [P, 8, T], at=R)
    vtok = place("vtok", [P, 4, T], at=R + 16 * KB)
    prob = place("prob", [P, 2, T], at=R + 24 * KB)
    probT = place("probT", [P, 2, T], at=R + 28 * KB)
    negc = place("negc", [8, T], at=R + 32 * KB)
    qk_r = place("qk_r", [16, T], at=R + 34 * KB)
    sel8 = place("sel8", [8, 8, P], at=aux)
    s5p = place("s5p", [P, 16, 16], at=aux + 4 * KB)
    pack = place("pack", [P, 32], at=aux + 5 * KB)
    ff_w = place("ff_w", [P, KD, 8], at=aux + 5 * KB + 128)
    causal = place("causal", [P, P], at=aux + 5 * KB + 384)
    att_m = place("att_m", [P, 32], at=aux + 6 * KB)
    att_l = place("att_l", [P, 32], at=aux + 6 * KB + 128)
    ff_b = place("ff_b", [8, 1], at=aux + 6 * KB + 256)
    s5_b = place("s5_b", [P, 2, 16, 16], at=work + 20 * KB)
    s5_c = place("s5_c", [P, 2, 16, 16], at=work + 22 * KB)
    s5_t = place("s5_t", [P, 2, 16, 16], at=work + 24 * KB)
    s5_bx = place("s5_bx", [P, 2, 16, 32], at=work + 16 * KB)
    spread = place("spread", [16, 8 * P], at=work + 28 * KB)
    su = place("su", [P, 4, T], at=work + 32 * KB)
    s5_cx = place("s5_cx", [P, 2, 16, 32], at=work + 40 * KB)
    s5_bt = place("s5_bt", [P, 2, 4, P], at=work + 44 * KB)
    rot = place("rot", [P, 2, 2, T], at=work + 16 * KB)
    s5_g = place("s5_g", [P, 2, T], at=work + 24 * KB)
    s5_m = place("s5_m", [P, 2, T], at=work + 28 * KB)
    iota = place("iota", [P, T], at=aux)
    turn = place("turn", [P, T], at=aux + 2 * KB)
    hq = place("hq", [P, 12, T], at=R)
    hv = place("hv", [P, 4, T], at=R + 24 * KB)
    hk = place("hk", [P, 4, T], at=R + 32 * KB)
    he = place("he", [P, 2, T], at=aux)
    hm = place("hm", [P, 8, P], U8, at=aux + 4 * KB)
    levels_f = place("levels_f", [P, 8 * P], at=work + 40 * KB)
    hS = place("hS", [P, 3, P], at=aux + 5 * KB)
    hdec = place("hdec", [P, 4], at=aux + 6 * KB + 512)
    memx = place("memx", [P, KD, NMEM], at=R)
    mem_hi = place("mem_hi", [P, KD, NMEM], F32R, at=R + 8 * KB)
    mem_lo = place("mem_lo", [P, KD, NMEM], F32R, at=R + 16 * KB)
    kx = place("kx", [P, KD, NMEM], at=R + 24 * KB)
    vx = place("vx", [P, 2, D], at=R + 32 * KB)
    msq = place("msq", [P, KD, NMEM], at=R + 24 * KB)
    qx = place("qx", [P, KD, T], at=work)
    o_hi = place("o_hi", [P, KD, T], F32R, at=work + 16 * KB)
    o_lo = place("o_lo", [P, KD, T], F32R, at=work + 32 * KB)
    rstd_m = place("rstd_m", [P, NMEM], at=aux)
    x_sel = place("x_sel", [4, 4, P], at=aux + 1 * KB)
    x_r = place("x_r", [4, T], at=aux + 3 * KB)
    rcol_m = place("rcol_m", [P, 2], at=aux + 5 * KB)
    pick = place("pick", [P, 8], at=aux + 5 * KB + 32)
    xa_m = place("xa_m", [P, 16], at=aux + 5 * KB + 64)
    xa_l = place("xa_l", [P, 16], at=aux + 5 * KB + 128)
    xprob = place("xprob", [P, 2, NMEM], at=R)
    xprobT = place("xprobT", [P, 2, 2, T], at=R + 8 * KB)

    def sem(name):
        return ctx.enter_context(nc.semaphore(name))

    w_loaded = [sem(f"w_loaded{r}") for r in range(RING)]
    w_hi_ready, w_lo_ready = sem("w_hi_ready"), sem("w_lo_ready")
    unit_used = sem("unit_used")
    taken = sem("taken")
    x_in, par_in, ones_set = sem("x_in"), sem("par_in"), sem("ones_set")
    xg_hi_ready, xg_lo_ready = sem("xg_hi_ready"), sem("xg_lo_ready")
    sq_ready, ss_added, ss_summed = sem("sq_ready"), sem("ss_added"), sem("ss_summed")
    std_ready, rstd_ready = sem("std_ready"), sem("rstd_ready")
    silu_done, prod_done = sem("silu_done"), sem("prod_done")
    h_hi_ready, h_lo_ready = sem("h_hi_ready"), sem("h_lo_ready")
    gate_w_in, gate_w_zero = sem("gate_w_in"), sem("gate_w_zero")
    pad_zero, conv_step, gates_mm, gates_sig = sem("pad_zero"), sem("conv_step"), sem("gates_mm"), sem("gates_sig")
    decay_step, mult2_done, mult_done = sem("decay_step"), sem("mult2_done"), sem("mult_done")
    drive_step, scan_done, gelu_done = sem("drive_step"), sem("scan_done"), sem("gelu_done")
    yh_done, yh_hi_ready, yh_lo_ready = sem("yh_done"), sem("yh_hi_ready"), sem("yh_lo_ready")
    ws_in, ws_zero, ws_ready = sem("ws_in"), sem("ws_zero"), sem("ws_ready")
    v_sum = sem("v_sum")
    v_gelu, v_sq, v_std, v_rstd, v_normed = sem("v_gelu"), sem("v_sq"), sem("v_std"), sem("v_rstd"), sem("v_normed")
    u_gelu, mixed, gated, sgy_hi_ready, sgy_lo_ready = (
        sem("u_gelu"), sem("mixed"), sem("gated"), sem("sgy_hi_ready"), sem("sgy_lo_ready"))
    final_step = sem("final_step")
    ident_in = sem("ident_in")
    col_summed, col_std, col_rstd = sem("col_summed"), sem("col_std"), sem("col_rstd")
    mix_in, su_ready = sem("mix_in"), sem("su_ready")
    qk_sq, qk_ss, qk_std, qk_rstd, qk_spread, qk_scaled = (
        sem(n) for n in ("qk_sq", "qk_ss", "qk_std", "qk_rstd", "qk_spread", "qk_scaled"))
    ff_mm, ff_z, ff_ln, negc_ready = (sem(n) for n in ("ff_mm", "ff_z", "ff_ln", "negc_ready"))
    att_s, att_nmax, att_exp, att_p, att_t, att_tc, att_o = (
        sem(n) for n in ("att_s", "att_nmax", "att_exp", "att_p", "att_t", "att_tc", "att_o"))
    fox_hi, fox_lo = sem("fox_hi"), sem("fox_lo")
    s5_act, s5_dve, s5_bx_ready, s5_bt_mm, s5_bt_ready, iota_in = (
        sem(n) for n in ("s5_act", "s5_dve", "s5_bx_ready", "s5_bt_mm", "s5_bt_ready", "iota_in"))
    s5_turn, s5_rot, s5_drive, s5_step, s5_prod, s5_ymm, s5_y = (
        sem(n) for n in ("s5_turn", "s5_rot", "s5_drive", "s5_step", "s5_prod", "s5_ymm", "s5_y"))
    z_ready, z_hi_ready, z_lo_ready, glu_z, glu_sig, glu_out, s5_hi, s5_lo = (
        sem(n) for n in ("z_ready", "z_hi_ready", "z_lo_ready", "glu_z", "glu_sig", "glu_out", "s5_hi", "s5_lo"))
    levels_in, levels_ready, hg_zero, hg_key, hg_silu, hg_ln, hg_cum = (
        sem(n) for n in ("levels_in", "levels_ready", "hg_zero", "hg_key", "hg_silu", "hg_ln", "hg_cum"))
    hg_diff, hg_exp, hg_fac, hg_score, hg_sel, hg_dec = (
        sem(n) for n in ("hg_diff", "hg_exp", "hg_fac", "hg_score", "hg_sel", "hg_dec"))
    hg_kt, hg_ktc, hg_update, hg_state, hg_o, hg_osq, hg_oss, hg_std, hg_y, hg_hi, hg_lo = (
        sem(n) for n in ("hg_kt", "hg_ktc", "hg_update", "hg_state", "hg_o", "hg_osq", "hg_oss", "hg_std", "hg_y", "hg_hi", "hg_lo"))
    gate_tanh, merge_step, m_hi_ready, m_lo_ready = (
        sem(n) for n in ("gate_tanh", "merge_step", "m_hi_ready", "m_lo_ready"))
    mem_in, mem_sq, mem_hi_ready, mem_lo_ready, mem_ss, mem_std, mem_rstd = (
        sem(n) for n in ("mem_in", "mem_sq", "mem_hi_ready", "mem_lo_ready", "mem_ss", "mem_std", "mem_rstd"))
    xn_sq, xn_ss, xn_std, xn_rstd, xn_spread, xn_scaled = (
        sem(n) for n in ("xn_sq", "xn_ss", "xn_std", "xn_rstd", "xn_spread", "xn_scaled"))
    xo_hi_ready, xo_lo_ready = sem("xo_hi_ready"), sem("xo_lo_ready")
    dve_chain, act_chain = Chain(sem("dve_chain")), Chain(sem("act_chain"))
    out_stored = sem("out_stored")
    block = ctx.enter_context(nc.Block())

    def f32(ap):
        return ap.bitcast(F32)

    def tile(t, i):
        return t[:, bass.ds(i, 1), :].rearrange("p a t -> p (a t)")

    def col(name, i=0):
        return par[:, bass.ds(i + PARAMS[name], 1)]

    def load_layer(sp, L):
        def body(b, first=False):
            for i, w in enumerate(L.widths):
                if not first or i >= RING:
                    sp.wait_ge(w_lo_ready, b * L.per + (L.base + i + 1 - RING))
                sp.dma_start(w_stage[:, i % RING, 0:w], L.src(b, i)).then_inc(w_loaded[i % RING], 16)
        if L.base == 0:
            body(0, first=True)
            with sp.Fori(1, L.bodies) as b:
                body(b)
        else:
            each_body(sp, L.bodies, body)

    def split_hi(act, L, b, i):
        if i >= L.per:
            b, i = b + 1, i - L.per
        if isinstance(b, int) and b == L.bodies:
            at = order.index(L) + 1
            if at == len(order):
                return
            L, b = order[at], 0
        r, w = i % RING, L.widths[i]
        act.wait_ge(w_loaded[r], b * (16 * L.per // RING) + 16 * (L.base // RING + i // RING + 1))
        if not (L.base == 0 and isinstance(b, int) and b == 0 and i < RING):
            act.wait_ge(unit_used, b * L.per + (L.base + i + 1 - RING))
        act.activation(w_hi[:, r, 0:w], w_stage[:, r, 0:w], ACT.Copy).then_inc(w_hi_ready, 1)

    def act_bodies(act, L, work=None, only=None):
        def body(b):
            for i in range(L.per):
                split_hi(act, L, b, i + AHEAD)
                if work is not None:
                    work(b, i)
        if only is not None:
            body(only)
            return
        if L.bodies > 1:
            each_body(act, L.bodies - 1, body)
        body(L.bodies - 1)

    def split_lo(pool, L):
        def body(b):
            for i, w in enumerate(L.widths):
                r = i % RING
                pool.wait_ge(w_hi_ready, b * L.per + (L.base + i + 1))
                pool.tensor_tensor(w_lo[:, r, 0:w], w_stage[:, r, 0:w], f32(w_hi[:, r, 0:w]),
                                   ALU.subtract).then_inc(w_lo_ready, 1)
        each_body(pool, L.bodies, body)

    def three_passes(pe, out, r, j, hi, lo, start, stop):
        c = slice(j * P, (j + 1) * P)
        pe.matmul(out, w_hi[:, r, c], hi, start=start, stop=False)
        pe.matmul(out, w_hi[:, r, c], lo, start=False, stop=False)
        return pe.matmul(out, w_lo[:, r, c], hi, start=False, stop=stop)

    def project_unit(pe, L, b, i, hi, lo, ready=None, width=T):
        r = i % RING
        pe.wait_ge(w_lo_ready, b * L.per + (L.base + i + 1))
        pe.wait_ge(taken, b * L.per + max(L.rbase + i + 1 - RING, 0))
        for k in range(KD):
            if i == 0 and ready is not None:
                pe.wait_ge(ready[0], ready[1] + k + 1)
            mm = three_passes(pe, bank[r][:, 0:width], r, k, hi[:, k, :], lo[:, k, :], k == 0, k == KD - 1)
        mm.then_inc(unit_used, 1)

    def pe_project(pe, L, hi, lo, ready, after_first=None, width=T):
        def body(b):
            for i in range(L.per):
                project_unit(pe, L, b, i, hi, lo, ready, width)
        if after_first is None:
            each_body(pe, L.bodies, body)
        else:
            body(0)
            after_first()
            if L.bodies > 2:
                with pe.Fori(1, L.bodies) as b:
                    body(b)
            else:
                body(1)

    def pe_tokens_unit(pe, L, b, i, hi, lo, ntt=4):
        pe.wait_ge(w_lo_ready, b * 4 + (L.base + i + 1))
        for kk in range(2):
            k = 2 * i + kk
            wh, wl = (w[:, i, kk * T:(kk + 1) * T] for w in (w_hi, w_lo))
            for t in range(ntt):
                if k == 0:
                    pe.wait_ge(taken, b * ntt + (L.rbase + t + 1 - RING))
                c = slice(t * P, (t + 1) * P)
                out = bank[t if ntt == RING else b * ntt + t][:]
                pe.matmul(out, hi[:, k, c], wh, start=k == 0, stop=False)
                pe.matmul(out, lo[:, k, c], wh, start=False, stop=False)
                mm = pe.matmul(out, hi[:, k, c], wl, start=False, stop=k == KD - 1)
        mm.then_inc(unit_used, 1)

    def pe_project_tokens(pe, L, hi, lo, ntt=4):
        def body(b):
            for i in range(4):
                pe_tokens_unit(pe, L, b, i, hi, lo, ntt)
        if ntt == RING:
            each_body(pe, L.bodies, body)
        else:
            for b in range(L.bodies):
                body(b)

    def split_count(q):
        return KD * (q - (q > FINAL))

    def act_norm_tile(act, q, gain, m, buf):
        if not (q == 0 and isinstance(m, int) and m < 2):
            act.wait_ge(ss_added, m + (KD + 1) * q)
        act.activation(sq[:, buf, :], tile(x, m), ACT.Square).then_inc(sq_ready, 1)
        if q != FINAL:
            act.activation(tile(xg_hi, m), tile(x, m), ACT.Copy, scale=col(*gain(m))).then_inc(xg_hi_ready, 1)

    def dve_norm_tile(dve, q, gain, m, buf):
        dve.wait_ge(sq_ready, m + (KD * q + 1))
        dve.wait_ge(ss_added, m + ((KD + 1) * q + 1))
        dve.tensor_tensor(ss[:], ss[:], sq[:, buf, :], ALU.add).then_inc(ss_added, 1)
        if q != FINAL:
            dve.wait_ge(xg_hi_ready, m + (split_count(q) + 1))
            dve.scalar_tensor_tensor(tile(xg_lo, m), tile(x, m), col(*gain(m)), f32(tile(xg_hi, m)),
                                     ALU.mult, ALU.subtract).then_inc(xg_lo_ready, 1)

    def pe_norm_sum(pe, q):
        pe.wait_ge(ss_added, (KD + 1) * (q + 1))
        pe.matmul(bank[4][:], ones[:], ss[:], start=True, stop=True).then_inc(ss_summed, 1)

    def act_norm_std(act, q):
        act.wait_ge(ss_summed, q + 1)
        act.activation(rstd[:], bank[4][:], ACT.Sqrt, bias=eps[:], scale=1.0 / D).then_inc(std_ready, 1)

    def dve_norm_rstd(dve, q):
        dve.wait_ge(std_ready, q + 1)
        dve.reciprocal(rstd[:], rstd[:]).then_inc(rstd_ready, 1)
        dve.wait_ge(rstd_ready, q + 1)

    def pe_norm_columns(pe):
        for t in range(4):
            mm = pe.matmul(bank[5][:, t:t + 1], ss[:, t * P:(t + 1) * P], ones[:, 0:1], start=True, stop=True)
        mm.then_inc(col_summed, 1)

    def act_norm_columns(act, n):
        act.wait_ge(col_summed, n)
        act.activation(rcol[:], bank[5][:, 0:4], ACT.Sqrt, bias=eps[:], scale=1.0 / D).then_inc(col_std, 1)

    def dve_norm_columns(dve, n):
        dve.wait_ge(col_std, n)
        dve.reciprocal(rcol[:], rcol[:]).then_inc(col_rstd, 1)
        dve.wait_ge(col_rstd, n)

    def pe_ffn(pe, i, q):
        U, L = layers[f"up{i}"], layers[f"down{i}"]
        pe_project(pe, U, xg_hi, xg_lo, (xg_lo_ready, split_count(q)), after_first=lambda: None)

        def down(b):
            for m in range(4):
                pe.wait_ge(taken, b * 4 + (L.rbase + m + 1 - RING))
                for part in range(3):
                    u = 3 * m + part
                    k1 = min(8 * part + 8, KF)
                    pe.wait_ge(w_lo_ready, b * L.per + (L.base + u + 1))
                    pe.wait_ge(h_lo_ready, KF * i + k1)
                    for k in range(8 * part, k1):
                        mm = three_passes(pe, bank[m][:], u % RING, k - 8 * part, h_hi[:, k, :], h_lo[:, k, :],
                                          k == 0, k == KF - 1)
                    mm.then_inc(unit_used, 1)
        each_body(pe, L.bodies, down)

    def act_ffn(act, i):
        U = layers[f"up{i}"]

        def up(b, u):
            if u % 2 == 1:
                act.wait_ge(taken, b * 4 + (U.rbase + u + 1))
                act.activation(gbuf[:], gbuf[:], ACT.Silu).then_inc(silu_done, 1)
                act.wait_ge(prod_done, b * 2 + (KF * i + u // 2 + 1))
                act.activation(tile(h_hi, b * 2 + u // 2), ubuf[:], ACT.Copy).then_inc(h_hi_ready, 1)
        act.preload_act_table(ACT.Silu)
        act_bodies(act, U, up)

    def dve_ffn(dve, i):
        U = layers[f"up{i}"]

        def up(b):
            for jj in range(2):
                j = b * 2 + jj
                dve.wait_ge(h_lo_ready, j + KF * i)
                dve.wait_ge(unit_used, b * 4 + (U.base + 2 * jj + 1))
                dve.tensor_tensor(ubuf[:], bank[2 * jj][:], rstd[:], ALU.mult).then_inc(taken, 1)
                dve.wait_ge(unit_used, b * 4 + (U.base + 2 * jj + 2))
                dve.tensor_tensor(gbuf[:], bank[2 * jj + 1][:], rstd[:], ALU.mult).then_inc(taken, 1)
                dve.wait_ge(silu_done, j + (KF * i + 1))
                dve.tensor_tensor(ubuf[:], gbuf[:], ubuf[:], ALU.mult).then_inc(prod_done, 1)
                dve.wait_ge(h_hi_ready, j + (KF * i + 1))
                dve.tensor_tensor(tile(h_lo, j), ubuf[:], f32(tile(h_hi, j)), ALU.subtract).then_inc(h_lo_ready, 1)
        each_body(dve, U.bodies, up)

    def dve_residual(dve, L, scale, q, gain):
        upr = L.n // KD
        mb = L.per // upr
        dve_chain(dve, dve.engine_nop()) if False else None
        if q is not None:
            dve.memset(ss[:], 0.0).then_inc(ss_added, 1)

        def body(b):
            for mm in range(mb):
                m = b * mb + mm
                dve.wait_ge(unit_used, b * L.per + (L.base + (mm + 1) * upr))
                dve.scalar_tensor_tensor(tile(x, m), bank[mm % 4][:], scale, tile(x, m),
                                         ALU.mult, ALU.add).then_inc(taken, 1)
                if q is not None:
                    dve_norm_tile(dve, q, gain, m, mm % 2)
        each_body(dve, L.bodies, body)
        if q is not None:
            dve_norm_rstd(dve, q)

    def act_residual(act, L, q, gain):
        upr = L.n // KD
        mb = L.per // upr

        def result(b, i):
            if q is not None and i % upr == upr - 1:
                m = b * mb + i // upr
                act.wait_ge(taken, m + (L.rbase + 1))
                act_norm_tile(act, q, gain, m, (i // upr) % 2)
        act_bodies(act, L, result)
        if q is not None:
            act_norm_std(act, q)

    def gain_of(name, i=0):
        return lambda m: (name, m + i * KD)

    def sp_rec(sp):
        sp.wait_ge(gate_w_zero, 1)
        for g, name in enumerate(("gate_a_w", "gate_x_w")):
            for s in range(2):
                h = slice(64 * s, 64 * s + 64)
                sp.dma_start(gate_w[h, g, :, h], io[name][h, :].rearrange("p (t j) -> p t j", j=64)).then_inc(gate_w_in, 16)

    def dve_softplus(dve):
        lam = par[:, PARAMS["rec_lambda"]:PARAMS["rec_lambda"] + KD]
        u, s, s2, p = (gbuf[:, KD * j:KD * (j + 1)] for j in range(4))
        dve.wait_ge(act_chain.sem, 2)
        dve_chain(dve, dve.tensor_scalar(s2, u, 2.0, None, ALU.add))
        dve_chain(dve, dve.reciprocal(s2, s2))
        dve_chain(dve, dve.tensor_tensor(s, u, s2, ALU.mult))
        dve_chain(dve, dve.tensor_tensor(s2, s, s, ALU.mult))
        dve_chain(dve, dve.tensor_scalar(p, s2, 1.0 / 19, 1.0 / 17, ALU.mult, ALU.add))
        for n in (15, 13, 11, 9, 7, 5, 3, 1):
            dve_chain(dve, dve.tensor_tensor(p, p, s2, ALU.mult))
            dve_chain(dve, dve.tensor_scalar(p, p, 1.0 / n, None, ALU.add))
        dve_chain(dve, dve.tensor_tensor(p, p, s, ALU.mult))
        dve_chain(dve, dve.tensor_scalar(s2, lam, -1.0, 0.0, ALU.mult, ALU.max))
        dve_chain(dve, dve.scalar_tensor_tensor(p, p, 2.0, s2, ALU.mult, ALU.add))
        dve_chain(dve, dve.tensor_scalar(c8[:, 0, :], p, 8.0, None, ALU.mult))
        dve_chain(dve, dve.tensor_scalar(c8[:, 1, :], p, -8.0, None, ALU.mult))

    def act_softplus(act):
        lam = par[:, PARAMS["rec_lambda"]:PARAMS["rec_lambda"] + KD]
        u = gbuf[:, 0:KD]
        act_chain(act, act.activation(u, lam, ACT.Abs))
        act_chain(act, act.activation(u, u, ACT.Exp, scale=-1.0))

    def pe_rec(pe, q):
        R, Y, L = layers["rec_r"], layers["rec_y"], layers["rec_out"]
        pe_project(pe, R, xg_hi, xg_lo, (xg_lo_ready, split_count(q)), after_first=lambda: pe_norm_sum(pe, q) if False else None)

        def gates():
            pe.wait_ge(gate_w_in, 64)
            for m in range(KD):
                pe.wait_ge(conv_step, 4 * (m + 1))
                if m >= 2:
                    pe.wait_ge(gates_sig, 2 * (m - 1))
                for g in range(2):
                    mm = pe.matmul(bank[4 + 2 * (m % 2) + g][:], gate_w[:, g, m, :], conv[:, m, :], start=True, stop=True)
                mm.then_inc(gates_mm, 1)
        pe_project(pe, Y, xg_hi, xg_lo, None, after_first=gates)
        pe_project(pe, L, yh_hi, yh_lo, (yh_lo_ready, 0))

    def dve_rec(dve):
        R, Y = layers["rec_r"], layers["rec_y"]
        dve.memset(r_pad[:, :, 0:3], 0.0).then_inc(pad_zero, 1)
        dve.wait_ge(pad_zero, 1)

        def r_tiles(b):
            for mm in range(4):
                m = b * 4 + mm
                dve.wait_ge(unit_used, b * 4 + (R.base + mm + 1))
                dve.tensor_tensor(r_pad[:, bass.ds(m, 1), 3:T + 3], bank[mm][:].unsqueeze(1),
                                  rstd[:].unsqueeze(1), ALU.mult).then_inc(taken, 1)
                dve.wait_ge(taken, b * 4 + (R.rbase + mm + 1))
                c = conv[:, bass.ds(m, 1), :]
                dve.tensor_scalar(c, r_pad[:, bass.ds(m, 1), 0:T], col("rec_conv_w", m), col("rec_conv_b", m),
                                  ALU.mult, ALU.add).then_inc(conv_step, 1)
                for k in range(1, 4):
                    dve.wait_ge(conv_step, m * 4 + k)
                    dve.scalar_tensor_tensor(c, r_pad[:, bass.ds(m, 1), k:k + T], col("rec_conv_w", m + KD * k), c,
                                             ALU.mult, ALU.add).then_inc(conv_step, 1)
        each_body(dve, R.bodies, r_tiles)
        dve.wait_ge(conv_step, 4 * KD)

        def y_tiles(b):
            for mm in range(4):
                dve.wait_ge(unit_used, b * 4 + (Y.base + mm + 1))
                dve.tensor_tensor(tile(y_rec, b * 4 + mm), bank[mm][:], rstd[:], ALU.mult).then_inc(taken, 1)
        each_body(dve, Y.bodies, y_tiles)

        def multiplier(b):
            for mm in range(2):
                m = b * 2 + mm
                dve.wait_ge(decay_step, m * 3 + 3)
                dve.scalar_tensor_tensor(tile(hs, m), sq[:, mm, :], 1.0, tile(hs, m), ALU.add, ALU.mult).then_inc(mult2_done, 1)
                dve.tensor_tensor(tile(conv, m), tile(conv, m), tile(gx, m), ALU.mult).then_inc(drive_step, 1)
        each_body(dve, KD // 2, multiplier)
        dve.wait_ge(drive_step, KD)

        def scans(m):
            dve.wait_ge(mult_done, m + 1)
            dve.tensor_tensor(tile(conv, m), tile(conv, m), tile(hs, m), ALU.mult).then_inc(drive_step, 1)
            dve.wait_ge(drive_step, m + KD + 1)
            dve.tensor_tensor_scan(tile(hs, m), tile(ga, m), tile(conv, m), 0.0, ALU.mult, ALU.add).then_inc(scan_done, 1)
            dve.wait_ge(scan_done, m + 1)
            dve.wait_ge(gelu_done, m + 1)
            dve.tensor_tensor(tile(hs, m), tile(hs, m), tile(y_rec, m), ALU.mult).then_inc(yh_done, 1)
            dve.wait_ge(yh_hi_ready, m + 1)
            dve.tensor_tensor(tile(yh_lo, m), tile(hs, m), f32(tile(yh_hi, m)), ALU.subtract).then_inc(yh_lo_ready, 1)
        each_body(dve, KD, scans)

    def act_rec(act):
        R, Y = layers["rec_r"], layers["rec_y"]
        act_bodies(act, R)
        act_bodies(act, Y, only=0)
        for m in range(KD):
            act.wait_ge(gates_mm, m + 1)
            for g, (out, bias) in enumerate(((ga, "rec_gate_a_b"), (gx, "rec_gate_x_b"))):
                act.activation(out[:, m, :], bank[4 + 2 * (m % 2) + g][:], ACT.Sigmoid, bias=col(bias, m)).then_inc(gates_sig, 1)
        act_bodies(act, Y, only=1)

        def decay(b):
            for mm in range(2):
                m = b * 2 + mm
                act.wait_ge(gates_sig, 2 * KD)
                act.activation(tile(hs, m), tile(ga, m), ACT.Tanh, scale=c8[:, 0, bass.ds(m, 1)]).then_inc(decay_step, 1)
                act.wait_ge(decay_step, m * 3 + 1)
                act.activation(tile(ga, m), tile(ga, m), ACT.Exp, scale=c8[:, 1, bass.ds(m, 1)]).then_inc(decay_step, 1)
                act.wait_ge(decay_step, m * 3 + 2)
                act.wait_ge(mult2_done, b * 2 + max(mm - 1, 0)) if mm else act.wait_ge(mult2_done, b * 2)
                act.activation(sq[:, mm, :], tile(ga, m), ACT.Square).then_inc(decay_step, 1)
        act.preload_act_table(ACT.Exp)
        for b in range(KD // 2):
            decay(b)

        def multiplier(m):
            act.wait_ge(mult2_done, m + 1)
            act.activation(tile(hs, m), tile(hs, m), ACT.Sqrt).then_inc(mult_done, 1)
        for m in range(KD):
            multiplier(m)

        def gelus(m):
            act.wait_ge(taken, m + (Y.rbase + 1))
            act.activation(tile(y_rec, m), tile(y_rec, m), ACT.Gelu_apprx_tanh).then_inc(gelu_done, 1)
        for m in range(KD):
            gelus(m)

        def split(m):
            act.wait_ge(yh_done, m + 1)
            act.activation(tile(yh_hi, m), tile(hs, m), ACT.Copy).then_inc(yh_hi_ready, 1)
        for m in range(KD):
            split(m)

    def act_load_sgu(act):
        act.dma_start(ws_raw[:].rearrange("p h t -> p (h t)"), io["sg_wsT"]).then_inc(ws_in, 16)
        act.dma_start(bsb[:].rearrange("p h t -> p (h t)"), io["sg_bs"].to_broadcast([P, D])).then_inc(ws_in, 16)
        act.dma_start(tri_f[:], io["c_tri"]).then_inc(ws_in, 16)

    def pe_sgu(pe, q):
        V, U, L = layers["sg_v"], layers["sg_u"], layers["sg_out"]
        pe.wait_ge(xg_lo_ready, split_count(q) + KD)
        pe_project_tokens(pe, V, xg_hi, xg_lo)
        pe_project(pe, U, xg_hi, xg_lo, None)
        pe.wait_ge(ws_ready, 1)
        for h in range(KD):
            if h >= 4:
                pe.wait_ge(gated, h - 3)
            for n in range(4):
                if h == 0:
                    pe.wait_ge(v_normed, n + 1)
                mm = pe.matmul(bank[4 + h % 4][:, n * P:(n + 1) * P], vt[:, n, h * P:(h + 1) * P], ws[:, h, :],
                               start=True, stop=True)
            mm.then_inc(mixed, 1)
        pe_project(pe, L, sgy_hi, sgy_lo, (sgy_lo_ready, 0))

    def dve_sgu(dve):
        V, U = layers["sg_v"], layers["sg_u"]
        dve.memset(ws[:], 0.0).then_inc(ws_zero, 1)
        dve.wait_ge(ws_zero, 1)
        dve.wait_ge(ws_in, 48)
        dve_chain(dve, dve.tensor_copy(tri[:], tri_f[:]))
        dve.copy_predicated(ws[:], tri[:].unsqueeze(1).to_broadcast([P, KD, P]), ws_raw[:]).then_inc(ws_ready, 1)

        def v_tiles(b):
            for t in range(4):
                dve.wait_ge(unit_used, b * 4 + (V.base + 4))
                dve.tensor_scalar(vt[:, t, bass.ds(b * T, T)], bank[t][:], rcol[:, t:t + 1], None, ALU.mult).then_inc(taken, 1)
        each_body(dve, V.bodies, v_tiles)
        dve.wait_ge(v_sq, 8)
        dve.tensor_tensor(vss[:, 1, 0:4], vss[:, 0, 0:4], vss[:, 0, 4:8], ALU.add).then_inc(v_sum, 1)
        dve.wait_ge(v_std, 1)
        dve.reciprocal(vss[:, 2, 0:4], vss[:, 2, 0:4]).then_inc(v_rstd, 1)
        dve.wait_ge(v_rstd, 1)
        for t in range(4):
            dve.tensor_scalar(vt[:, t, :], vt[:, t, :], vss[:, 2, t:t + 1], None, ALU.mult).then_inc(v_normed, 1)

        def u_tiles(b):
            for mm in range(4):
                dve.wait_ge(unit_used, b * 4 + (U.base + mm + 1))
                dve.tensor_tensor(tile(ug, b * 4 + mm), bank[mm][:], rstd[:], ALU.mult).then_inc(taken, 1)
        each_body(dve, U.bodies, u_tiles)
        for h in range(KD):
            g4 = gbuf[:].rearrange("p (n t) -> p n t", t=P)
            if h:
                dve.wait_ge(sgy_lo_ready, h)
            dve.wait_ge(mixed, h + 1)
            dve.scalar_tensor_tensor(g4, bank[4 + h % 4][:].rearrange("p (n t) -> p n t", t=P), col("sg_v_norm", h),
                                     bsb[:, h, :].unsqueeze(1).to_broadcast([P, 4, P]), ALU.mult, ALU.add).then_inc(gated, 1)
            dve.wait_ge(gated, h + 1)
            dve.wait_ge(u_gelu, h + 1)
            dve.tensor_tensor(ug[:, h, :], ug[:, h, :], gbuf[:], ALU.mult).then_inc(yh_done, 1)
            dve.wait_ge(sgy_hi_ready, h + 1)
            dve.tensor_tensor(sgy_lo[:, h, :], ug[:, h, :], f32(sgy_hi[:, h, :]), ALU.subtract).then_inc(sgy_lo_ready, 1)

    def act_sgu(act):
        V, U = layers["sg_v"], layers["sg_u"]
        for b in range(V.bodies):
            act_bodies(act, V, only=b)
            for t in range(4):
                act.wait_ge(taken, V.rbase + 4 * b + t + 1)
                c = vt[:, t, b * T:(b + 1) * T]
                act.activation(c, c, ACT.Gelu_apprx_tanh).then_inc(v_gelu, 1)
                act.wait_ge(v_gelu, 4 * b + t + 1)
                act.wait_ge(v_sq, 4 * b + t)
                act.activation(sq[:, 0, :], c, ACT.Square, accum_out=vss[:, 0, 4 * b + t:4 * b + t + 1]).then_inc(v_sq, 1)

        def gelus(b, i):
            act.wait_ge(taken, b * 4 + (U.rbase + i + 1))
            t = tile(ug, b * 4 + i)
            act.activation(t, t, ACT.Gelu_apprx_tanh).then_inc(u_gelu, 1)
        act.wait_ge(v_sum, 1)
        act.activation(vss[:, 2, 0:4], vss[:, 1, 0:4], ACT.Sqrt, bias=eps[:], scale=1.0 / D).then_inc(v_std, 1)
        act.preload_act_table(ACT.Gelu_apprx_tanh)
        act_bodies(act, U, gelus)
        for h in range(KD):
            act.wait_ge(yh_done, KD + h + 1)
            act.activation(sgy_hi[:, h, :], ug[:, h, :], ACT.Copy).then_inc(sgy_hi_ready, 1)

    def dve_final(dve, gain):
        q = FINAL + 1
        dve.memset(ss[:], 0.0).then_inc(ss_added, 1)

        def body(b):
            for mm in range(2):
                m = b * 2 + mm
                dve.scalar_tensor_tensor(tile(x, m), tile(x, m), col("final_norm", m), rstd[:], ALU.mult, ALU.mult).then_inc(final_step, 1)
                dve.wait_ge(final_step, m + 1)
                dve_norm_tile(dve, q, gain, m, mm)
        each_body(dve, KD // 2, body)
        dve_norm_rstd(dve, q)

    def act_final(act, gain):
        q = FINAL + 1

        def body(b):
            for mm in range(2):
                act.wait_ge(final_step, b * 2 + mm + 1)
                act_norm_tile(act, q, gain, b * 2 + mm, mm)
        each_body(act, KD // 2, body)
        act_norm_std(act, q)

    def done(eng, ins, sem, n):
        ins.then_inc(sem, 1)
        eng.wait_ge(sem, n)

    def bcast(ap, n):
        return ap.unsqueeze(2).to_broadcast([ap.shape[0], ap.shape[1], n])

    MIX_LOADS = 10

    def act_load_mix(act):
        for dst, src in ((sel8[:].rearrange("p h t -> p (h t)"), "c_sel8"), (pack[:], "c_pack"),
                         (ff_w[:].rearrange("p k h -> p (k h)"), "ff_w"), (causal[:], "c_causal"), (ff_b[:], "ff_b"),
                         (spread[:], "c_spread"), (s5_b[:, 0].rearrange("p t h -> p (t h)"), "s5_b_re"),
                         (s5_b[:, 1].rearrange("p t h -> p (t h)"), "s5_b_im"),
                         (s5_c[:, 0].rearrange("p t h -> p (t h)"), "s5_c_re"),
                         (s5_c[:, 1].rearrange("p t h -> p (t h)"), "s5_c_im")):
            act.dma_start(dst, io[src]).then_inc(mix_in, 16)

    def pe_mix_a(pe):
        QK, V, S = layers["fox_qk"], layers["fox_v"], layers["s5_in"]
        pe_project(pe, QK, xg_hi, xg_lo, (xg_lo_ready, split_count(FINAL + 1)))
        pe.wait_ge(mix_in, 16 * MIX_LOADS)
        for k in range(KD):
            pe.matmul(bank[5][0:8, :], ff_w[:, k, :], f32(xg_hi[:, k, :]), start=k == 0, stop=False)
            mm = pe.matmul(bank[5][0:8, :], ff_w[:, k, :], f32(xg_lo[:, k, :]), start=False, stop=k == KD - 1)
        mm.then_inc(ff_mm, 1)
        for i in range(8):
            pe.wait_ge(qk_sq, i + 1)
            pe.matmul(bank[6][0:16, :], pack[:, 16 - 2 * i:32 - 2 * i], sq[:, i % 2, :],
                      start=i == 0, stop=i == 7).then_inc(qk_ss, 1)
        pe_project_tokens(pe, V, xg_hi, xg_lo)
        for i in range(8):
            if i == 0:
                pe.wait_ge(qk_rstd, 1)
            if i >= 2:
                pe.wait_ge(qk_scaled, i - 1)
            pe.matmul(bank[6 + i % 2][:], spread[:, i * P:(i + 1) * P], qk_r[:], start=True, stop=True).then_inc(qk_spread, 1)
        pe_project(pe, S, xg_hi, xg_lo, None)
        pe.wait_ge(s5_bx_ready, 4)
        pe.wait_ge(qk_scaled, 8)
        for c in range(2):
            for j in range(4):
                mm = pe.transpose(bank[6 + c][:, j * P:(j + 1) * P],
                                  s5_bx[:, c, 4 * j:4 * j + 4, :].rearrange("p t h -> p (t h)"), ident[:])
            mm.then_inc(s5_bt_mm, 1)

    def dve_mix_a(dve):
        QK, V, S = layers["fox_qk"], layers["fox_v"], layers["s5_in"]

        def qk_tiles(b):
            for mm in range(4):
                dve.wait_ge(unit_used, b * 4 + (QK.base + mm + 1))
                dve.tensor_tensor(tile(qk, b * 4 + mm), bank[mm][:], rstd[:], ALU.mult).then_inc(taken, 1)
        each_body(dve, QK.bodies, qk_tiles)
        dve.wait_ge(ff_mm, 1)
        z, l = gbuf[0:8, :], ubuf[0:8, :]
        dve_chain(dve, dve.tensor_tensor(z, bank[5][0:8, :], rstd[0:8, :], ALU.mult))
        done(dve, dve.tensor_scalar(z, z, ff_b[:, 0:1], None, ALU.add), ff_z, 1)
        dve.wait_ge(qk_std, 1)
        done(dve, dve.reciprocal(qk_r[:], qk_r[:]), qk_rstd, 1)
        dve.wait_ge(ff_ln, 1)
        dve_chain(dve, dve.scalar_tensor_tensor(l, z, 0.0, l, ALU.min, ALU.subtract))
        dve_chain(dve, dve.tensor_scalar(l, l, -1.0, None, ALU.mult))
        done(dve, dve.tensor_tensor_scan(negc[:], ones[0:8, 0:1].to_broadcast([8, T]), l, 0.0, ALU.mult, ALU.add), negc_ready, 1)
        dve_s5_setup(dve)

        for t in range(4):
            dve.wait_ge(unit_used, V.base + 4)
            dve.tensor_scalar(vtok[:, t, :], bank[t][:], rcol[:, t:t + 1], None, ALU.mult).then_inc(taken, 1)
        for i in range(8):
            dve.wait_ge(qk_spread, i + 1)
            dve.scalar_tensor_tensor(qk[:, i, :], qk[:, i, :], col("fox_qnorm_2" if i < 4 else "fox_knorm_2"),
                                     bank[6 + i % 2][:], ALU.mult, ALU.mult).then_inc(qk_scaled, 1)
        for m in range(4):
            dve.wait_ge(unit_used, S.base + m + 1)
            dve.tensor_tensor(su[:, m, :], bank[m][:], rstd[:], ALU.mult).then_inc(taken, 1)
        for c in range(2):
            dve.wait_ge(s5_bt_mm, c + 1)
            dve.tensor_copy(s5_bt[:, c].rearrange("p j t -> p (j t)"), bank[6 + c][:]).then_inc(s5_bt_ready, 1)

    def act_mix_a(act):
        QK, V, S = layers["fox_qk"], layers["fox_v"], layers["s5_in"]
        act.activation(s5v(0), parv("s5_log_dt_2"), ACT.Exp).then_inc(s5_act, 1)
        act_bodies(act, QK)
        for i in range(8):
            act.wait_ge(taken, QK.rbase + i + 1)
            if i >= 2:
                act.wait_ge(qk_ss, i - 1)
            act.activation(sq[:, i % 2, :], qk[:, i, :], ACT.Square).then_inc(qk_sq, 1)
        act_bodies(act, V)
        act.wait_ge(ff_z, 1)
        z, l = gbuf[0:8, :], ubuf[0:8, :]
        act_chain(act, act.activation(l, z, ACT.Abs))
        act_chain(act, act.activation(l, l, ACT.Exp, scale=-1.0))
        act.activation(l, l, ACT.Ln, bias=1.0).then_inc(ff_ln, 1)
        act.wait_ge(qk_ss, 8)
        act.activation(qk_r[:], bank[6][0:16, :], ACT.Sqrt, bias=eps[0:16, :], scale=1.0 / 64).then_inc(qk_std, 1)
        act.wait_ge(s5_dve, 2)
        act.activation(s5v(3), s5v(2), ACT.Exp).then_inc(s5_act, 1)
        act.wait_ge(s5_dve, 3)
        act.activation(s5v(7), s5v(5), ACT.Sin).then_inc(s5_act, 1)
        act.activation(s5v(8), s5v(5), ACT.Sin, scale=0.5).then_inc(s5_act, 1)
        act_bodies(act, S)

    def s5v(i):
        return s5p[:, i, :]

    def parv(name):
        return par[:, PARAMS[name]:PARAMS[name] + 16]

    def dve_s5_setup(dve):
        are, aim = parv("s5_a_re_2"), parv("s5_a_im_2")

        def op(out, a, b, alu):
            dve_chain(dve, dve.tensor_tensor(out, a, b, alu))
        dve.wait_ge(s5_act, 1)
        done(dve, dve.tensor_tensor(s5v(1), s5v(0), aim, ALU.mult), s5_dve, 1)
        done(dve, dve.tensor_tensor(s5v(2), s5v(0), are, ALU.mult), s5_dve, 2)
        dve_chain(dve, dve.tensor_scalar(s5v(4), s5v(1), 1.0 / (2 * np.pi), ROUND, ALU.mult, ALU.add))
        dve_chain(dve, dve.tensor_scalar(s5v(4), s5v(4), ROUND, None, ALU.subtract))
        dve_chain(dve, dve.scalar_tensor_tensor(s5v(5), s5v(4), -TWO_PI[0], s5v(1), ALU.mult, ALU.add))
        dve_chain(dve, dve.scalar_tensor_tensor(s5v(5), s5v(4), -TWO_PI[1], s5v(5), ALU.mult, ALU.add))
        dve_chain(dve, dve.scalar_tensor_tensor(s5v(5), s5v(4), -TWO_PI[2], s5v(5), ALU.mult, ALU.add))
        done(dve, dve.tensor_scalar(s5v(5), s5v(5), PI_BELOW, -PI_BELOW, ALU.min, ALU.max), s5_dve, 3)
        dve_chain(dve, dve.tensor_scalar(s5v(6), s5v(5), 1.0 / (2 * np.pi), None, ALU.mult))
        dve.wait_ge(s5_act, 4)
        op(s5v(9), s5v(8), s5v(8), ALU.mult)
        dve_chain(dve, dve.tensor_scalar(s5v(9), s5v(9), -2.0, 1.0, ALU.mult, ALU.add))
        op(s5v(10), s5v(3), s5v(9), ALU.mult)
        op(s5v(11), s5v(3), s5v(7), ALU.mult)
        dve_chain(dve, dve.tensor_scalar(s5v(10), s5v(10), 1.0, None, ALU.subtract))
        op(s5v(12), are, are, ALU.mult)
        op(s5v(13), aim, aim, ALU.mult)
        op(s5v(12), s5v(12), s5v(13), ALU.add)
        dve_chain(dve, dve.reciprocal(s5v(12), s5v(12)))
        op(s5v(13), s5v(10), are, ALU.mult)
        op(s5v(14), s5v(11), aim, ALU.mult)
        op(s5v(13), s5v(13), s5v(14), ALU.add)
        op(s5v(13), s5v(13), s5v(12), ALU.mult)
        op(s5v(14), s5v(11), are, ALU.mult)
        op(s5v(15), s5v(10), aim, ALU.mult)
        op(s5v(14), s5v(14), s5v(15), ALU.subtract)
        op(s5v(14), s5v(14), s5v(12), ALU.mult)
        cr, ci = bcast(s5v(13), 16), bcast(s5v(14), 16)
        dve.wait_ge(mix_in, 16 * MIX_LOADS)
        dve_chain(dve, dve.memset(s5_bx[:], 0.0))
        dve_chain(dve, dve.memset(s5_cx[:], 0.0))
        halves = (slice(0, 64), slice(0, 16)), (slice(64, 128), slice(16, 32))
        for c, (a0, a1, alu) in enumerate(((cr, ci, ALU.subtract), (ci, cr, ALU.add))):
            op(s5_t[:, 0], s5_b[:, 0], a0, ALU.mult)
            op(s5_t[:, 1], s5_b[:, 1], a1, ALU.mult)
            for n, (p, h) in enumerate(halves):
                done(dve, dve.tensor_tensor(s5_bx[p, c, :, h], s5_t[p, 0], s5_t[p, 1], alu), s5_bx_ready, 2 * c + n + 1)
        for p, h in halves:
            dve_chain(dve, dve.tensor_copy(s5_cx[p, 0, :, h], s5_c[p, 0]))
            dve_chain(dve, dve.tensor_scalar(s5_cx[p, 1, :, h], s5_c[p, 1], -1.0, None, ALU.mult))

    def pe_fox(pe):
        pe.wait_ge(negc_ready, 1)
        pe.wait_ge(qk_scaled, 8)
        pe.wait_ge(taken, layers["fox_v"].rbase + 4)
        pe.wait_ge(s5_bt_ready, 2)

        def scores(n):
            h, qi = n // 4, n % 4
            o, keys = 64 * (h % 2), (qi + 1) * P
            out = bank[4 + n % 2]
            if n >= 2:
                pe.wait_ge(att_exp, n - 1)
            pe.matmul(out[:, 0:keys], qk[o:o + 64, h // 2, qi * P:keys], qk[o:o + 64, 4 + h // 2, 0:keys],
                      start=True, stop=False)
            pe.matmul(out[:, 0:keys], sel8[:, h, :], negc[:, 0:keys], start=False, stop=False)
            pe.matmul(out[:, qi * P:keys], ident[:], causal[:], start=False, stop=True).then_inc(att_s, 1)

        scores(0)
        for n in range(32):
            h, qi = n // 4, n % 4
            if n < 31:
                scores(n + 1)
            pe.wait_ge(att_p, n + 1)
            if n >= 1:
                pe.wait_ge(att_tc, n)
            for kb in range(qi + 1):
                mm = pe.transpose(bank[6][:, kb * P:(kb + 1) * P], prob[:, n % 2, kb * P:(kb + 1) * P], ident[:])
            mm.then_inc(att_t, 1)
            if n % 8 == 0 and n:
                pe.wait_ge(fox_lo, n // 8)
            pe.wait_ge(att_tc, n + 1)
            o = 64 * (h % 2)
            for kb in range(qi + 1):
                mm = pe.matmul(bank[7][o:o + 64, qi * P:(qi + 1) * P], vtok[:, kb, h * 64:(h + 1) * 64],
                               probT[:, n % 2, kb * P:(kb + 1) * P], start=kb == 0, stop=kb == qi)
            mm.then_inc(att_o, 1)

    def dve_fox(dve):
        def row_max(n):
            keys = (n % 4 + 1) * P
            dve.wait_ge(att_s, n + 1)
            dve_chain(dve, dve.reduce_max(att_m[:, n:n + 1], bank[4 + n % 2][:, 0:keys], AX.X, negate=True))
            dve.tensor_scalar(att_m[:, n:n + 1], att_m[:, n:n + 1], 0.125, None, ALU.mult).then_inc(att_nmax, 1)

        row_max(0)
        for n in range(32):
            if n < 31:
                row_max(n + 1)
            keys = (n % 4 + 1) * P
            dve.wait_ge(att_exp, n + 1)
            dve_chain(dve, dve.reciprocal(att_l[:, n:n + 1], att_l[:, n:n + 1]))
            dve.tensor_scalar(prob[:, n % 2, 0:keys], prob[:, n % 2, 0:keys], att_l[:, n:n + 1], None, ALU.mult).then_inc(att_p, 1)
            if n % 8 == 7:
                i = n // 8
                dve.wait_ge(fox_hi, i + 1)
                dve.tensor_tensor(y0_lo[:, i, :], bank[7][:], f32(y0_hi[:, i, :]), ALU.subtract).then_inc(fox_lo, 1)

    def act_fox(act):
        def exps(n):
            keys = (n % 4 + 1) * P
            act.wait_ge(att_nmax, n + 1)
            if n >= 2:
                act.wait_ge(att_t, n - 1)
            act.activation(prob[:, n % 2, 0:keys], bank[4 + n % 2][:, 0:keys], ACT.Exp, bias=att_m[:, n:n + 1],
                           scale=0.125, accum_out=att_l[:, n:n + 1]).then_inc(att_exp, 1)

        exps(0)
        for n in range(32):
            if n < 31:
                exps(n + 1)
            keys = (n % 4 + 1) * P
            act.wait_ge(att_t, n + 1)
            if n >= 2:
                act.wait_ge(att_o, n - 1)
            act.activation(probT[:, n % 2, 0:keys], bank[6][:, 0:keys], ACT.Copy).then_inc(att_tc, 1)
            if n % 8 == 7:
                act.wait_ge(att_o, n + 1)
                act.activation(y0_hi[:, n // 8, :], bank[7][:], ACT.Copy).then_inc(fox_hi, 1)

    def pe_s5(pe):
        QFG, V = layers["hg_qfg"], layers["hg_v"]

        def outputs(t):
            j = 32 * (t % 4)
            out = bank[6 + (t // 4) % 2][j:j + 32, :]
            if t >= 8 and t % 4 == 0:
                pe.wait_ge(s5_y, t // 4 - 1)
            for n, c in enumerate((0, 0, 1, 1)):
                pe.wait_ge(s5_prod, 4 * t + n + 1)
                mm = pe.matmul(out, s5_cx[:, c, t, :], (gbuf[:], ubuf[:], sq[:, 0, :], sq[:, 1, :])[n],
                               start=n == 0, stop=n == 3)
            mm.then_inc(s5_ymm, 1)

        for u in range(16):
            L = QFG if u < 12 else V
            i = u - (0 if u < 12 else 12)
            if u < 12:
                project_unit(pe, L, i // 4, i % 4, xg_hi, xg_lo)
            else:
                pe_tokens_unit(pe, L, 0, i, xg_hi, xg_lo)
            t, j = u, 32 * (u % 4)
            if t >= 1:
                pe.wait_ge(s5_step, 6 * t - 2)
            if t == 0:
                pe.wait_ge(s5_bt_ready, 2)
                pe.wait_ge(taken, layers["s5_in"].rbase + 4)
            for c in range(2):
                mm = pe.matmul(bank[4 + c][:], s5_bt[j:j + 32, c, t // 4, :], su[j:j + 32, t // 4, :], start=True, stop=True)
            mm.then_inc(s5_drive, 1)
            if t >= 1:
                outputs(t - 1)
        outputs(15)

    def dve_s5(dve):
        QFG, V = layers["hg_qfg"], layers["hg_v"]

        def turns(t):
            tok = s5p[:, 6, t:t + 1]
            if t >= 1:
                dve.wait_ge(s5_rot, 3 * t)
            dve_chain(dve, dve.tensor_scalar(turn[:], iota[:], tok, ROUND, ALU.mult, ALU.add))
            dve_chain(dve, dve.tensor_scalar(turn[:], turn[:], ROUND, None, ALU.subtract))
            dve.scalar_tensor_tensor(turn[:], iota[:], tok, turn[:], ALU.mult, ALU.subtract).then_inc(s5_turn, 1)

        dve.wait_ge(iota_in, 16)
        turns(0)
        for u in range(16):
            if u < 12:
                dve.wait_ge(unit_used, QFG.base + u + 1)
                dve.tensor_tensor(hq[:, u, :], bank[u % 4][:], rstd[:], ALU.mult).then_inc(taken, 1)
            t = u
            sin, cos = rot[:, t % 2, 0, :], rot[:, t % 2, 1, :]
            dr, di = bank[4][:], bank[5][:]
            gr, gi, m0, m1 = s5_g[:, 0, :], s5_g[:, 1, :], s5_m[:, 0, :], s5_m[:, 1, :]
            n0 = 6 * t
            dve.wait_ge(s5_rot, 3 * t + 3)
            dve_chain(dve, dve.tensor_scalar(cos, cos, -2.0, 1.0, ALU.mult, ALU.add))
            dve.wait_ge(s5_drive, t + 1)
            dve.tensor_tensor(m0, dr, cos, ALU.mult).then_inc(s5_step, 1)
            dve.tensor_tensor(m1, di, sin, ALU.mult).then_inc(s5_step, 1)
            dve.tensor_tensor(gi, di, cos, ALU.mult).then_inc(s5_step, 1)
            dve.tensor_tensor(gr, dr, sin, ALU.mult).then_inc(s5_step, 1)
            dve.wait_ge(s5_step, n0 + 2)
            dve_chain(dve, dve.tensor_tensor(m0, m0, m1, ALU.add))
            dve.wait_ge(s5_step, n0 + 4)
            dve_chain(dve, dve.tensor_tensor(m1, gi, gr, ALU.subtract))
            mag = s5p[:, 3, t:t + 1].to_broadcast([P, T])
            dve.tensor_tensor_scan(gr, mag, m0, 0.0, ALU.mult, ALU.add).then_inc(s5_step, 1)
            dve.tensor_tensor_scan(gi, mag, m1, 0.0, ALU.mult, ALU.add).then_inc(s5_step, 1)
            if t >= 1:
                dve.wait_ge(s5_ymm, t)
            dve.wait_ge(s5_step, n0 + 5)
            dve.tensor_tensor(gbuf[:], gr, cos, ALU.mult).then_inc(s5_prod, 1)
            dve.wait_ge(s5_step, n0 + 6)
            dve.scalar_tensor_tensor(ubuf[:], gi, -1.0, sin, ALU.mult, ALU.mult).then_inc(s5_prod, 1)
            dve.tensor_tensor(sq[:, 0, :], gr, sin, ALU.mult).then_inc(s5_prod, 1)
            dve.tensor_tensor(sq[:, 1, :], gi, cos, ALU.mult).then_inc(s5_prod, 1)
            if t < 15:
                turns(t + 1)
            dve.wait_ge(s5_prod, 4 * t + 4)
            if t % 4 == 0 and t:
                s5_result(dve, t // 4 - 1)
        s5_result(dve, 3)
        for t in range(4):
            dve.wait_ge(unit_used, V.base + 4)
            dve.tensor_scalar(hv[:, t, :], bank[t][:], rcol[:, t:t + 1], None, ALU.mult).then_inc(taken, 1)

    def s5_result(dve, i):
        dve.wait_ge(s5_ymm, 4 * i + 4)
        dve.scalar_tensor_tensor(su[:, i, :], su[:, i, :], col("s5_d_2", i), bank[6 + i % 2][:],
                                 ALU.mult, ALU.add).then_inc(s5_y, 1)

    def act_s5(act):
        QFG, V = layers["hg_qfg"], layers["hg_v"]
        act.dma_start(iota[:], io["c_iota"]).then_inc(iota_in, 16)
        act.preload_act_table(ACT.Sin)

        def rots(t):
            act.wait_ge(s5_turn, t + 1)
            if t >= 2:
                act.wait_ge(s5_prod, 4 * (t - 1))
            sin, cos = rot[:, t % 2, 0, :], rot[:, t % 2, 1, :]
            act.activation(sin, turn[:], ACT.Sin, scale=TURN).then_inc(s5_rot, 1)
            act.activation(cos, turn[:], ACT.Sin, scale=TURN / 2).then_inc(s5_rot, 1)
            act.wait_ge(s5_rot, 3 * t + 2)
            act.activation(cos, cos, ACT.Square).then_inc(s5_rot, 1)

        rots(0)

        def work(b, i):
            u = 4 * b + i
            if u < 15:
                rots(u + 1)
        for b in range(3):
            act_bodies(act, QFG, work, only=b)
        act_bodies(act, V, lambda b, i: work(3, i), only=0)
        for i in range(4):
            act.wait_ge(s5_y, i + 1)
            act.activation(su[:, i, :], su[:, i, :], ACT.Gelu_apprx_tanh).then_inc(z_ready, 1)
        for i in range(4):
            act.wait_ge(z_ready, i + 1)
            act.activation(y1_hi[:, i, :], su[:, i, :], ACT.Copy).then_inc(z_hi_ready, 1)

    def dve_z(dve):
        for i in range(4):
            dve.wait_ge(z_hi_ready, i + 1)
            dve.tensor_tensor(y1_lo[:, i, :], su[:, i, :], f32(y1_hi[:, i, :]), ALU.subtract).then_inc(z_lo_ready, 1)

    def pe_glu(pe):
        L = layers["s5_glu"]
        for i in range(4):
            pe.wait_ge(w_lo_ready, L.base + i + 1)
            pe.wait_ge(taken, L.rbase + i + 1 - RING)
            for k in range(4):
                if i == 0:
                    pe.wait_ge(z_lo_ready, k + 1)
                mm = three_passes(pe, bank[i][:], i, k, y1_hi[:, k, :], y1_lo[:, k, :], k == 0, k == 3)
            mm.then_inc(unit_used, 1)

    def dve_glu(dve):
        L = layers["s5_glu"]
        buf = (gbuf[:], ubuf[:])
        for i in range(4):
            dve.wait_ge(unit_used, L.base + i + 1)
            if i >= 2:
                dve.wait_ge(glu_out, i - 1)
            done(dve, dve.tensor_copy(buf[i % 2], bank[i][:]), taken, L.rbase + i + 1)
            dve.wait_ge(glu_sig, i + 1)
            dve.tensor_tensor(su[:, i, :], su[:, i, :], buf[i % 2], ALU.mult).then_inc(glu_out, 1)
        for i in range(4):
            dve.wait_ge(s5_hi, i + 1)
            dve.tensor_tensor(y1_lo[:, i, :], su[:, i, :], f32(y1_hi[:, i, :]), ALU.subtract).then_inc(s5_lo, 1)

    def act_glu(act):
        L = layers["s5_glu"]
        buf = (gbuf[:], ubuf[:])

        def sigmoids(b, i):
            act.wait_ge(taken, L.rbase + i + 1)
            act.activation(buf[i % 2], buf[i % 2], ACT.Sigmoid, bias=col("s5_b_glu_2", i)).then_inc(glu_sig, 1)
        act_bodies(act, L, sigmoids)
        act.wait_ge(unit_used, L.base + 4)
        for i in range(4):
            act.wait_ge(glu_out, i + 1)
            act.activation(y1_hi[:, i, :], su[:, i, :], ACT.Copy).then_inc(s5_hi, 1)


    def pe_merge_gate(pe, b, p, i):
        L = layers[f"merge{b}"]
        r = (3 * p + i) % RING
        pe.wait_ge(w_lo_ready, L.base + 3 * p + i + 1)
        pe.wait_ge(taken, L.rbase + 4 * p + i + 1 - RING)
        for k in range(KD):
            mm = three_passes(pe, bank[i][:], r, k, xg_hi[:, k, :], xg_lo[:, k, :], k == 0, k == KD - 1)
        mm.then_inc(unit_used, 1)

    def pe_merge_branch(pe, b, p, y_hi, y_lo, ready):
        L = layers[f"merge{b}"]
        r = (3 * p + 2) % RING
        pe.wait_ge(w_lo_ready, L.base + 3 * p + 3)
        pe.wait_ge(ready, 4)
        for i in range(2):
            pe.wait_ge(taken, L.rbase + 4 * p + 3 + i - RING)
            for k in range(4):
                mm = three_passes(pe, bank[2 + i][:], r, 4 * i + k, y_hi[:, k, :], y_lo[:, k, :], k == 0, k == 3)
        mm.then_inc(unit_used, 1)

    gate_buf = (gbuf, ubuf)

    def dve_merge_gate(dve, b, p, i):
        L = layers[f"merge{b}"]
        if i == 0:
            dve.wait_ge(taken, L.rbase + 4 * p)
            if b:
                dve.wait_ge(merge_step, 2 * (4 * (b - 1) + p))
        dve.wait_ge(unit_used, L.base + 3 * p + i + 1)
        dve.tensor_tensor(gate_buf[i][:], bank[i][:], rstd[:], ALU.mult).then_inc(taken, 1)

    def dve_merge_branch(dve, b, p):
        L = layers[f"merge{b}"]
        dve.wait_ge(unit_used, L.base + 3 * p + 3)
        for i in range(2):
            m = 2 * p + i
            dve.wait_ge(gate_tanh, 2 * (4 * b + p) + i + 1)
            dst = merged[:, m, :] if b == 0 else gate_buf[i][:]
            dve.scalar_tensor_tensor(dst, gate_buf[i][:], 1.0, bank[2 + i][:], ALU.add, ALU.mult).then_inc(taken, 1)
            dve.wait_ge(taken, L.rbase + 4 * p + 3 + i)
            if b:
                dve.tensor_tensor(merged[:, m, :], merged[:, m, :], gate_buf[i][:], ALU.add).then_inc(merge_step, 1)

    def act_merge_split(act, b, p, i):
        split_hi(act, layers[f"merge{b}"], 0, 3 * p + i + AHEAD)

    def act_merge_gate(act, b, p, i):
        L = layers[f"merge{b}"]
        act.wait_ge(taken, L.rbase + 4 * p + i + 1)
        act.activation(gate_buf[i][:], gate_buf[i][:], ACT.Tanh, scale=0.5).then_inc(gate_tanh, 1)

    m_hi = place("m_hi", [P, KD, T], F32R, at=work)
    m_lo = place("m_lo", [P, KD, T], F32R, at=work + 16 * KB)
    x_gain = {"k": "x_knorm_2", "q": "x_qnorm_2"}

    def act_load_mem(act):
        act.wait_ge(hg_lo, 4)
        for k in range(KD):
            act.dma_start(memx[:, k, :], io["memT"][k * P:(k + 1) * P, :]).then_inc(mem_in, 16)
        act.dma_start(x_sel[:].rearrange("p h t -> p (h t)"), io["c_selx"]).then_inc(mem_in, 16)
        act.dma_start(pick[:], io["c_pick"]).then_inc(mem_in, 16)

    def act_mem(act):
        act.wait_ge(mem_in, 16 * (KD + 2))
        for k in range(KD):
            act.activation(msq[:, k, :], memx[:, k, :], ACT.Square).then_inc(mem_sq, 1)
            act.activation(mem_hi[:, k, :], memx[:, k, :], ACT.Copy, scale=col("norm_mem_2", k)).then_inc(mem_hi_ready, 1)
        act.wait_ge(mem_ss, 1)
        act.activation(rstd_m[:], bank[4][:, 0:NMEM], ACT.Sqrt, bias=eps[:], scale=1.0 / D).then_inc(mem_std, 1)
        act.wait_ge(mem_ss, 2)
        act.activation(rcol_m[:], bank[5][:, 0:2], ACT.Sqrt, bias=eps[:], scale=1.0 / D).then_inc(mem_std, 1)

    def dve_mem(dve):
        for k in range(KD):
            dve.wait_ge(mem_hi_ready, k + 1)
            dve.scalar_tensor_tensor(mem_lo[:, k, :], memx[:, k, :], col("norm_mem_2", k), f32(mem_hi[:, k, :]),
                                     ALU.mult, ALU.subtract).then_inc(mem_lo_ready, 1)
        dve.wait_ge(mem_std, 1)
        dve.reciprocal(rstd_m[:], rstd_m[:]).then_inc(mem_rstd, 1)
        dve.wait_ge(mem_std, 2)
        dve.reciprocal(rcol_m[:], rcol_m[:]).then_inc(mem_rstd, 1)
        dve.wait_ge(mem_rstd, 2)

    def pe_mem(pe):
        pe.wait_ge(mem_sq, KD)
        for k in range(KD):
            mm = pe.matmul(bank[4][:, 0:NMEM], ones[:], msq[:, k, :], start=k == 0, stop=k == KD - 1)
        mm.then_inc(mem_ss, 1)
        for t in range(2):
            for k in range(KD):
                mm = pe.matmul(bank[5][:, t:t + 1], msq[:, k, t * P:(t + 1) * P], ones[:, 0:1], start=k == 0, stop=k == KD - 1)
        mm.then_inc(mem_ss, 1)

    def pe_e(pe):
        K, V, O = layers["xk"], layers["xv"], layers["w_out"]
        for p in range(4):
            if p:
                pe_merge_gate(pe, 2, p, 0)
                pe_merge_gate(pe, 2, p, 1)
            pe_merge_branch(pe, 2, p, *merge_y(2))
            if p == 1:
                pe_mem(pe)
        pe_project(pe, K, mem_hi, mem_lo, (mem_lo_ready, 0), width=NMEM)
        pe_project_tokens(pe, V, mem_hi, mem_lo, 2)
        pe_head_squares(pe, "k")
        pe_project(pe, O, m_hi, m_lo, (m_lo_ready, 0), after_first=lambda: pe_head_spread(pe, "k"))

    def dve_e(dve):
        K, V, O = layers["xk"], layers["xv"], layers["w_out"]
        for p in range(4):
            dve_merge_gate(dve, 2, p, 0)
            dve_merge_gate(dve, 2, p, 1)
            dve_merge_branch(dve, 2, p)
            if p == 1:
                dve_mem(dve)

        def k_tiles(b):
            for mm in range(4):
                m = b * 4 + mm
                dve.wait_ge(unit_used, b * 4 + (K.base + mm + 1))
                dve.tensor_tensor(kx[:, bass.ds(m, 1), :], bank[mm][:, 0:NMEM].unsqueeze(1), rstd_m[:].unsqueeze(1),
                                  ALU.mult).then_inc(taken, 1)
        each_body(dve, K.bodies, k_tiles)
        for m in range(KD):
            dve.wait_ge(m_hi_ready, m + 1)
            dve.scalar_tensor_tensor(m_lo[:, m, :], merged[:, m, :], 0.5, f32(m_hi[:, m, :]), ALU.mult, ALU.subtract).then_inc(m_lo_ready, 1)

        def v_tiles(b):
            for t in range(2):
                dve.wait_ge(unit_used, b * 4 + (V.base + 4))
                dve.tensor_scalar(vx[:, t, b * T:(b + 1) * T], bank[2 * b + t][:], rcol_m[:, t:t + 1], None, ALU.mult).then_inc(taken, 1)
        for b in range(V.bodies):
            v_tiles(b)
        dve_head_rstd(dve, "k")

    def act_e(act):
        K, V = layers["xk"], layers["xv"]
        for p in range(4):
            for i in range(3):
                act_merge_split(act, 2, p, i)
                if i < 2:
                    act_merge_gate(act, 2, p, i)
            if p == 0:
                act_load_mem(act)
            if p == 1:
                act_mem(act)
        for m in range(KD):
            act.wait_ge(merge_step, KD + m + 1)
            if m == 0:
                act.wait_ge(unit_used, layers["merge2"].base + 12)
            act.activation(m_hi[:, m, :], merged[:, m, :], ACT.Copy, scale=0.5).then_inc(m_hi_ready, 1)
        act_bodies(act, K)
        act_bodies(act, V)
        act_head_squares(act, "k")

    def head_norm(which):
        return (kx, NMEM, 0) if which == "k" else (qx, T, 1)

    def act_head_squares(act, which):
        t, n, later = head_norm(which)
        L = layers["xk" if which == "k" else "xq"]
        for i in range(KD):
            act.wait_ge(taken, L.rbase + i + 1)
            if i >= 2:
                act.wait_ge(xn_ss, KD * later + i - 1)
            act.activation(sq[:, i % 2, 0:n], t[:, i, :], ACT.Square).then_inc(xn_sq, 1)
        act.wait_ge(xn_ss, KD * later + KD)
        act.activation(x_r[:, 0:n], bank[6][0:4, 0:n], ACT.Sqrt, bias=eps[0:4, :], scale=1.0 / (2 * P)).then_inc(xn_std, 1)

    def pe_head_squares(pe, which):
        t, n, later = head_norm(which)
        for i in range(KD):
            pe.wait_ge(xn_sq, KD * later + i + 1)
            pe.matmul(bank[6][0:4, 0:n], pick[:, 4 - i // 2:8 - i // 2], sq[:, i % 2, 0:n],
                      start=i == 0, stop=i == KD - 1).then_inc(xn_ss, 1)

    def pe_head_spread(pe, which):
        t, n, later = head_norm(which)
        pe.wait_ge(xn_rstd, later + 1)
        for h in range(4):
            s = 4 * later + h
            if s >= 2:
                pe.wait_ge(xn_scaled, 2 * (s - 1))
            pe.matmul(bank[6 + h % 2][:, 0:n], x_sel[:, h, :], x_r[:, 0:n], start=True, stop=True).then_inc(xn_spread, 1)

    def dve_head_rstd(dve, which):
        t, n, later = head_norm(which)
        dve.wait_ge(xn_std, later + 1)
        dve.reciprocal(x_r[:, 0:n], x_r[:, 0:n]).then_inc(xn_rstd, 1)
        for h in range(4):
            dve.wait_ge(xn_spread, 4 * later + h + 1)
            for i in range(2):
                m = 2 * h + i
                dve.scalar_tensor_tensor(t[:, m, :], t[:, m, :], col(x_gain[which], i), bank[6 + h % 2][:, 0:n],
                                         ALU.mult, ALU.mult).then_inc(xn_scaled, 1)

    FOX_STEPS = 32

    def pe_cross(pe):
        Q, O = layers["xq"], layers["xo"]
        pe_project(pe, Q, xg_hi, xg_lo, (xg_lo_ready, split_count(8)))
        pe_head_squares(pe, "q")
        pe_head_spread(pe, "q")

        def scores(n):
            h, qi = n // 4, n % 4
            if n >= 2:
                pe.wait_ge(att_exp, FOX_STEPS + n - 1)
            if qi == 0:
                pe.wait_ge(xn_scaled, KD + 2 * h + 2)
            for i in range(2):
                mm = pe.matmul(bank[4 + n % 2][:, 0:NMEM], qx[:, 2 * h + i, qi * P:(qi + 1) * P], kx[:, 2 * h + i, :],
                               start=i == 0, stop=i == 1)
            mm.then_inc(att_s, 1)
        scores(0)
        for n in range(16):
            h, qi = n // 4, n % 4
            if n < 15:
                scores(n + 1)
            pe.wait_ge(att_p, FOX_STEPS + n + 1)
            if n >= 1:
                pe.wait_ge(att_tc, FOX_STEPS + n)
            else:
                pe.wait_ge(xn_scaled, 2 * KD)
            for kb in range(2):
                mm = pe.transpose(bank[6][:, kb * P:(kb + 1) * P], xprob[:, n % 2, kb * P:(kb + 1) * P], ident[:])
            mm.then_inc(att_t, 1)
            if qi == 3:
                pe.wait_ge(att_tc, FOX_STEPS + n + 1)
                for i in range(2):
                    m = 2 * h + i
                    if m >= 2:
                        pe.wait_ge(xo_lo_ready, m - 1)
                    for kb in range(2):
                        mm = pe.matmul(bank[(7, 3)[i]][:], vx[:, kb, m * P:(m + 1) * P], xprobT[:, h % 2, kb, :],
                                       start=kb == 0, stop=kb == 1)
                    mm.then_inc(att_o, 1)
        pe_project(pe, O, o_hi, o_lo, (xo_lo_ready, 0))

    def dve_cross(dve):
        Q = layers["xq"]

        def q_tiles(b):
            for mm in range(4):
                dve.wait_ge(unit_used, b * 4 + (Q.base + mm + 1))
                dve.tensor_tensor(tile(qx, b * 4 + mm), bank[mm][:], rstd[:], ALU.mult).then_inc(taken, 1)
        each_body(dve, Q.bodies, q_tiles)
        dve_head_rstd(dve, "q")

        def row_max(n):
            dve.wait_ge(att_s, FOX_STEPS + n + 1)
            dve_chain(dve, dve.reduce_max(xa_m[:, n:n + 1], bank[4 + n % 2][:, 0:NMEM], AX.X, negate=True))
            dve.tensor_scalar(xa_m[:, n:n + 1], xa_m[:, n:n + 1], 1.0 / 16, None, ALU.mult).then_inc(att_nmax, 1)
        row_max(0)
        for n in range(16):
            h, qi = n // 4, n % 4
            if n < 15:
                row_max(n + 1)
            dve.wait_ge(att_exp, FOX_STEPS + n + 1)
            dve_chain(dve, dve.reciprocal(xa_l[:, n:n + 1], xa_l[:, n:n + 1]))
            dve.tensor_scalar(xprob[:, n % 2, :], xprob[:, n % 2, :], xa_l[:, n:n + 1], None, ALU.mult).then_inc(att_p, 1)
            if qi == 3:
                for i in range(2):
                    m = 2 * h + i
                    dve.wait_ge(xo_hi_ready, m + 1)
                    dve.tensor_tensor(o_lo[:, m, :], bank[(7, 3)[i]][:], f32(o_hi[:, m, :]), ALU.subtract).then_inc(xo_lo_ready, 1)

    def act_cross(act):
        Q = layers["xq"]
        act_bodies(act, Q)
        act_head_squares(act, "q")

        def exps(n):
            act.wait_ge(att_nmax, FOX_STEPS + n + 1)
            if n >= 2:
                act.wait_ge(att_t, FOX_STEPS + n - 1)
            act.activation(xprob[:, n % 2, :], bank[4 + n % 2][:, 0:NMEM], ACT.Exp, bias=xa_m[:, n:n + 1],
                           scale=1.0 / 16, accum_out=xa_l[:, n:n + 1]).then_inc(att_exp, 1)
        exps(0)
        for n in range(16):
            h, qi = n // 4, n % 4
            if n < 15:
                exps(n + 1)
            act.wait_ge(att_t, FOX_STEPS + n + 1)
            if h >= 2:
                act.wait_ge(att_o, FOX_STEPS + 2 * (h - 1))
            act.activation(xprobT[:, h % 2, :, qi * P:(qi + 1) * P], bank[6][:, 0:2 * P].rearrange("p (k t) -> p k t", t=P),
                           ACT.Copy).then_inc(att_tc, 1)
            if qi == 3:
                for i in range(2):
                    m = 2 * h + i
                    act.wait_ge(att_o, FOX_STEPS + m + 1)
                    act.activation(o_hi[:, m, :], bank[(7, 3)[i]][:], ACT.Copy).then_inc(xo_hi_ready, 1)


    HEADS = 4
    LEVELS = [64, 32, 16, 8, 4, 2, 1]
    STEPS = len(LEVELS) + 2
    KD_STEP, QE_STEP = len(LEVELS), len(LEVELS) + 1
    hsc, kdT = sq[:, 0, :], sq[:, 1, :]

    def chunks(ap):
        return ap.rearrange("p (n t) -> p n t", t=P)

    def hg_q(h):
        return hq[:, h, :]

    def hg_b(h):
        return hq[:, 4 + h, :]

    def hg_g(h):
        return hq[:, 8 + h, :]

    def act_hg_setup(act):
        act.dma_start(levels_f[:], io["c_levels"]).then_inc(levels_in, 16)
        act.wait_ge(taken, layers["hg_qfg"].rbase + 12)
        for h in range(HEADS):
            act.activation(hk[:, h, :], hg_b(h), ACT.Sigmoid, scale=-1.0).then_inc(hg_key, 1)
        for i in (0, 1, 2, 3, 8, 9, 10, 11):
            act.activation(hq[:, i, :], hq[:, i, :], ACT.Silu).then_inc(hg_silu, 1)
        for h in range(HEADS):
            l = he[:, h % 2, :]
            if h >= 2:
                act.wait_ge(hg_cum, 4 * (h - 1))
            act_chain(act, act.activation(l, hg_b(h), ACT.Abs))
            act_chain(act, act.activation(l, l, ACT.Exp, scale=-1.0))
            act.activation(l, l, ACT.Ln, bias=1.0).then_inc(hg_ln, 1)
        act.wait_ge(levels_in, 16)
        act.activation(hm[:].rearrange("p l t -> p (l t)"), levels_f[:], ACT.Copy).then_inc(levels_ready, 1)

    def dve_hg_setup(dve):
        dve.memset(hsc, 0.0).then_inc(hg_zero, 1)
        for h in range(HEADS):
            l = he[:, h % 2, :]
            dve.wait_ge(hg_ln, h + 1)
            dve_chain(dve, dve.scalar_tensor_tensor(l, hg_b(h), 0.0, l, ALU.min, ALU.subtract))
            for n in range(4):
                c = slice(n * P, (n + 1) * P)
                dve.tensor_tensor_scan(hg_b(h)[:, c], ones[:], l[:, c], 0.0, ALU.mult, ALU.add).then_inc(hg_cum, 1)
        dve.wait_ge(hg_cum, 4 * HEADS)
        dve.wait_ge(levels_ready, 1)

    def halves(ap, w):
        v = ap.rearrange("p (k two w) -> p k two w", two=2, w=w)
        return v[:, :, 0, :], v[:, :, 1, :]

    def wait_step_used(eng, j):
        h, l = j // STEPS, j % STEPS
        if l < KD_STEP:
            eng.wait_ge(hg_score, (len(LEVELS) + 1) * h + l + 1)
        else:
            eng.wait_ge(hg_kt if l == KD_STEP else hg_o, h + 1)

    def dve_hg_difference(dve, h, l):
        j = STEPS * h + l
        e, b = he[:, j % 2, :], hg_b(h)
        if j >= 2:
            wait_step_used(dve, j - 2)
        elif h == 0:
            dve.wait_ge(hg_cum, 4 * HEADS)
        if l < KD_STEP:
            w = LEVELS[l]
            b0, b1 = halves(b, w)
            e0, e1 = halves(e, w)
            ref = b0[:, :, w - 1:w].to_broadcast([P, T // (2 * w), w])
            dve.tensor_tensor(e0, ref, b0, ALU.subtract).then_inc(hg_diff, 1)
            dve.tensor_tensor(e1, b1, ref, ALU.subtract).then_inc(hg_diff, 1)
        elif l == KD_STEP:
            last = chunks(b)[:, :, P - 1:P].to_broadcast([P, 4, P])
            dve.tensor_tensor(chunks(e), last, chunks(b), ALU.subtract).then_inc(hg_diff, 1)

    def diff_count(h, l):
        per = 2 * len(LEVELS) + 1
        return per * h + min(2 * (l + 1), per)

    def act_hg_exp(act, h, l):
        j = STEPS * h + l
        e = he[:, j % 2, :]
        if l == QE_STEP:
            wait_step_used(act, j - 2)
            act.activation(e, hg_b(h), ACT.Exp).then_inc(hg_exp, 1)
            if h:
                act.wait_ge(hg_state, 3 * h)
            act.activation(hdec[:], chunks(hg_b(h))[:, :, P - 1], ACT.Exp).then_inc(hg_dec, 1)
            return
        act.wait_ge(hg_diff, diff_count(h, l))
        act.activation(e, e, ACT.Exp).then_inc(hg_exp, 1)

    def dve_hg_factor(dve, h, l):
        j = STEPS * h + l
        e, k, q = he[:, j % 2, :], hk[:, h, :], hg_q(h)
        dve.wait_ge(hg_exp, j + 1)
        if h == 0 and l == 0:
            dve.wait_ge(hg_key, HEADS)
            dve.wait_ge(hg_silu, 8)
        if l < KD_STEP:
            w = LEVELS[l]
            (e0, e1), k0, q1 = halves(e, w), halves(k, w)[0], halves(q, w)[1]
            dve.tensor_tensor(e0, e0, k0, ALU.mult).then_inc(hg_fac, 1)
            dve.tensor_tensor(e1, e1, q1, ALU.mult).then_inc(hg_fac, 1)
        elif l == KD_STEP:
            dve.tensor_tensor(e, e, k, ALU.mult).then_inc(hg_fac, 1)
        else:
            dve.tensor_tensor(e, e, q, ALU.mult).then_inc(hg_fac, 1)

    def fac_count(h, l):
        n = len(LEVELS)
        return (2 * n + 2) * h + (2 * (l + 1) if l < n else 2 * n + l - n + 1)

    def pe_hg_scores(pe, h, l):
        n = len(LEVELS) + 1
        s = n * h + l
        if s >= 2:
            pe.wait_ge(hg_sel, s - 1)
        if l < len(LEVELS):
            pe.wait_ge(hg_fac, fac_count(h, l))
            a = b = he[:, (STEPS * h + l) % 2, :]
        else:
            a, b = hk[:, h, :], hg_q(h)
        for c in range(4):
            cs = slice(c * P, (c + 1) * P)
            mm = pe.matmul(bank[6 + s % 2][:, cs], a[:, cs], b[:, cs], start=True, stop=True)
        mm.then_inc(hg_score, 1)

    def dve_hg_select(dve, h, l):
        s = (len(LEVELS) + 1) * h + l
        if s == 0:
            dve.wait_ge(levels_ready, 1)
            dve.wait_ge(hg_zero, 1)
        if h and l == 0:
            dve.wait_ge(hg_o, h)
        dve.wait_ge(hg_score, s + 1)
        if s:
            dve.wait_ge(hg_sel, s)
        dve.copy_predicated(chunks(hsc), hm[:, l, :].unsqueeze(1).to_broadcast([P, 4, P]),
                            chunks(bank[6 + s % 2][:])).then_inc(hg_sel, 1)

    def pe_hg_keys(pe, h):
        pe.wait_ge(hg_fac, fac_count(h, KD_STEP))
        if h:
            pe.wait_ge(hg_y, h)
        e = he[:, (STEPS * h + KD_STEP) % 2, :]
        for c in range(4):
            cs = slice(c * P, (c + 1) * P)
            mm = pe.transpose(bank[4][:, cs], e[:, cs], ident[:])
        mm.then_inc(hg_kt, 1)

    def act_hg_keys(act, h):
        act.wait_ge(hg_kt, h + 1)
        if h:
            act.wait_ge(hg_update, h)
        act.activation(kdT, bank[4][:], ACT.Copy).then_inc(hg_ktc, 1)

    def pe_hg_update(pe, h):
        pe.wait_ge(hg_ktc, h + 1)
        if h:
            pe.wait_ge(hg_std, h)
        if h == 0:
            pe.wait_ge(taken, layers["hg_v"].rbase + 4)
        for n in range(3):
            mm = pe.matmul(bank[5][:, n * P:(n + 1) * P], kdT[:, n * P:(n + 1) * P], hv[:, n, h * P:(h + 1) * P],
                           start=True, stop=True)
        mm.then_inc(hg_update, 1)

    def dve_hg_state(dve, h):
        dve.wait_ge(hg_update, h + 1)
        if h:
            dve.wait_ge(hg_o, h)
        dve.wait_ge(hg_dec, h + 1)
        for n in range(3):
            u = bank[5][:, n * P:(n + 1) * P]
            if n == 0:
                dve.tensor_copy(hS[:, 0, :], u).then_inc(hg_state, 1)
            else:
                dve.wait_ge(hg_state, 3 * h + n)
                dve.scalar_tensor_tensor(hS[:, n, :], hS[:, n - 1, :], hdec[:, n:n + 1], u, ALU.mult, ALU.add).then_inc(hg_state, 1)

    def pe_hg_out(pe, h):
        pe.wait_ge(hg_sel, (len(LEVELS) + 1) * (h + 1))
        pe.wait_ge(hg_fac, fac_count(h, QE_STEP))
        pe.wait_ge(hg_state, 3 * h + 3)
        qe = he[:, (STEPS * h + QE_STEP) % 2, :]
        for n in range(4):
            cs = slice(n * P, (n + 1) * P)
            mm = pe.matmul(bank[4][:, cs], hv[:, n, h * P:(h + 1) * P], hsc[:, cs], start=True, stop=n == 0)
            if n:
                mm = pe.matmul(bank[4][:, cs], hS[:, n - 1, :], qe[:, cs], start=False, stop=True)
        mm.then_inc(hg_o, 1)

    def act_hg_square(act, h):
        act.wait_ge(hg_o, h + 1)
        if h:
            act.wait_ge(hg_y, h)
        act.activation(ss[:], bank[4][:], ACT.Square).then_inc(hg_osq, 1)

    def pe_hg_sum(pe, h):
        pe.wait_ge(hg_osq, h + 1)
        pe.matmul(bank[5][:], ones[:], ss[:], start=True, stop=True).then_inc(hg_oss, 1)

    def act_hg_std(act, h):
        act.wait_ge(hg_oss, h + 1)
        act.activation(ss[:], bank[5][:], ACT.Sqrt, bias=eps[:], scale=1.0 / P).then_inc(hg_std, 1)

    def dve_hg_y(dve, h):
        dve.wait_ge(hg_std, h + 1)
        dve_chain(dve, dve.reciprocal(ss[:], ss[:]))
        dve_chain(dve, dve.scalar_tensor_tensor(ss[:], bank[4][:], col("hg_onorm_2"), ss[:], ALU.mult, ALU.mult))
        dve.tensor_tensor(hg_g(h), hg_g(h), ss[:], ALU.mult).then_inc(hg_y, 1)

    def act_hg_split(act, h):
        act.wait_ge(hg_y, h + 1)
        if h == 0:
            act.wait_ge(unit_used, layers["merge0"].base + 12)
        act.activation(y0_hi[:, h, :], hg_g(h), ACT.Copy).then_inc(hg_hi, 1)

    def dve_hg_split(dve, h):
        dve.wait_ge(hg_hi, h + 1)
        dve.tensor_tensor(y0_lo[:, h, :], hg_g(h), f32(y0_hi[:, h, :]), ALU.subtract).then_inc(hg_lo, 1)

    def merge_y(b):
        return ((y0_hi, y0_lo, fox_lo), (y1_hi, y1_lo, s5_lo), (y0_hi, y0_lo, hg_lo))[b]

    def pe_hg(pe):
        for h in range(HEADS):
            b, p = h // 2, 2 * (h % 2)
            y = merge_y(b)
            pe_merge_gate(pe, b, p, 0)
            if h:
                pe_hg_sum(pe, h - 1)
            pe_hg_scores(pe, h, 0)
            pe_merge_gate(pe, b, p, 1)
            pe_hg_scores(pe, h, 1)
            pe_hg_scores(pe, h, 2)
            pe_merge_branch(pe, b, p, *y)
            pe_hg_scores(pe, h, 3)
            pe_hg_scores(pe, h, 4)
            pe_merge_gate(pe, b, p + 1, 0)
            pe_hg_scores(pe, h, 5)
            pe_hg_scores(pe, h, 6)
            pe_hg_scores(pe, h, KD_STEP)
            pe_hg_keys(pe, h)
            pe_merge_gate(pe, b, p + 1, 1)
            pe_hg_update(pe, h)
            pe_merge_branch(pe, b, p + 1, *y)
            pe_hg_out(pe, h)
        pe_merge_gate(pe, 2, 0, 0)
        pe_merge_gate(pe, 2, 0, 1)
        pe_hg_sum(pe, HEADS - 1)

    def dve_hg(dve):
        for h in range(HEADS):
            b, p = h // 2, 2 * (h % 2)
            dve_hg_difference(dve, h, 0)
            dve_hg_difference(dve, h, 1)
            dve_hg_factor(dve, h, 0)
            dve_merge_gate(dve, b, p, 0)
            if h:
                dve_hg_y(dve, h - 1)
            dve_hg_difference(dve, h, 2)
            dve_hg_factor(dve, h, 1)
            dve_hg_select(dve, h, 0)
            dve_hg_difference(dve, h, 3)
            dve_hg_factor(dve, h, 2)
            dve_merge_gate(dve, b, p, 1)
            dve_hg_select(dve, h, 1)
            dve_hg_select(dve, h, 2)
            dve_hg_difference(dve, h, 4)
            dve_hg_factor(dve, h, 3)
            dve_merge_branch(dve, b, p)
            dve_hg_difference(dve, h, 5)
            dve_hg_factor(dve, h, 4)
            dve_hg_select(dve, h, 3)
            dve_hg_difference(dve, h, 6)
            dve_hg_factor(dve, h, 5)
            dve_merge_gate(dve, b, p + 1, 0)
            dve_hg_select(dve, h, 4)
            dve_hg_difference(dve, h, KD_STEP)
            dve_hg_factor(dve, h, 6)
            dve_hg_factor(dve, h, KD_STEP)
            dve_hg_select(dve, h, 5)
            dve_hg_select(dve, h, 6)
            dve_hg_select(dve, h, KD_STEP)
            dve_hg_factor(dve, h, QE_STEP)
            dve_merge_gate(dve, b, p + 1, 1)
            dve_hg_state(dve, h)
            dve_merge_branch(dve, b, p + 1)
            if h == HEADS - 1:
                for i in range(HEADS - 1):
                    dve_hg_split(dve, i)
        dve_hg_y(dve, HEADS - 1)
        dve_hg_split(dve, HEADS - 1)

    def act_hg(act):
        act.preload_act_table(ACT.Exp)
        for h in range(HEADS):
            b, p = h // 2, 2 * (h % 2)
            act_hg_exp(act, h, 0)
            act_merge_split(act, b, p, 0)
            if h:
                act_hg_square(act, h - 1)
            act_hg_exp(act, h, 1)
            act_merge_gate(act, b, p, 0)
            if h:
                act_hg_std(act, h - 1)
            act_hg_exp(act, h, 2)
            act_merge_split(act, b, p, 1)
            act_hg_exp(act, h, 3)
            act_merge_gate(act, b, p, 1)
            act_merge_split(act, b, p, 2)
            act_hg_exp(act, h, 4)
            act_merge_split(act, b, p + 1, 0)
            act_hg_exp(act, h, 5)
            act_hg_exp(act, h, 6)
            act_merge_gate(act, b, p + 1, 0)
            act_hg_exp(act, h, KD_STEP)
            act_merge_split(act, b, p + 1, 1)
            act_hg_exp(act, h, QE_STEP)
            act_hg_keys(act, h)
            act_merge_gate(act, b, p + 1, 1)
            act_merge_split(act, b, p + 1, 2)
            if h == HEADS - 1:
                for i in range(HEADS - 1):
                    act_hg_split(act, i)
        act_hg_square(act, HEADS - 1)
        act_hg_std(act, HEADS - 1)
        act_hg_split(act, HEADS - 1)

    def has(name):
        return name in [L.name for L in order]

    @block.sync
    def _(sp):
        sp.dma_start(par[:], io["params"]).then_inc(par_in, 16)
        for k in range(KD):
            sp.dma_start(x[:, k, :], io["xT"][k * P:(k + 1) * P, :]).then_inc(x_in, 16)
        sp.dma_start(ident[:], io["c_ident"]).then_inc(ident_in, 16)
        sp_rec(sp)
        for L in order:
            load_layer(sp, L)
        if stop == "first":
            sp.wait_ge(final_step, KD)
        dbg = {"yfox": (fox_lo, y0_hi, y0_lo), "ys5": (s5_lo, y1_hi, y1_lo), "yhg": (hg_lo, y0_hi, y0_lo)}.get(stop)
        if dbg:
            sp.wait_ge(dbg[0], 4)
            for j in range(8):
                sp.dma_start(io["outT"][j * P:(j + 1) * P, :], f32(dbg[1 + j // 4][:, j % 4, :])).then_inc(out_stored, 16)
            sp.wait_ge(out_stored, 16 * KD)
            return
        L = order[-1]
        sp.wait_ge(taken, L.rbase + L.results)
        for k in range(KD):
            sp.dma_start(io["outT"][k * P:(k + 1) * P, :], x[:, k, :]).then_inc(out_stored, 16)
        sp.wait_ge(out_stored, 16 * KD)

    @block.gpsimd
    def _(pool):
        pool.memset(ones[:], 1.0).then_inc(ones_set, 1)
        pool.memset(eps[:], EPS).then_inc(ones_set, 1)
        pool.memset(gate_w[:], 0.0).then_inc(gate_w_zero, 1)
        for L in order:
            split_lo(pool, L)

    @block.scalar
    def _(act):
        act.wait_ge(par_in, 16)
        act_softplus(act)
        act.wait_ge(x_in, 16 * KD)
        act.wait_ge(ones_set, 2)
        for i in range(AHEAD):
            split_hi(act, order[0], 0, i)
        for m in range(KD):
            act_norm_tile(act, 0, gain_of("ffn1_norm", 0), m, m % 2)
        act_norm_std(act, 0)
        act_ffn(act, 0)
        act_residual(act, layers["down0"], 1, gain_of("mix_norm", 0))
        if not has("rec_r"): return
        act_rec(act)
        act_residual(act, layers["rec_out"], 2, gain_of("ffn2_norm", 0))
        if not has("up1"): return
        act_ffn(act, 1)
        act_residual(act, layers["down1"], 3, gain_of("ffn1_norm", 1))
        if not has("up2"): return
        act_ffn(act, 2)
        act_residual(act, layers["down2"], 4, gain_of("mix_norm", 1))
        if not has("sg_v"): return
        act_norm_columns(act, 1)
        act_load_sgu(act)
        act_sgu(act)
        act_residual(act, layers["sg_out"], 5, gain_of("ffn2_norm", 1))
        if not has("up3"): return
        act_ffn(act, 3)
        act_residual(act, layers["down3"], 6, None)
        if stop == "ffn3": return
        act_final(act, gain_of("norm_mix_2"))
        if stop == "first": return
        act_norm_columns(act, 2)
        act_load_mix(act)
        act_mix_a(act)
        act_fox(act)
        if stop == "yfox": return
        act_s5(act)
        act_glu(act)
        if stop == "ys5": return
        act_hg_setup(act)
        act_hg(act)
        if stop == "yhg": return
        act_e(act)
        act_residual(act, layers["w_out"], 8, gain_of("norm_x_2"))
        if stop == "mix": return
        act_cross(act)
        act_residual(act, layers["xo"], 9, gain_of("norm_ffn_2"))
        if stop == "xattn": return
        act_ffn(act, 4)
        act_residual(act, layers["down4"], None, None)

    @block.vector
    def _(dve):
        dve.wait_ge(par_in, 16)
        dve_softplus(dve)
        dve.wait_ge(x_in, 16 * KD)
        dve.memset(ss[:], 0.0).then_inc(ss_added, 1)
        for m in range(KD):
            dve_norm_tile(dve, 0, gain_of("ffn1_norm", 0), m, m % 2)
        dve_norm_rstd(dve, 0)
        dve_ffn(dve, 0)
        dve_residual(dve, layers["down0"], 0.5, 1, gain_of("mix_norm", 0))
        if not has("rec_r"): return
        dve_rec(dve)
        dve_residual(dve, layers["rec_out"], 1.0, 2, gain_of("ffn2_norm", 0))
        if not has("up1"): return
        dve_ffn(dve, 1)
        dve_residual(dve, layers["down1"], 0.5, 3, gain_of("ffn1_norm", 1))
        if not has("up2"): return
        dve_ffn(dve, 2)
        dve_residual(dve, layers["down2"], 0.5, 4, gain_of("mix_norm", 1))
        if not has("sg_v"): return
        dve_norm_columns(dve, 1)
        dve_sgu(dve)
        dve_residual(dve, layers["sg_out"], 1.0, 5, gain_of("ffn2_norm", 1))
        if not has("up3"): return
        dve_ffn(dve, 3)
        dve_residual(dve, layers["down3"], 0.5, 6, None)
        if stop == "ffn3": return
        dve_final(dve, gain_of("norm_mix_2"))
        if stop == "first": return
        dve_norm_columns(dve, 2)
        dve_mix_a(dve)
        dve_fox(dve)
        if stop == "yfox": return
        dve_s5(dve)
        dve_z(dve)
        dve_glu(dve)
        if stop == "ys5": return
        dve_hg_setup(dve)
        dve_hg(dve)
        if stop == "yhg": return
        dve_e(dve)
        dve_residual(dve, layers["w_out"], 1.0, 8, gain_of("norm_x_2"))
        if stop == "mix": return
        dve_cross(dve)
        dve_residual(dve, layers["xo"], 1.0, 9, gain_of("norm_ffn_2"))
        if stop == "xattn": return
        dve_ffn(dve, 4)
        dve_residual(dve, layers["down4"], 1.0, None, None)

    @block.tensor
    def _(pe):
        pe.wait_ge(ones_set, 1)
        pe_norm_sum(pe, 0)
        pe_ffn(pe, 0, 0)
        pe_norm_sum(pe, 1)
        if not has("rec_r"): return
        pe_rec(pe, 1)
        pe_norm_sum(pe, 2)
        if not has("up1"): return
        pe_ffn(pe, 1, 2)
        pe_norm_sum(pe, 3)
        if not has("up2"): return
        pe_ffn(pe, 2, 3)
        pe_norm_sum(pe, 4)
        if not has("sg_v"): return
        pe_norm_columns(pe)
        pe_sgu(pe, 4)
        pe_norm_sum(pe, 5)
        if not has("up3"): return
        pe_ffn(pe, 3, 5)
        pe_norm_sum(pe, 6)
        if stop == "ffn3": return
        pe_norm_sum(pe, 7)
        if stop == "first": return
        pe_norm_columns(pe)
        pe_mix_a(pe)
        pe_fox(pe)
        if stop == "yfox": return
        pe_s5(pe)
        pe_glu(pe)
        if stop == "ys5": return
        pe_hg(pe)
        if stop == "yhg": return
        pe_e(pe)
        pe_norm_sum(pe, 8)
        if stop == "mix": return
        pe_cross(pe)
        pe_norm_sum(pe, 9)
        if stop == "xattn": return
        pe_ffn(pe, 4, 9)

    ctx.close()


def columns(w, order=None):
    k, m = w.shape
    u = w.reshape(k // P, P, m // P, P).transpose(2, 1, 0, 3)
    if order is not None:
        u = u[order]
    return np.ascontiguousarray(u).reshape(m, k)


def token_blocks(w):
    k, m = w.shape
    u = w.reshape(k // P // 2, 2, P, m // T, T).transpose(3, 0, 2, 1, 4)
    return np.ascontiguousarray(u).reshape(-1, UNIT)


def features(v):
    return np.asarray(v).reshape(-1, P).T


def layout(a):
    a = {k: np.asarray(v) for k, v in a.items()}
    out = {"xT": np.ascontiguousarray(a["x"][0].T)}
    cols = []
    for name in PARAMS:
        v = a[name]
        if name in ("fox_qnorm_2", "fox_knorm_2"):
            v = np.tile(v.reshape(-1), 2)
        if name == "s5_log_dt_2":
            v = np.repeat(v.reshape(-1), 64)
        cols.append(features(v))
    out["params"] = np.ascontiguousarray(np.concatenate(cols, axis=1))
    ug = [h * KF + j for j in range(KF) for h in (1, 0)]
    ffn = [(a["ffn1_w_in"][0], a["ffn1_w_out"][0]), (a["ffn2_w_in"][0], a["ffn2_w_out"][0]),
           (a["ffn1_w_in"][1], a["ffn1_w_out"][1]), (a["ffn2_w_in"][1], a["ffn2_w_out"][1]),
           (a["w_gate_up_2"][0], a["w_down_2"][0])]
    for i, (up, down) in enumerate(ffn):
        out[f"w_up{i}"] = columns(up, ug)
        out[f"w_down{i}"] = columns(down)
    a_w = {"gate_a_w": a["rec_gate_a_w"][0], "gate_x_w": a["rec_gate_x_w"][0]}
    for name, w in a_w.items():
        out[name] = np.concatenate([w[s::2].transpose(1, 0, 2).reshape(64, 8 * 64) for s in range(2)])
    w = a["rec_w_in"][0]
    out["rec_r"], out["rec_y"] = columns(w[:, D:]), columns(w[:, :D])
    out["rec_out"] = columns(a["rec_w_out"][0])
    w = a["sg_w_in"][0]
    out["sg_v"], out["sg_u"] = token_blocks(w[:, D:]), columns(w[:, :D])
    out["sg_out"] = columns(a["sg_w_out"][0])
    out["sg_wsT"] = np.ascontiguousarray(a["sg_w_s"][0].transpose(2, 0, 1)).reshape(P, D)
    out["sg_bs"] = np.ascontiguousarray(a["sg_b_s"][0].reshape(1, D))
    w = a["w_in_2"][0]
    part = {}
    at = 0
    for name, n in (("fq", 512), ("fk", 512), ("fv", 512), ("ff", 8), ("su", 512), ("hq", 512), ("hf", 512), ("hi", 512),
                    ("hg", 512), ("gl", 3 * D)):
        part[name] = w[:, at:at + n]
        at += n
    out["fox_qk"] = columns(np.concatenate([part["fq"], part["fk"]], axis=1))
    out["fox_v"], out["hg_v"] = token_blocks(part["fv"]), token_blocks(part["hi"])
    out["ff_w"] = np.ascontiguousarray(part["ff"].reshape(KD, P, 8).transpose(1, 0, 2)).reshape(P, KD * 8)
    out["ff_b"] = a["fox_fbias_2"].reshape(8, 1)
    out["s5_in"] = columns(part["su"])
    out["hg_qfg"] = columns(np.concatenate([part["hq"], part["hf"], part["hg"]], axis=1))
    wb = a["w_branch_2"][0]
    for b in range(3):
        gate = columns(part["gl"][:, b * D:(b + 1) * D]).reshape(4, 2, P, UNIT)
        branch = columns(wb[b * 512:(b + 1) * 512]).reshape(4, 2, P, 512).transpose(0, 2, 1, 3).reshape(4, 1, P, UNIT)
        out[f"merge{b}"] = np.concatenate([gate, branch], axis=1).reshape(12 * P, UNIT)
    for c in ("re", "im"):
        out[f"s5_b_{c}"] = np.ascontiguousarray(a[f"s5_b_{c}_2"][0].reshape(16, 2, 64, 16).transpose(1, 2, 0, 3)).reshape(P, 256)
        out[f"s5_c_{c}"] = np.ascontiguousarray(a[f"s5_c_{c}_2"][0].reshape(16, 2, 16, 64).transpose(1, 3, 0, 2)).reshape(P, 256)
    out["s5_glu"] = columns(a["s5_w_glu_2"][0])
    for name in ("xk", "xq", "xo", "w_out"):
        out[name] = columns(a[name + "_2"][0])
    out["xv"] = token_blocks(a["xv_2"][0])
    out["memT"] = np.ascontiguousarray(a["mem_2"][0].T)
    def rows(n, width, value):
        return np.repeat(np.eye(n, dtype=np.float32) * np.float32(value), width, axis=1)
    out["c_sel8"], out["c_selx"] = rows(8, P, 8.0), rows(4, P, 1.0)
    out["c_spread"] = rows(16, 64, 1.0)
    out["c_pack"] = np.zeros((P, 32), np.float32)
    out["c_pack"][np.arange(P), 16 + np.arange(P) // 64] = 1.0
    out["c_pick"] = np.zeros((P, 8), np.float32)
    out["c_pick"][:, 4] = 1.0
    out["c_iota"] = np.tile(np.arange(T, dtype=np.float32), (P, 1))
    i = np.arange(P)
    out["c_ident"] = np.eye(P, dtype=np.float32)
    out["c_tri"] = (i[:, None] <= i[None, :]).astype(np.float32)
    out["c_causal"] = np.where(i[None, :] <= i[:, None], 0.0, -1e30).astype(np.float32)
    levels = [(i[:, None] // (2 * w) == i[None, :] // (2 * w)) & (i[:, None] % (2 * w) < w) & (i[None, :] % (2 * w) >= w)
              for w in (64, 32, 16, 8, 4, 2, 1)]
    out["c_levels"] = np.stack(levels + [i[:, None] == i[None, :]], axis=1).astype(np.float32).reshape(P, 8 * P)
    return out


def kernel(**inputs):
    import concourse.bacc as bacc
    from concourse.bass_utils import run_bass_kernel_spmd

    nc = bacc.Bacc("TRN2", target_bir_lowering=False, num_devices=1)
    arrays = layout(inputs)
    io = {k: nc.dram_tensor(k, list(v.shape), mybir.dt.from_np(v.dtype), kind="ExternalInput").ap()
          for k, v in arrays.items()}
    io["outT"] = nc.dram_tensor("outT", [D, T], F32, kind="ExternalOutput").ap()
    build(nc, io)
    r = run_bass_kernel_spmd(nc, [arrays], core_ids=[0])
    return np.ascontiguousarray(r.results[0]["outT"].T)[None]
```

```python
from contextlib import ExitStack

import numpy as np

import concourse.bass as bass
from concourse import mybir

P = 128
T = 512
D = 1024
KD = D // P
FF = 2816
KF = FF // P
NMEM = 256
EPS = 1e-6
RING = 4
UNIT = 8 * P
AHEAD = 3
ROUND = 12582912.0
TWO_PI = (6.28125, 0.0019350051879882812, 3.0199159819e-07)
PI_BELOW = 3.1415925
TURN = 6.283185
FINAL = 6
F32 = mybir.dt.float32
F32R = mybir.dt.float32r
U8 = mybir.dt.uint8
ACT = mybir.ActivationFunctionType
ALU = mybir.AluOpType
AX = mybir.AxisListType

PARAMS = {}
_at = 0
for _name, _n in (("ffn1_norm", 2 * KD), ("ffn2_norm", 2 * KD), ("mix_norm", 2 * KD), ("final_norm", KD),
                  ("norm_mix_2", KD), ("norm_x_2", KD), ("norm_mem_2", KD), ("norm_ffn_2", KD),
                  ("rec_conv_w", 4 * KD), ("rec_conv_b", KD), ("rec_gate_a_b", KD), ("rec_gate_x_b", KD),
                  ("rec_lambda", KD), ("sg_v_norm", KD), ("s5_d_2", 4), ("s5_b_glu_2", 4), ("hg_onorm_2", 1),
                  ("x_qnorm_2", 2), ("x_knorm_2", 2), ("fox_qnorm_2", 1), ("fox_knorm_2", 1),
                  ("s5_a_re_2", 16), ("s5_a_im_2", 16), ("s5_log_dt_2", 16)):
    PARAMS[_name] = _at
    _at += _n
NPAR = _at


class Layer:

    def __init__(self, name, src, widths, bodies, results, base, rbase):
        self.name, self.src, self.widths, self.bodies = name, src, widths, bodies
        self.per = len(widths)
        self.n = self.per * bodies
        self.results, self.base, self.rbase = results, base, rbase
        assert self.per % RING == 0 and self.base % RING == 0 and self.rbase % RING == 0


class Chain:

    def __init__(self, sem):
        self.sem, self.n = sem, 0

    def __call__(self, eng, ins):
        self.n += 1
        ins.then_inc(self.sem, 1)
        eng.wait_ge(self.sem, self.n)


def each_body(eng, n, body):
    if n == 1:
        body(0)
    else:
        with eng.Fori(0, n) as b:
            body(b)


def build(nc, io):
    ctx = ExitStack()
    layers = {}
    order = []

    def layer(name, dram, widths, bodies, results, cols=None):
        base = order[-1].base + order[-1].n if order else 0
        rbase = order[-1].rbase + order[-1].results if order else 0

        def src(b, i):
            if cols is None:
                return io[dram][bass.ds((b * len(widths) + i) * P, P), 0:widths[i]]
            row, c0, c1 = cols(i)
            rows = len(widths) // (KF * P // UNIT + 1)
            return io[dram][bass.ds((b * rows + row) * P, P), c0:c1]
        order.append(Layer(name, src, widths, bodies, results, base, rbase))
        layers[name] = order[-1]

    DOWN_W = [UNIT, UNIT, KF * P - 2 * UNIT]

    def ffn_layers(i):
        layer(f"up{i}", f"w_up{i}", [UNIT] * 4, 11, 44)
        layer(f"down{i}", f"w_down{i}", DOWN_W * 4, 2, 8,
              cols=lambda j: (j // 3, (j % 3) * UNIT, min((j % 3 + 1) * UNIT, KF * P)))

    def column_layer(name, n, widths=(UNIT,) * 4, results=None):
        layer(name, name, list(widths), n // len(widths), n if results is None else results)

    ffn_layers(0)
    column_layer("rec_r", 8)
    column_layer("rec_y", 8)
    column_layer("rec_out", 8)
    ffn_layers(1)
    ffn_layers(2)
    column_layer("sg_v", 8)
    column_layer("sg_u", 8)
    column_layer("sg_out", 8)
    ffn_layers(3)
    column_layer("fox_qk", 8)
    column_layer("fox_v", 4)
    column_layer("s5_in", 4)
    column_layer("hg_qfg", 12)
    column_layer("hg_v", 4)
    column_layer("merge01", 28, (UNIT,) * 6 + (UNIT // 2,) * 4 + (UNIT,) * 18, 36)
    column_layer("merge2", 12, (UNIT,) * 12, 16)
    column_layer("xk", 8)
    column_layer("xv", 8, results=4)
    column_layer("w_out", 8)
    column_layer("xq", 8)
    column_layer("xo", 8)
    ffn_layers(4)

    base = -(-nc.sbuf_base // 64) * 64
    cursor = [base]

    def place(name, shape, dt=F32, at=None):
        size = int(np.prod(shape[1:])) * mybir.dt.size(dt)
        off = cursor[0] if at is None else at
        t = nc.alloc_sbuf_tensor_at(name, list(shape), dt, offset=off)
        if at is None:
            cursor[0] += -(-size // 32) * 32
        return t

    x = place("x_res", [P, KD, T])
    xg_hi = place("xg_hi", [P, KD, T], F32R)
    xg_lo = place("xg_lo", [P, KD, T], F32R)
    w_stage = place("w_stage", [P, RING, UNIT])
    w_hi = place("w_hi", [P, RING, UNIT], F32R)
    w_lo = place("w_lo", [P, RING, UNIT], F32R)
    ubuf = place("ubuf", [P, T])
    gbuf = place("gbuf", [P, T])
    sq = place("sq", [P, 2, T])
    ss = place("ss", [P, T])
    rstd = place("rstd", [P, T])
    par = place("par", [P, NPAR])
    ones = place("ones", [P, P])
    eps = place("eps", [P, 1])
    rcol = place("rcol", [P, 4])
    ident_r = place("ident_r", [P, P], F32R)
    s5p = place("s5p", [P, 16, 16])
    c8 = place("c8", [P, 2, KD])
    gain12 = place("gain12", [P, KD])
    eps2 = place("eps2", [P, 1])
    soft = place("soft", [P, 4, KD])
    ident = place("ident", [P, P])
    aux = cursor[0]
    cursor[0] += 8192
    work = cursor[0]
    h_hi = place("h_hi", [P, KF, T], F32R)
    h_lo = place("h_lo", [P, KF, T], F32R)
    KB = 1024

    gate_w = place("gate_w", [P, 2, KD, P], at=aux)
    r_pad = place("r_pad", [P, KD, T + 3], at=work)
    y_rec = place("y_rec", [P, KD, T], at=work)
    conv = place("conv", [P, KD, T], at=work + 17 * KB)
    ga = place("ga", [P, KD, T], at=work + 33 * KB)
    gx = place("gx", [P, KD, T], at=work + 49 * KB)
    hs = place("hs", [P, KD, T], at=work + 65 * KB)
    yh_hi = place("yh_hi", [P, KD, T], F32R, at=work + 17 * KB)
    yh_lo = place("yh_lo", [P, KD, T], F32R, at=work + 49 * KB)

    ws_raw = place("ws_raw", [P, KD, P], at=aux)
    bsb = place("bsb", [P, KD, P], at=aux + 4 * KB)
    vt = place("vt", [P, 4, D], at=work)
    ug = place("ug", [P, KD, T], at=work + 16 * KB)
    sgy_hi = place("sgy_hi", [P, KD, T], F32R, at=work + 32 * KB)
    sgy_lo = place("sgy_lo", [P, KD, T], F32R, at=work + 48 * KB)
    ws = place("ws", [P, KD, P], at=work + 64 * KB)
    tri = place("tri", [P, P], U8, at=work + 68 * KB)
    tri_f = place("tri_f", [P, P], at=work + 69 * KB)
    vss = place("vss", [P, 3, 8], at=work + 68 * KB + 128)

    gate_buf = (gbuf, ubuf)

    bank = [ctx.enter_context(nc.psum_tensor(f"bank{i}", [P, T], F32)) for i in range(8)]

    R = work + 48 * KB
    y0_hi = place("y0_hi", [P, 4, T], F32R, at=work)
    y0_lo = place("y0_lo", [P, 4, T], F32R, at=work + 8 * KB)
    y1_hi = place("y1_hi", [P, 4, T], F32R, at=work + 16 * KB)
    y1_lo = place("y1_lo", [P, 4, T], F32R, at=work + 24 * KB)
    merged = place("merged", [P, KD, T], at=work + 32 * KB)
    qk = place("qk", [P, 8, T], at=R)
    vtok = place("vtok", [P, 4, T], at=R + 16 * KB)
    prob = place("prob", [P, 3, T], at=R + 34 * KB)
    probT = place("probT", [P, 2, T], at=R + 24 * KB)
    negc = place("negc", [8, T], at=R + 34 * KB)
    negc_hi = place("negc_hi", [8, T], F32R, at=R + 28 * KB)
    negc_lo = place("negc_lo", [8, T], F32R, at=R + 30 * KB)
    qk_r = place("qk_r", [16, T], at=R + 32 * KB)
    sel8 = place("sel8", [8, 8, P], at=aux)
    pack = place("pack", [P, 32], at=aux + 5 * KB)
    ff_w = place("ff_w", [P, KD, 8], at=aux + 5 * KB + 128)
    causal = place("causal", [P, P], at=aux + 5 * KB + 384)
    sel8_r = place("sel8_r", [8, 8, P], F32R, at=aux)
    causal_r = place("causal_r", [P, P], F32R, at=aux + 5 * KB + 384)
    att_m = place("att_m", [P, 32], at=aux + 6 * KB)
    att_l = place("att_l", [P, 32], at=aux + 6 * KB + 128)
    ff_b = place("ff_b", [8, 1], at=aux + 6 * KB + 256)
    ff_hi = place("ff_hi", [P, KD, 8], F32R, at=aux + 6 * KB + 512)
    ff_lo = place("ff_lo", [P, KD, 8], F32R, at=aux + 6 * KB + 768)
    s5_b = place("s5_b", [P, 2, 16, 16], at=work + 20 * KB)
    s5_c = place("s5_c", [P, 2, 16, 16], at=work + 22 * KB)
    s5_t = place("s5_t", [P, 2, 2, 16, 16], at=work + 24 * KB)
    s5_bx = place("s5_bx", [P, 2, 16, 32], at=work + 16 * KB)
    spread = place("spread", [16, 8 * P], at=work + 28 * KB)
    su = place("su", [P, 4, T], at=work + 32 * KB)
    s5_cx = place("s5_cx", [P, 2, 16, 32], at=work + 40 * KB)
    s5_bt = place("s5_bt", [P, 2, 4, P], at=work + 44 * KB)
    rot = place("rot", [P, 2, 2, T], at=work + 16 * KB)
    s5_g = [place("s5_g0", [P, 2, T], at=R + 24 * KB),
            place("s5_g1", [P, 2, T], at=work + 24 * KB)]
    s5_m = place("s5_m", [P, 2, T], at=work + 28 * KB)
    iota = place("iota", [P, T], at=aux)
    turn = place("turn", [P, T], at=aux + 2 * KB)
    hq = place("hq", [P, 12, T], at=R)
    hv = place("hv", [P, 4, T], at=R + 24 * KB)
    hk = place("hk", [P, 4, T], at=R + 32 * KB)
    he = place("he", [P, 2, T], at=aux)
    hm = place("hm", [P, 8, P], U8, at=aux + 5 * KB + 512)
    levels_f = place("levels_f", [P, 8 * P], at=work + 24 * KB)
    hS = place("hS", [P, 3, P], at=aux + 4 * KB)
    hf_odd = place("hf_odd", [P, T], at=R + 28 * KB)
    hdec = place("hdec", [P, 4], at=aux + 6 * KB + 512)
    memx = place("memx", [P, KD, NMEM], at=R)
    mem_hi = place("mem_hi", [P, KD, NMEM], F32R, at=R + 8 * KB)
    mem_lo = place("mem_lo", [P, KD, NMEM], F32R, at=R + 16 * KB)
    kx = place("kx", [P, KD, NMEM], at=R + 24 * KB)
    vx = place("vx", [P, 2, D], at=R + 32 * KB)
    msq = place("msq", [P, KD, NMEM], at=R + 24 * KB)
    qx = place("qx", [P, KD, T], at=work)
    o_hi = place("o_hi", [P, KD, T], F32R, at=work + 16 * KB)
    o_lo = place("o_lo", [P, KD, T], F32R, at=work + 32 * KB)
    rstd_m = place("rstd_m", [P, NMEM], at=aux)
    rcol_m = place("rcol_m", [P, 2], at=aux + 5 * KB)
    xa_m = place("xa_m", [P, 16], at=aux + 5 * KB + 64)
    xa_l = place("xa_l", [P, 16], at=aux + 5 * KB + 128)
    xa_r = place("xa_r", [P, 16], at=aux + 5 * KB + 192)
    gain_kq = place("gain_kq", [P, 2], at=aux + 5 * KB + 256)
    eps256 = place("eps256", [P, 1], at=aux + 5 * KB + 288)
    xprob = place("xprob", [P, 3, NMEM], at=R)
    xprobT = place("xprobT", [P, 2, 2, T], at=R + 8 * KB)

    def sem(name):
        return ctx.enter_context(nc.semaphore(name))

    w_loaded = [sem(f"w_loaded{r}") for r in range(RING)]
    w_hi_ready, w_lo_ready = sem("w_hi_ready"), sem("w_lo_ready")
    unit_used = sem("unit_used")
    taken = sem("taken")
    x_in = [sem(f"x_in{j}") for j in range(KD // 2)]
    par_in, ones_set = sem("par_in"), sem("ones_set")
    xg_hi_ready, xg_lo_ready = sem("xg_hi_ready"), sem("xg_lo_ready")
    sq_ready, ss_added, ss_summed = sem("sq_ready"), sem("ss_added"), sem("ss_summed")
    std_ready, rstd_ready = sem("std_ready"), sem("rstd_ready")
    silu_done, prod_done = sem("silu_done"), sem("prod_done")
    h_hi_ready, h_lo_ready = sem("h_hi_ready"), sem("h_lo_ready")
    gate_w_in, gate_w_zero = sem("gate_w_in"), sem("gate_w_zero")
    pad_zero, conv_step, gates_mm, gates_sig = sem("pad_zero"), sem("conv_step"), sem("gates_mm"), sem("gates_sig")
    c8_ready = sem("c8_ready")
    decay_step, mult2_done, mult_done = sem("decay_step"), sem("mult2_done"), sem("mult_done")
    gated_in = sem("gated_in")
    drive_step, scan_done, gelu_done = sem("drive_step"), sem("scan_done"), sem("gelu_done")
    yh_done, yh_hi_ready, yh_lo_ready = sem("yh_done"), sem("yh_hi_ready"), sem("yh_lo_ready")
    ws_in, ws_zero, ws_ready = sem("ws_in"), sem("ws_zero"), sem("ws_ready")
    v_sum = sem("v_sum")
    v_gelu, v_sq, v_std, v_rstd, v_normed = sem("v_gelu"), sem("v_sq"), sem("v_std"), sem("v_rstd"), sem("v_normed")
    u_gelu, mixed, gated, sgy_hi_ready, sgy_lo_ready = (
        sem("u_gelu"), sem("mixed"), sem("gated"), sem("sgy_hi_ready"), sem("sgy_lo_ready"))
    final_gain, final_sum, final_step = sem("final_gain"), sem("final_sum"), sem("final_step")
    ident_in = sem("ident_in")
    col_summed, col_std, col_rstd = sem("col_summed"), sem("col_std"), sem("col_rstd")
    mix_in = sem("mix_in")
    qk_sq, qk_ss, qk_std, qk_rstd, qk_spread, qk_scaled = (
        sem(n) for n in ("qk_sq", "qk_ss", "qk_std", "qk_rstd", "qk_spread", "qk_scaled"))
    ff_split, ff_mm, ff_z, ff_ln, negc_step, negc_ready = (sem(n) for n in ("ff_split", "ff_mm", "ff_z", "ff_ln", "negc_step", "negc_ready"))
    att_s, att_nmax, att_exp, att_p, att_t, att_tc, att_o = (
        sem(n) for n in ("att_s", "att_nmax", "att_exp", "att_p", "att_t", "att_tc", "att_o"))
    fox_hi, fox_lo = sem("fox_hi"), sem("fox_lo")
    s5_act, s5_dve, s5_zero, s5_bprod, s5_bbar, s5_cx_ready, s5_bx_ready, s5_bt_mm, s5_bt_ready, iota_in = (
        sem(n) for n in ("s5_act", "s5_dve", "s5_zero", "s5_bprod", "s5_bbar", "s5_cx_ready", "s5_bx_ready", "s5_bt_mm", "s5_bt_ready", "iota_in"))
    s5_turn, s5_rot, s5_drive, s5_step, s5_prod, s5_nprod, s5_ymm, s5_y = (
        sem(n) for n in ("s5_turn", "s5_rot", "s5_drive", "s5_step", "s5_prod", "s5_nprod", "s5_ymm", "s5_y"))
    z_ready, z_hi_ready, z_lo_ready, glu_sig, glu_out, s5_hi, s5_lo = (
        sem(n) for n in ("z_ready", "z_hi_ready", "z_lo_ready", "glu_sig", "glu_out", "s5_hi", "s5_lo"))
    levels_in, levels_ready, hg_zero, hg_key, hg_silu, hg_ln, hg_cum = (
        sem(n) for n in ("levels_in", "levels_ready", "hg_zero", "hg_key", "hg_silu", "hg_ln", "hg_cum"))
    hg_diff, hg_exp, hg_fac, hg_score, hg_sel, hg_dec = (
        sem(n) for n in ("hg_diff", "hg_exp", "hg_fac", "hg_score", "hg_sel", "hg_dec"))
    hg_kt, hg_ktc, hg_update, hg_state, hg_o, hg_osq, hg_oss, hg_std, hg_y, hg_hi, hg_lo = (
        sem(n) for n in ("hg_kt", "hg_ktc", "hg_update", "hg_state", "hg_o", "hg_osq", "hg_oss", "hg_std", "hg_y", "hg_hi", "hg_lo"))
    gate_tanh, merge_step, m_hi_ready, m_lo_ready = (
        sem(n) for n in ("gate_tanh", "merge_step", "m_hi_ready", "m_lo_ready"))
    mem_in, mem_sq, mem_hi_ready, mem_lo_ready, mem_ss, mem_std, mem_rstd = (
        sem(n) for n in ("mem_in", "mem_sq", "mem_hi_ready", "mem_lo_ready", "mem_ss", "mem_std", "mem_rstd"))
    xn_sq, xn_ss, xn_std, xn_scaled = (sem(n) for n in ("xn_sq", "xn_ss", "xn_std", "xn_scaled"))
    xo_hi_ready, xo_lo_ready = sem("xo_hi_ready"), sem("xo_lo_ready")
    dve_chain, act_chain = Chain(sem("dve_chain")), Chain(sem("act_chain"))
    out_stored = sem("out_stored")
    block = ctx.enter_context(nc.Block())

    def f32(ap):
        return ap.bitcast(F32)

    def tile(t, i):
        return t[:, bass.ds(i, 1), :].rearrange("p a t -> p (a t)")

    def col(name, i=0):
        return par[:, bass.ds(i + PARAMS[name], 1)]

    def load_layer(sp, L):
        def body(b, first=False):
            for i, w in enumerate(L.widths):
                if first and i < 2:
                    continue
                if not first or i >= RING:
                    sp.wait_ge(w_lo_ready, b * L.per + (L.base + i + 1 - RING))
                sp.dma_start(w_stage[:, i % RING, 0:w], L.src(b, i)).then_inc(w_loaded[i % RING], 16)
        if L.base == 0:
            body(0, first=True)
            with sp.Fori(1, L.bodies) as b:
                body(b)
        else:
            each_body(sp, L.bodies, body)

    def split_hi(act, L, b, i):
        if i >= L.per:
            b, i = b + 1, i - L.per
        if isinstance(b, int) and b == L.bodies:
            at = order.index(L) + 1
            if at == len(order):
                return
            L, b = order[at], 0
        r, w = i % RING, L.widths[i]
        act.wait_ge(w_loaded[r], b * (16 * L.per // RING) + 16 * (L.base // RING + i // RING + 1))
        if not (L.base == 0 and isinstance(b, int) and b == 0 and i < RING):
            act.wait_ge(unit_used, b * L.per + (L.base + i + 1 - RING))
        act.activation(w_hi[:, r, 0:w], w_stage[:, r, 0:w], ACT.Copy).then_inc(w_hi_ready, 1)

    def act_bodies(act, L, work=None, only=None):
        def body(b):
            for i in range(L.per):
                split_hi(act, L, b, i + AHEAD)
                if work is not None:
                    work(b, i)
        if only is not None:
            body(only)
            return
        body(0)
        if L.bodies > 2:
            with act.Fori(1, L.bodies - 1) as b:
                body(b)
        if L.bodies > 1:
            body(L.bodies - 1)

    def split_lo(pool, L):
        def body(b):
            for i, w in enumerate(L.widths):
                r = i % RING
                pool.wait_ge(w_hi_ready, b * L.per + (L.base + i + 1))
                pool.tensor_tensor(w_lo[:, r, 0:w], w_stage[:, r, 0:w], f32(w_hi[:, r, 0:w]),
                                   ALU.subtract).then_inc(w_lo_ready, 1)
        each_body(pool, L.bodies, body)

    def split_lo_unit(pool, L, b, i):
        r, w = i % RING, L.widths[i]
        pool.wait_ge(w_hi_ready, L.base + b * L.per + i + 1)
        pool.tensor_tensor(w_lo[:, r, 0:w], w_stage[:, r, 0:w], f32(w_hi[:, r, 0:w]), ALU.subtract).then_inc(w_lo_ready, 1)

    def three_passes(pe, out, r, j, hi, lo, start, stop):
        c = slice(j * P, (j + 1) * P)
        pe.matmul(out, w_hi[:, r, c], hi, start=start, stop=False)
        pe.matmul(out, w_hi[:, r, c], lo, start=False, stop=False)
        return pe.matmul(out, w_lo[:, r, c], hi, start=False, stop=stop)

    def project_unit(pe, L, b, i, hi, lo, ready=None, width=T):
        r = i % RING
        pe.wait_ge(w_lo_ready, b * L.per + (L.base + i + 1))
        if L.rbase or not isinstance(b, int) or b:
            pe.wait_ge(taken, b * L.per + (L.rbase + i + 1 - RING))
        for k in range(KD):
            if i == 0 and ready is not None:
                pe.wait_ge(ready[0], ready[1] + k + 1)
            mm = three_passes(pe, bank[r][:, 0:width], r, k, hi[:, k, :], lo[:, k, :], k == 0, k == KD - 1)
        mm.then_inc(unit_used, 1)

    def pe_project(pe, L, hi, lo, ready, norm=None, width=T, norm_after=0):
        def body(b):
            for i in range(L.per):
                project_unit(pe, L, b, i, hi, lo, ready, width)
                if norm is not None and isinstance(b, int) and b == 0 and i == norm_after:
                    norm(pe)
        if norm is None:
            each_body(pe, L.bodies, body)
            return
        body(0)
        if L.bodies == 2:
            body(1)
        else:
            with pe.Fori(1, L.bodies) as b:
                body(b)

    def pe_tokens_unit(pe, L, b, i, hi, lo, ntt=4, ready=None):
        pe.wait_ge(w_lo_ready, b * 4 + (L.base + i + 1))
        for kk in range(2):
            k = 2 * i + kk
            wh, wl = (w[:, i, kk * T:(kk + 1) * T] for w in (w_hi, w_lo))
            for t in range(ntt):
                if k == 0:
                    pe.wait_ge(taken, b * ntt + (L.rbase + t + 1 - RING))
                if t == 0 and ready is not None and b == 0:
                    pe.wait_ge(ready[0], ready[1] + k + 1)
                c = slice(t * P, (t + 1) * P)
                out = bank[t if ntt == RING else b * ntt + t][:]
                pe.matmul(out, hi[:, k, c], wh, start=k == 0, stop=False)
                pe.matmul(out, lo[:, k, c], wh, start=False, stop=False)
                mm = pe.matmul(out, hi[:, k, c], wl, start=False, stop=k == KD - 1)
        mm.then_inc(unit_used, 1)

    def pe_project_tokens(pe, L, hi, lo, ntt=4, norm=None, ready=None):
        for b in range(L.bodies):
            for i in range(4):
                pe_tokens_unit(pe, L, b, i, hi, lo, ntt, ready)
                if norm is not None and b == 0 and i == 0:
                    norm(pe)

    def split_count(q):
        return KD * (q - (q > FINAL))

    def act_norm_tile(act, q, gain, m, buf):
        act.activation(tile(xg_hi, m), tile(x, m), ACT.Copy, scale=col(*gain(m))).then_inc(xg_hi_ready, 1)
        act_norm_square(act, q, m, buf)

    def act_norm_square(act, q, m, buf):
        if not (q == 0 and isinstance(m, int) and m < 2):
            act.wait_ge(ss_added, m + (KD + 1) * q)
        act.activation(sq[:, buf, :], tile(x, m), ACT.Square).then_inc(sq_ready, 1)

    def dve_norm_tile(dve, q, gain, m, buf):
        dve.wait_ge(xg_hi_ready, m + (split_count(q) + 1))
        dve.scalar_tensor_tensor(tile(xg_lo, m), tile(x, m), col(*gain(m)), f32(tile(xg_hi, m)),
                                 ALU.mult, ALU.subtract).then_inc(xg_lo_ready, 1)
        dve_norm_add(dve, q, m, buf)

    def dve_norm_add(dve, q, m, buf):
        dve.wait_ge(sq_ready, m + (KD * q + 1))
        dve.wait_ge(ss_added, m + ((KD + 1) * q + 1))
        dve.tensor_tensor(ss[:], ss[:], sq[:, buf, :], ALU.add).then_inc(ss_added, 1)

    def pe_norm_sum(pe, q):
        pe.wait_ge(ss_added, (KD + 1) * (q + 1))
        pe.matmul(bank[4][:], ones[:], ss[:], start=True, stop=True).then_inc(ss_summed, 1)

    def act_norm_std(act, q):
        act.wait_ge(ss_summed, q + 1)
        act.activation(rstd[:], bank[4][:], ACT.Sqrt, bias=eps[:], scale=1.0 / D).then_inc(std_ready, 1)

    def dve_norm_rstd(dve, q):
        dve_norm_rstd_of(dve, rstd, q)

    def dve_norm_rstd_of(dve, std, q):
        dve.wait_ge(std_ready, q + 1)
        dve.reciprocal(std[:], std[:]).then_inc(rstd_ready, 1)
        dve.wait_ge(rstd_ready, q + 1)

    def pe_norm_columns(pe, squares):
        for t in range(4):
            mm = pe.matmul(bank[5][:, t:t + 1], squares[:, t * P:(t + 1) * P], ones[:, 0:1], start=True, stop=True)
        mm.then_inc(col_summed, 1)

    def act_norm_columns(act, n):
        act.wait_ge(col_summed, n)
        act.activation(rcol[:], bank[5][:, 0:4], ACT.Sqrt, bias=eps[:], scale=1.0 / D).then_inc(col_std, 1)

    def dve_norm_columns(dve, n):
        dve.wait_ge(col_std, n)
        dve.reciprocal(rcol[:], rcol[:]).then_inc(col_rstd, 1)
        dve.wait_ge(col_rstd, n)

    def pe_ffn(pe, i, q):
        U, L = layers[f"up{i}"], layers[f"down{i}"]
        pe_project(pe, U, xg_hi, xg_lo, (xg_lo_ready, split_count(q)), norm=lambda pe: pe_norm_sum(pe, q),
                   norm_after=0 if q else 2)

        def down(b):
            for m in range(4):
                pe.wait_ge(taken, b * 4 + (L.rbase + m + 1 - RING))
                for part in range(3):
                    u = 3 * m + part
                    k1 = min(8 * part + 8, KF)
                    pe.wait_ge(w_lo_ready, b * L.per + (L.base + u + 1))
                    pe.wait_ge(h_lo_ready, KF * i + k1)
                    for k in range(8 * part, k1):
                        mm = three_passes(pe, bank[m][:], u % RING, k - 8 * part, h_hi[:, k, :], h_lo[:, k, :],
                                          k == 0, k == KF - 1)
                    mm.then_inc(unit_used, 1)
        each_body(pe, L.bodies, down)

    def act_ffn(act, i):
        U = layers[f"up{i}"]

        def up(b, u):
            if i == 0 and u == 0 and isinstance(b, int) and b == 0:
                act.wait_ge(ones_set, 3)
                act_norm_std(act, 0)
            if u % 2 == 1:
                act.wait_ge(taken, b * 4 + (U.rbase + u + 1))
                act.activation(gbuf[:], gbuf[:], ACT.Silu).then_inc(silu_done, 1)
                act.wait_ge(prod_done, b * 2 + (KF * i + u // 2 + 1))
                act.activation(tile(h_hi, b * 2 + u // 2), ubuf[:], ACT.Copy).then_inc(h_hi_ready, 1)
        act.preload_act_table(ACT.Silu)
        act_bodies(act, U, up)

    def dve_ffn(dve, i):
        U = layers[f"up{i}"]

        def up(b):
            for jj in range(2):
                j = b * 2 + jj
                if i or not isinstance(j, int) or j:
                    dve.wait_ge(h_lo_ready, j + KF * i)
                dve.wait_ge(unit_used, b * 4 + (U.base + 2 * jj + 1))
                dve.tensor_tensor(ubuf[:], bank[2 * jj][:], rstd[:], ALU.mult).then_inc(taken, 1)
                dve.wait_ge(unit_used, b * 4 + (U.base + 2 * jj + 2))
                dve.tensor_tensor(gbuf[:], bank[2 * jj + 1][:], rstd[:], ALU.mult).then_inc(taken, 1)
                dve.wait_ge(silu_done, j + (KF * i + 1))
                dve.tensor_tensor(ubuf[:], gbuf[:], ubuf[:], ALU.mult).then_inc(prod_done, 1)
                dve.wait_ge(h_hi_ready, j + (KF * i + 1))
                dve.tensor_tensor(tile(h_lo, j), ubuf[:], f32(tile(h_hi, j)), ALU.subtract).then_inc(h_lo_ready, 1)
        up(0)
        with dve.Fori(1, U.bodies) as b:
            up(b)

    def dve_residual(dve, L, scale, q, gain):
        upr = L.n // KD
        mb = L.per // upr
        if q is not None:
            dve.memset(ss[:], 0.0).then_inc(ss_added, 1)

        def body(b):
            for mm in range(mb):
                m = b * mb + mm
                dve.wait_ge(unit_used, b * L.per + (L.base + (mm + 1) * upr))
                dve.scalar_tensor_tensor(tile(x, m), bank[mm % 4][:], scale, tile(x, m),
                                         ALU.mult, ALU.add).then_inc(taken, 1)
                if q is not None:
                    dve_norm_tile(dve, q, gain, m, mm % 2)
        each_body(dve, L.bodies, body)
        if q is not None:
            dve_norm_rstd(dve, q)

    def act_residual(act, L, q, gain):
        upr = L.n // KD
        mb = L.per // upr

        def result(b, i):
            if q is not None and i % upr == upr - 1:
                m = b * mb + i // upr
                act.wait_ge(taken, m + (L.rbase + 1))
                act_norm_tile(act, q, gain, m, (i // upr) % 2)
        act_bodies(act, L, result)
        if q is not None:
            act_norm_std(act, q)

    def gain_of(name, i=0):
        return lambda m: (name, m + i * KD)

    def sp_rec(sp):
        sp.wait_ge(gate_w_zero, 1)
        for g, name in enumerate(("gate_a_w", "gate_x_w")):
            for s in range(2):
                h = slice(64 * s, 64 * s + 64)
                sp.dma_start(gate_w[h, g, :, h], io[name][h, :].rearrange("p (t j) -> p t j", j=64)).then_inc(gate_w_in, 16)

    def dve_softplus(dve):
        lam = par[:, PARAMS["rec_lambda"]:PARAMS["rec_lambda"] + KD]
        u, s, s2, p = (soft[:, j, :] for j in range(4))
        dve.wait_ge(act_chain.sem, 2)
        dve_chain(dve, dve.tensor_scalar(s2, u, 2.0, None, ALU.add))
        dve_chain(dve, dve.reciprocal(s2, s2))
        dve_chain(dve, dve.tensor_tensor(s, u, s2, ALU.mult))
        dve_chain(dve, dve.tensor_tensor(s2, s, s, ALU.mult))
        dve_chain(dve, dve.tensor_scalar(p, s2, 1.0 / 19, 1.0 / 17, ALU.mult, ALU.add))
        for n in (15, 13, 11, 9, 7, 5, 3, 1):
            dve_chain(dve, dve.tensor_tensor(p, p, s2, ALU.mult))
            dve_chain(dve, dve.tensor_scalar(p, p, 1.0 / n, None, ALU.add))
        dve_chain(dve, dve.tensor_tensor(p, p, s, ALU.mult))
        dve_chain(dve, dve.tensor_scalar(s2, lam, -1.0, 0.0, ALU.mult, ALU.max))
        dve_chain(dve, dve.scalar_tensor_tensor(p, p, 2.0, s2, ALU.mult, ALU.add))
        dve.tensor_scalar(c8[:, 0, :], p, 8.0, None, ALU.mult).then_inc(c8_ready, 1)
        dve.tensor_scalar(c8[:, 1, :], p, -8.0, None, ALU.mult).then_inc(c8_ready, 1)

    def act_softplus(act):
        lam = par[:, PARAMS["rec_lambda"]:PARAMS["rec_lambda"] + KD]
        u = soft[:, 0, :]
        act_chain(act, act.activation(u, lam, ACT.Abs))
        act_chain(act, act.activation(u, u, ACT.Exp, scale=-1.0))

    REC_EARLY = 5
    def pe_rec(pe, q):
        R, Y, L = layers["rec_r"], layers["rec_y"], layers["rec_out"]

        def gates(m):
            if m == 0:
                pe.wait_ge(gate_w_in, 64)
            pe.wait_ge(conv_step, 4 * (m + 1))
            if m >= 2:
                pe.wait_ge(gates_sig, 2 * (m - 1))
            for g in range(2):
                mm = pe.matmul(bank[4 + 2 * (m % 2) + g][:], gate_w[:, g, m, :], conv[:, m, :], start=True, stop=True)
            mm.then_inc(gates_mm, 1)

        for u in range(KD):
            project_unit(pe, R, u // 4, u % 4, xg_hi, xg_lo, (xg_lo_ready, split_count(q)) if u == 0 else None)
            if u == 0:
                pe_norm_sum(pe, q)
            if u == 2:
                gates(0)
            if u >= 2:
                gates(u - 1)
        for u in range(KD):
            project_unit(pe, Y, u // 4, u % 4, xg_hi, xg_lo)
            if u == 0:
                gates(KD - 1)
        pe_project(pe, L, yh_hi, yh_lo, (yh_lo_ready, 0))

    def dve_rec(dve):
        R, Y = layers["rec_r"], layers["rec_y"]
        dve.memset(r_pad[:, :, 0:3], 0.0).then_inc(pad_zero, 1)
        dve.wait_ge(pad_zero, 1)

        def r_tiles(b):
            for mm in range(4):
                m = b * 4 + mm
                dve.wait_ge(unit_used, b * 4 + (R.base + mm + 1))
                dve.tensor_tensor(r_pad[:, bass.ds(m, 1), 3:T + 3], bank[mm][:].unsqueeze(1),
                                  rstd[:].unsqueeze(1), ALU.mult).then_inc(taken, 1)
                dve.wait_ge(taken, b * 4 + (R.rbase + mm + 1))
                c = conv[:, bass.ds(m, 1), :]
                dve.tensor_scalar(c, r_pad[:, bass.ds(m, 1), 0:T], col("rec_conv_w", m), col("rec_conv_b", m),
                                  ALU.mult, ALU.add).then_inc(conv_step, 1)
                for k in range(1, 4):
                    dve.wait_ge(conv_step, m * 4 + k)
                    dve.scalar_tensor_tensor(c, r_pad[:, bass.ds(m, 1), k:k + T], col("rec_conv_w", m + KD * k), c,
                                             ALU.mult, ALU.add).then_inc(conv_step, 1)
        each_body(dve, R.bodies, r_tiles)
        dve.wait_ge(conv_step, 4 * KD)

        def multiplier(m):
            dve.wait_ge(decay_step, 3 * m + 3)
            dve.scalar_tensor_tensor(hs[:, m, :], sq[:, m % 2, :], 1.0, hs[:, m, :], ALU.add, ALU.mult).then_inc(mult2_done, 1)

        def scan(m):
            dve.wait_ge(mult_done, m + 1)
            dve.wait_ge(gated_in, m + 1)
            dve.tensor_tensor(conv[:, m, :], conv[:, m, :], hs[:, m, :], ALU.mult).then_inc(drive_step, 1)
            dve.wait_ge(drive_step, m + 1)
            dve.tensor_tensor_scan(hs[:, m, :], ga[:, m, :], conv[:, m, :], 0.0, ALU.mult, ALU.add).then_inc(scan_done, 1)

        def yh(m):
            dve.wait_ge(gelu_done, m + 1)
            dve.tensor_tensor(hs[:, m, :], hs[:, m, :], y_rec[:, m, :], ALU.mult).then_inc(yh_done, 1)

        def low(m):
            dve.wait_ge(yh_hi_ready, m + 1)
            dve.tensor_tensor(yh_lo[:, m, :], hs[:, m, :], f32(yh_hi[:, m, :]), ALU.subtract).then_inc(yh_lo_ready, 1)

        for u in range(KD):
            dve.wait_ge(unit_used, Y.base + u + 1)
            dve.tensor_tensor(y_rec[:, u, :], bank[u % 4][:], rstd[:], ALU.mult).then_inc(taken, 1)
            if u < 4:
                multiplier(2 * u)
                multiplier(2 * u + 1)
            if 4 <= u < 6:
                for m in range(4):
                    scan(4 * (u - 4) + m)
            if u == 6:
                dve.wait_ge(scan_done, KD)
                for m in range(REC_EARLY):
                    yh(m)
                    if m:
                        low(m - 1)
        for m in range(REC_EARLY, KD):
            yh(m)
            low(m - 1)
        low(KD - 1)

    def pool_rec(pool):
        Y = layers["rec_y"]
        for u in range(KD):
            split_lo_unit(pool, Y, u // 4, u % 4)
            pool.wait_ge(gates_sig, 2 * (u + 1))
            pool.tensor_tensor(conv[:, u, :], conv[:, u, :], gx[:, u, :], ALU.mult).then_inc(gated_in, 1)

    def act_rec(act):
        R, Y = layers["rec_r"], layers["rec_y"]

        def sigmoids(m):
            act.wait_ge(gates_mm, m + 1)
            for g, (out, bias) in enumerate(((ga, "rec_gate_a_b"), (gx, "rec_gate_x_b"))):
                act.activation(out[:, m, :], bank[4 + 2 * (m % 2) + g][:], ACT.Sigmoid, bias=col(bias, m)).then_inc(gates_sig, 1)

        def decay(m):
            act.activation(hs[:, m, :], ga[:, m, :], ACT.Tanh, scale=c8[:, 0, m:m + 1]).then_inc(decay_step, 1)
            act.wait_ge(decay_step, 3 * m + 1)
            act.activation(ga[:, m, :], ga[:, m, :], ACT.Exp, scale=c8[:, 1, m:m + 1]).then_inc(decay_step, 1)
            act.wait_ge(decay_step, 3 * m + 2)
            if m >= 2:
                act.wait_ge(mult2_done, m - 1)
            act.activation(sq[:, m % 2, :], ga[:, m, :], ACT.Square).then_inc(decay_step, 1)

        def multiplier(m):
            act.wait_ge(mult2_done, m + 1)
            act.activation(hs[:, m, :], hs[:, m, :], ACT.Sqrt).then_inc(mult_done, 1)

        def gelus(tiles):
            for m in tiles:
                act.wait_ge(taken, Y.rbase + m + 1)
                act.activation(y_rec[:, m, :], y_rec[:, m, :], ACT.Gelu_apprx_tanh).then_inc(gelu_done, 1)

        def copies(tiles):
            for m in tiles:
                act.wait_ge(yh_done, m + 1)
                act.activation(yh_hi[:, m, :], hs[:, m, :], ACT.Copy).then_inc(yh_hi_ready, 1)

        for u in range(2 * KD):
            L = R if u < KD else Y
            split_hi(act, L, u % KD // 4, u % 4 + AHEAD)
            if 2 <= u < 2 + KD:
                sigmoids(u - 2)
            if u == KD + 1:
                act.wait_ge(gates_sig, 2 * KD)
                act.wait_ge(c8_ready, 2)
            if KD + 1 <= u < KD + 5:
                decay(2 * (u - KD - 1))
                decay(2 * (u - KD - 1) + 1)
            if u in (KD + 3, KD + 5):
                for m in range(4):
                    multiplier(2 * (u - KD - 3) + m)
            if u == 2 * KD - 2:
                gelus(range(REC_EARLY))
        copies(range(REC_EARLY))
        gelus(range(REC_EARLY, KD))
        copies(range(REC_EARLY, KD))

    def act_load_sgu(act):
        act.dma_start(ws_raw[:].rearrange("p h t -> p (h t)"), io["sg_wsT"]).then_inc(ws_in, 16)
        act.dma_start(bsb[:].rearrange("p h t -> p (h t)"), io["sg_bs"].to_broadcast([P, D])).then_inc(ws_in, 16)
        act.dma_start(tri_f[:], io["c_tri"]).then_inc(ws_in, 16)

    def pe_sgu(pe, q):
        V, U, L = layers["sg_v"], layers["sg_u"], layers["sg_out"]
        def norms(pe):
            pe_norm_sum(pe, q)
            pe_norm_columns(pe, ss)
        pe_project_tokens(pe, V, xg_hi, xg_lo, norm=norms, ready=(xg_lo_ready, split_count(q)))

        def mix(h):
            if h >= 4:
                pe.wait_ge(gated, h - 3)
            for n in range(4):
                if h == 0:
                    pe.wait_ge(v_normed, n + 1)
                mm = pe.matmul(bank[4 + h % 4][:, n * P:(n + 1) * P], vt[:, n, h * P:(h + 1) * P], ws[:, h, :],
                               start=True, stop=True)
            mm.then_inc(mixed, 1)
        for u in range(KD):
            project_unit(pe, U, u // 4, u % 4, xg_hi, xg_lo)
            if u == 2:
                pe.wait_ge(ws_ready, 1)
                mix(0)
            if u >= 2:
                mix(u - 1)
        mix(KD - 1)
        pe_project(pe, L, sgy_hi, sgy_lo, (sgy_lo_ready, 0))

    def dve_sgu(dve):
        V, U = layers["sg_v"], layers["sg_u"]
        dve.memset(ws[:], 0.0).then_inc(ws_zero, 1)
        dve.wait_ge(ws_zero, 1)
        dve.wait_ge(ws_in, 48)
        dve_chain(dve, dve.tensor_copy(tri[:], tri_f[:]))
        dve.copy_predicated(ws[:], tri[:].unsqueeze(1).to_broadcast([P, KD, P]), ws_raw[:]).then_inc(ws_ready, 1)

        def v_tiles(b):
            for t in range(4):
                dve.wait_ge(unit_used, b * 4 + (V.base + 4))
                dve.tensor_scalar(vt[:, t, bass.ds(b * T, T)], bank[t][:], rcol[:, t:t + 1], None, ALU.mult).then_inc(taken, 1)
        each_body(dve, V.bodies, v_tiles)
        dve.wait_ge(v_sq, 8)
        dve.tensor_tensor(vss[:, 1, 0:4], vss[:, 0, 0:4], vss[:, 0, 4:8], ALU.add).then_inc(v_sum, 1)
        dve.wait_ge(v_std, 1)
        dve.reciprocal(vss[:, 2, 0:4], vss[:, 2, 0:4]).then_inc(v_rstd, 1)
        dve.wait_ge(v_rstd, 1)
        for t in range(4):
            dve.tensor_scalar(vt[:, t, :], vt[:, t, :], vss[:, 2, t:t + 1], None, ALU.mult).then_inc(v_normed, 1)

        def gate(h):
            g4 = gate_buf[h % 2][:].rearrange("p (n t) -> p n t", t=P)
            dve.wait_ge(mixed, h + 1)
            dve.scalar_tensor_tensor(g4, bank[4 + h % 4][:].rearrange("p (n t) -> p n t", t=P), col("sg_v_norm", h),
                                     bsb[:, h, :].unsqueeze(1).to_broadcast([P, 4, P]), ALU.mult, ALU.add).then_inc(gated, 1)
            dve.wait_ge(gated, h + 1)
            dve.wait_ge(u_gelu, h + 1)
            dve.tensor_tensor(ug[:, h, :], ug[:, h, :], gate_buf[h % 2][:], ALU.mult).then_inc(yh_done, 1)

        def low(h):
            dve.wait_ge(sgy_hi_ready, h + 1)
            dve.tensor_tensor(sgy_lo[:, h, :], ug[:, h, :], f32(sgy_hi[:, h, :]), ALU.subtract).then_inc(sgy_lo_ready, 1)

        for u in range(KD + 2):
            if u < KD:
                dve.wait_ge(unit_used, U.base + u + 1)
                dve.tensor_tensor(ug[:, u, :], bank[u % 4][:], rstd[:], ALU.mult).then_inc(taken, 1)
            if u == 3:
                gate(0)
                gate(1)
            elif 4 <= u <= KD:
                gate(u - 2)
            elif u == KD + 1:
                gate(KD - 1)
            if 4 <= u <= KD:
                low(u - 4)
        for h in range(KD - 3, KD):
            low(h)

    def act_sgu(act):
        V, U = layers["sg_v"], layers["sg_u"]
        for b in range(V.bodies):
            act_bodies(act, V, only=b)
            for t in range(4):
                act.wait_ge(taken, V.rbase + 4 * b + t + 1)
                c = vt[:, t, b * T:(b + 1) * T]
                act.activation(c, c, ACT.Gelu_apprx_tanh).then_inc(v_gelu, 1)
                act.wait_ge(v_gelu, 4 * b + t + 1)
                act.wait_ge(v_sq, 4 * b + t)
                act.activation(sq[:, 0, :], c, ACT.Square, accum_out=vss[:, 0, 4 * b + t:4 * b + t + 1]).then_inc(v_sq, 1)

        def copies(h):
            act.wait_ge(yh_done, KD + h + 1)
            act.activation(sgy_hi[:, h, :], ug[:, h, :], ACT.Copy).then_inc(sgy_hi_ready, 1)

        def gelus(b, i):
            u = 4 * b + i
            if u >= 5:
                copies(u - 5)
            act.wait_ge(taken, U.rbase + u + 1)
            act.activation(ug[:, u, :], ug[:, u, :], ACT.Gelu_apprx_tanh).then_inc(u_gelu, 1)
        act.wait_ge(v_sum, 1)
        act.activation(vss[:, 2, 0:4], vss[:, 1, 0:4], ACT.Sqrt, bias=eps[:], scale=1.0 / D).then_inc(v_std, 1)
        act.preload_act_table(ACT.Gelu_apprx_tanh)
        for b in range(U.bodies):
            act_bodies(act, U, gelus, only=b)
        for h in range(KD - 5, KD):
            copies(h)

    SUM2 = gbuf

    def final_columns():
        return par[:, PARAMS["final_norm"]:PARAMS["final_norm"] + KD], par[:, PARAMS["norm_mix_2"]:PARAMS["norm_mix_2"] + KD]

    def dve_final(dve, L):
        g1, g2 = final_columns()
        dve.tensor_tensor(gain12[:], g1, g2, ALU.mult).then_inc(final_gain, 1)
        dve.memset(ss[:], 0.0).then_inc(ss_added, 1)
        dve.memset(SUM2[:], 0.0).then_inc(ss_added, 1)
        dve.wait_ge(final_gain, 1)
        added = (KD + 1) * FINAL + 2

        def body(b):
            for mm in range(4):
                m = b * 4 + mm
                dve.wait_ge(unit_used, b * L.per + (L.base + (mm + 1) * 3))
                dve.scalar_tensor_tensor(tile(x, m), bank[mm][:], 0.5, tile(x, m), ALU.mult, ALU.add).then_inc(taken, 1)
                dve.wait_ge(xg_hi_ready, m + (KD * FINAL + 1))
                dve.scalar_tensor_tensor(tile(xg_lo, m), tile(x, m), gain12[:, bass.ds(m, 1)], f32(tile(xg_hi, m)),
                                         ALU.mult, ALU.subtract).then_inc(xg_lo_ready, 1)
                dve.wait_ge(ss_added, m * 2 + added)
                dve.wait_ge(sq_ready, m * 2 + (KD * FINAL + 1))
                dve.tensor_tensor(ss[:], ss[:], sq[:, 0, :], ALU.add).then_inc(ss_added, 1)
                dve.wait_ge(sq_ready, m * 2 + (KD * FINAL + 2))
                dve.tensor_tensor(SUM2[:], SUM2[:], sq[:, 1, :], ALU.add).then_inc(ss_added, 1)
        each_body(dve, L.bodies, body)
        dve.wait_ge(ss_added, added + 2 * KD)
        dve.scalar_tensor_tensor(SUM2[:], ss[:], EPS, SUM2[:], ALU.mult, ALU.add).then_inc(final_sum, 1)
        dve_norm_rstd(dve, FINAL)
        dve_norm_columns(dve, 2)

    def act_final(act, L):
        act.wait_ge(final_gain, 1)

        def result(b, i):
            if i % 3 == 2:
                m = b * 4 + i // 3
                act.wait_ge(taken, m + (L.rbase + 1))
                act.activation(tile(xg_hi, m), tile(x, m), ACT.Copy, scale=gain12[:, bass.ds(m, 1)]).then_inc(xg_hi_ready, 1)
                act.wait_ge(ss_added, m * 2 + ((KD + 1) * FINAL + 2))
                act.activation(sq[:, 0, :], tile(x, m), ACT.Square).then_inc(sq_ready, 1)
                act.activation(sq[:, 1, :], tile(x, m), ACT.Square, scale=col("final_norm", m)).then_inc(sq_ready, 1)
        for b in range(L.bodies):
            act_bodies(act, L, result, only=b)
        act.wait_ge(ss_summed, FINAL + 1)
        act.activation(rstd[:], bank[4][:], ACT.Sqrt, bias=eps2[:], scale=1.0 / D).then_inc(std_ready, 1)
        act.wait_ge(col_summed, 2)
        act.activation(rcol[:], bank[5][:, 0:4], ACT.Sqrt, bias=eps2[:], scale=1.0 / D).then_inc(col_std, 1)
        act.wait_ge(ss_summed, FINAL + 2)
        act.activation(ss[:], bank[6][:], ACT.Sqrt, bias=eps[:], scale=1.0 / D).then_inc(std_ready, 1)

    def pe_final_sums(pe):
        pe.wait_ge(final_sum, 1)
        pe.matmul(bank[4][:], ones[:], SUM2[:], start=True, stop=True).then_inc(ss_summed, 1)
        pe_norm_columns(pe, SUM2)
        pe.matmul(bank[6][:], ones[:], ss[:], start=True, stop=True).then_inc(ss_summed, 1)

    def dve_final_x(dve):
        dve_norm_rstd_of(dve, ss, FINAL + 1)
        for m in range(KD):
            dve.scalar_tensor_tensor(x[:, m, :], x[:, m, :], col("final_norm", m), ss[:], ALU.mult, ALU.mult).then_inc(final_step, 1)

    def done(eng, ins, sem, n):
        ins.then_inc(sem, 1)
        eng.wait_ge(sem, n)

    def bcast(ap, n):
        return ap.unsqueeze(2).to_broadcast([ap.shape[0], ap.shape[1], n])

    MIX_LOADS = 10

    def act_load_mix(act):
        for dst, src in ((sel8[:].rearrange("p h t -> p (h t)"), "c_sel8"), (pack[:], "c_pack"),
                         (ff_w[:].rearrange("p k h -> p (k h)"), "ff_w"), (causal[:], "c_causal"), (ff_b[:], "ff_b"),
                         (spread[:], "c_spread"), (s5_b[:, 0].rearrange("p t h -> p (t h)"), "s5_b_re"),
                         (s5_b[:, 1].rearrange("p t h -> p (t h)"), "s5_b_im"),
                         (s5_c[:, 0].rearrange("p t h -> p (t h)"), "s5_c_re"),
                         (s5_c[:, 1].rearrange("p t h -> p (t h)"), "s5_c_im")):
            act.dma_start(dst, io[src]).then_inc(mix_in, 16)

    def pe_mix_a(pe):
        QK, V, S = layers["fox_qk"], layers["fox_v"], layers["s5_in"]
        pe_project(pe, QK, xg_hi, xg_lo, (xg_lo_ready, split_count(FINAL + 1)), norm=pe_final_sums)
        pe.wait_ge(mix_in, 16 * MIX_LOADS)
        for i in range(8):
            pe.wait_ge(qk_sq, i + 1)
            pe.matmul(bank[6][0:16, :], pack[:, 16 - 2 * i:32 - 2 * i], sq[:, i % 2, :],
                      start=i == 0, stop=i == 7).then_inc(qk_ss, 1)
        pe_project_tokens(pe, V, xg_hi, xg_lo)
        pe.wait_ge(ff_split, 2)
        for k in range(KD):
            pe.matmul(bank[5][0:8, :], ff_hi[:, k, :], xg_hi[:, k, :], start=k == 0, stop=False)
            pe.matmul(bank[5][0:8, :], ff_hi[:, k, :], xg_lo[:, k, :], start=False, stop=False)
            mm = pe.matmul(bank[5][0:8, :], ff_lo[:, k, :], xg_hi[:, k, :], start=False, stop=k == KD - 1)
        mm.then_inc(ff_mm, 1)
        for i in range(8):
            if i == 0:
                pe.wait_ge(qk_rstd, 1)
            if i >= 2:
                pe.wait_ge(qk_scaled, i - 1)
            pe.matmul(bank[6 + i % 2][:], spread[:, i * P:(i + 1) * P], qk_r[:], start=True, stop=True).then_inc(qk_spread, 1)
        pe_project(pe, S, xg_hi, xg_lo, None)
        pe.wait_ge(ident_in, 16)
        pe.wait_ge(s5_bx_ready, 4)
        pe.wait_ge(qk_scaled, 8)
        for c in range(2):
            for j in range(4):
                mm = pe.transpose(bank[6 + c][:, j * P:(j + 1) * P],
                                  s5_bx[:, c, 4 * j:4 * j + 4, :].rearrange("p t h -> p (t h)"), ident[:])
            mm.then_inc(s5_bt_mm, 1)

    def dve_mix_a(dve):
        QK, V, S = layers["fox_qk"], layers["fox_v"], layers["s5_in"]

        def qk_tiles(b):
            for mm in range(4):
                dve.wait_ge(unit_used, b * 4 + (QK.base + mm + 1))
                dve.tensor_tensor(tile(qk, b * 4 + mm), bank[mm][:], rstd[:], ALU.mult).then_inc(taken, 1)
        each_body(dve, QK.bodies, qk_tiles)
        dve.wait_ge(mix_in, 16 * MIX_LOADS)
        done(dve, dve.tensor_copy(ff_hi[:], ff_w[:]), ff_split, 1)
        dve.tensor_tensor(ff_lo[:], ff_w[:], f32(ff_hi[:]), ALU.subtract).then_inc(ff_split, 1)
        dve.tensor_copy(sel8_r[:], sel8[:]).then_inc(negc_step, 1)
        dve.tensor_copy(causal_r[:], causal[:]).then_inc(negc_step, 1)
        dve.wait_ge(ident_in, 16)
        dve.tensor_copy(ident_r[:], ident[:]).then_inc(negc_step, 1)
        dve_final_x(dve)
        dve.wait_ge(qk_std, 1)
        done(dve, dve.reciprocal(qk_r[:], qk_r[:]), qk_rstd, 1)
        for t in range(4):
            dve.wait_ge(unit_used, V.base + 4)
            dve.tensor_scalar(vtok[:, t, :], bank[t][:], rcol[:, t:t + 1], None, ALU.mult).then_inc(taken, 1)
        dve.wait_ge(ff_mm, 1)
        z, l = gbuf[0:8, :], ubuf[0:8, :]
        dve_chain(dve, dve.tensor_tensor(z, bank[5][0:8, :], rstd[0:8, :], ALU.mult))
        done(dve, dve.tensor_scalar(z, z, ff_b[:, 0:1], None, ALU.add), ff_z, 1)
        for i in range(8):
            dve.wait_ge(qk_spread, i + 1)
            dve.scalar_tensor_tensor(qk[:, i, :], qk[:, i, :], col("fox_qnorm_2" if i < 4 else "fox_knorm_2"),
                                     bank[6 + i % 2][:], ALU.mult, ALU.mult).then_inc(qk_scaled, 1)
        dve.wait_ge(ff_ln, 1)
        dve_chain(dve, dve.scalar_tensor_tensor(l, z, 0.0, l, ALU.min, ALU.subtract))
        dve_chain(dve, dve.tensor_scalar(l, l, -1.0, None, ALU.mult))
        done(dve, dve.tensor_tensor_scan(negc[:], ones[0:8, 0:1].to_broadcast([8, T]), l, 0.0, ALU.mult, ALU.add), negc_ready, 1)
        dve.tensor_copy(negc_hi[:], negc[:]).then_inc(negc_step, 1)
        dve.wait_ge(negc_step, 4)
        dve.tensor_tensor(negc_lo[:], negc[:], f32(negc_hi[:]), ALU.subtract).then_inc(negc_ready, 1)
        for m in range(4):
            dve.wait_ge(unit_used, S.base + m + 1)
            dve.tensor_tensor(su[:, m, :], bank[m][:], rstd[:], ALU.mult).then_inc(taken, 1)
        for c in range(2):
            dve.wait_ge(s5_bt_mm, c + 1)
            dve.tensor_copy(s5_bt[:, c].rearrange("p j t -> p (j t)"), bank[6 + c][:]).then_inc(s5_bt_ready, 1)

    def act_mix_a(act):
        QK, V, S = layers["fox_qk"], layers["fox_v"], layers["s5_in"]
        act_bodies(act, QK)
        for i in range(8):
            act.wait_ge(taken, QK.rbase + i + 1)
            if i >= 2:
                act.wait_ge(qk_ss, i - 1)
            act.activation(sq[:, i % 2, :], qk[:, i, :], ACT.Square).then_inc(qk_sq, 1)
        act.wait_ge(qk_ss, 8)
        act.activation(qk_r[:], bank[6][0:16, :], ACT.Sqrt, bias=eps[0:16, :], scale=1.0 / 64).then_inc(qk_std, 1)
        act_bodies(act, V)
        act.wait_ge(ff_z, 1)
        z, l = gbuf[0:8, :], ubuf[0:8, :]
        act_chain(act, act.activation(l, z, ACT.Abs))
        act_chain(act, act.activation(l, l, ACT.Exp, scale=-1.0))
        act.activation(l, l, ACT.Ln, bias=1.0).then_inc(ff_ln, 1)
        act_s5_weights(act)
        act_bodies(act, S)

    def s5v(i):
        return s5p[:, i, :]

    def parv(name):
        return par[:, PARAMS[name]:PARAMS[name] + 16]

    def dve_s5_angles(dve):
        are, aim = parv("s5_a_re_2"), parv("s5_a_im_2")
        dve.wait_ge(s5_act, 1)
        done(dve, dve.tensor_tensor(s5v(1), s5v(0), aim, ALU.mult), s5_dve, 1)
        done(dve, dve.tensor_tensor(s5v(2), s5v(0), are, ALU.mult), s5_dve, 2)
        dve_chain(dve, dve.tensor_scalar(s5v(4), s5v(1), 1.0 / (2 * np.pi), ROUND, ALU.mult, ALU.add))
        dve_chain(dve, dve.tensor_scalar(s5v(4), s5v(4), ROUND, None, ALU.subtract))
        dve_chain(dve, dve.scalar_tensor_tensor(s5v(5), s5v(4), -TWO_PI[0], s5v(1), ALU.mult, ALU.add))
        dve_chain(dve, dve.scalar_tensor_tensor(s5v(5), s5v(4), -TWO_PI[1], s5v(5), ALU.mult, ALU.add))
        dve_chain(dve, dve.scalar_tensor_tensor(s5v(5), s5v(4), -TWO_PI[2], s5v(5), ALU.mult, ALU.add))
        done(dve, dve.tensor_scalar(s5v(5), s5v(5), PI_BELOW, -PI_BELOW, ALU.min, ALU.max), s5_dve, 3)
        dve_chain(dve, dve.tensor_scalar(s5v(6), s5v(5), 1.0 / (2 * np.pi), None, ALU.mult))

    def act_s5_coefficients(act):
        act.wait_ge(s5_dve, 3)
        act.activation(s5v(3), s5v(2), ACT.Exp).then_inc(s5_act, 1)
        act.activation(s5v(7), s5v(5), ACT.Sin).then_inc(s5_act, 1)
        act.activation(s5v(8), s5v(5), ACT.Sin, scale=0.5).then_inc(s5_act, 1)

    def dve_s5_coefficients(dve):
        are, aim = parv("s5_a_re_2"), parv("s5_a_im_2")

        def op(out, a, b, alu):
            dve_chain(dve, dve.tensor_tensor(out, a, b, alu))
        dve.wait_ge(s5_act, 4)
        op(s5v(9), s5v(8), s5v(8), ALU.mult)
        dve_chain(dve, dve.tensor_scalar(s5v(9), s5v(9), -2.0, 1.0, ALU.mult, ALU.add))
        op(s5v(10), s5v(3), s5v(9), ALU.mult)
        op(s5v(11), s5v(3), s5v(7), ALU.mult)
        dve_chain(dve, dve.tensor_scalar(s5v(10), s5v(10), 1.0, None, ALU.subtract))
        op(s5v(12), are, are, ALU.mult)
        op(s5v(13), aim, aim, ALU.mult)
        op(s5v(12), s5v(12), s5v(13), ALU.add)
        dve_chain(dve, dve.reciprocal(s5v(12), s5v(12)))
        op(s5v(13), s5v(10), are, ALU.mult)
        op(s5v(14), s5v(11), aim, ALU.mult)
        op(s5v(13), s5v(13), s5v(14), ALU.add)
        op(s5v(13), s5v(13), s5v(12), ALU.mult)
        op(s5v(14), s5v(11), are, ALU.mult)
        op(s5v(15), s5v(10), aim, ALU.mult)
        op(s5v(14), s5v(14), s5v(15), ALU.subtract)
        done(dve, dve.tensor_tensor(s5v(14), s5v(14), s5v(12), ALU.mult), s5_dve, 4)

    group_halves = (slice(0, 64), slice(0, 16)), (slice(64, 128), slice(16, 32))

    def pool_s5_weights(pool):
        pool.wait_ge(mix_in, 16 * MIX_LOADS)
        pool.memset(s5_bx[:], 0.0).then_inc(s5_zero, 1)
        pool.memset(s5_cx[:], 0.0).then_inc(s5_zero, 1)
        pool.wait_ge(s5_dve, 4)
        cr, ci = bcast(s5v(13), 16), bcast(s5v(14), 16)
        for c, (a0, a1, alu) in enumerate(((cr, ci, ALU.subtract), (ci, cr, ALU.add))):
            pool.tensor_tensor(s5_t[:, c, 0], s5_b[:, 0], a0, ALU.mult).then_inc(s5_bprod, 1)
            pool.tensor_tensor(s5_t[:, c, 1], s5_b[:, 1], a1, ALU.mult).then_inc(s5_bprod, 1)
            pool.wait_ge(s5_bprod, 2 * c + 2)
            pool.tensor_tensor(s5_t[:, c, 0], s5_t[:, c, 0], s5_t[:, c, 1], alu).then_inc(s5_bbar, 1)

    def act_s5_weights(act):
        act.wait_ge(s5_zero, 2)
        for p, h in group_halves:
            act.activation(s5_cx[p, 0, :, h], s5_c[p, 0], ACT.Copy).then_inc(s5_cx_ready, 1)
            act.activation(s5_cx[p, 1, :, h], s5_c[p, 1], ACT.Copy, scale=-1.0).then_inc(s5_cx_ready, 1)
        for c in range(2):
            act.wait_ge(s5_bbar, c + 1)
            for p, h in group_halves:
                act.activation(s5_bx[p, c, :, h], s5_t[p, c, 0], ACT.Copy).then_inc(s5_bx_ready, 1)

    FOX_STEPS = 32
    fox_tr, fox_o = (bank[6], bank[0]), (bank[7], bank[3])

    def fox_keys(n):
        return (n % 4 + 1) * P

    def pe_fox(pe):
        pe.wait_ge(negc_ready, 2)
        pe.wait_ge(qk_scaled, 8)
        pe.wait_ge(taken, layers["s5_in"].rbase + 4)
        pe.wait_ge(s5_bt_ready, 2)

        def scores(n):
            h, qi, keys = n // 4, n % 4, fox_keys(n)
            o, out = 64 * (h % 2), bank[4 + n % 2]
            if n >= 2:
                pe.wait_ge(att_exp, n - 1)
            pe.matmul(out[:, 0:keys], qk[o:o + 64, h // 2, qi * P:keys], qk[o:o + 64, 4 + h // 2, 0:keys],
                      start=True, stop=False)
            pe.matmul(out[:, 0:keys], sel8_r[:, h, :], negc_hi[:, 0:keys], start=False, stop=False)
            pe.matmul(out[:, 0:keys], sel8_r[:, h, :], negc_lo[:, 0:keys], start=False, stop=False)
            pe.matmul(out[:, qi * P:keys], ident_r[:], causal_r[:], start=False, stop=True).then_inc(att_s, 1)

        def transposes(n):
            pe.wait_ge(att_p, n + 1)
            if n >= 2:
                pe.wait_ge(att_tc, n - 1)
            for kb in range(n % 4 + 1):
                mm = pe.transpose(fox_tr[n % 2][:, kb * P:(kb + 1) * P], prob[:, n % 3, kb * P:(kb + 1) * P], ident[:])
            mm.then_inc(att_t, 1)

        def outputs(n):
            h, qi, pair = n // 4, n % 4, n // 8
            if n % 8 == 0 and pair >= 2:
                pe.wait_ge(fox_lo, pair - 1)
            pe.wait_ge(att_tc, n + 1)
            o = 64 * (h % 2)
            for kb in range(qi + 1):
                mm = pe.matmul(fox_o[pair % 2][o:o + 64, qi * P:(qi + 1) * P], vtok[:, kb, h * 64:(h + 1) * 64],
                               probT[:, n % 2, kb * P:(kb + 1) * P], start=kb == 0, stop=kb == qi)
            mm.then_inc(att_o, 1)

        for n in range(FOX_STEPS + 3):
            if n < FOX_STEPS:
                scores(n)
            if 0 <= n - 2 < FOX_STEPS:
                transposes(n - 2)
            if n >= 3:
                outputs(n - 3)

    def dve_fox(dve):
        def row_max(n):
            dve.wait_ge(att_s, n + 1)
            dve_chain(dve, dve.reduce_max(att_m[:, n:n + 1], bank[4 + n % 2][:, 0:fox_keys(n)], AX.X, negate=True))
            dve.tensor_scalar(att_m[:, n:n + 1], att_m[:, n:n + 1], 0.125, None, ALU.mult).then_inc(att_nmax, 1)

        def scale(n):
            p = prob[:, n % 3, 0:fox_keys(n)]
            dve.wait_ge(att_exp, n + 1)
            dve_chain(dve, dve.reciprocal(att_l[:, n:n + 1], att_l[:, n:n + 1]))
            dve.tensor_scalar(p, p, att_l[:, n:n + 1], None, ALU.mult).then_inc(att_p, 1)

        for n in range(FOX_STEPS + 5):
            if n < FOX_STEPS:
                row_max(n)
            if 0 <= n - 1 < FOX_STEPS:
                scale(n - 1)
            if n >= 12 and (n - 4) % 8 == 0:
                i = (n - 4) // 8 - 1
                dve.wait_ge(fox_hi, i + 1)
                dve.tensor_tensor(y0_lo[:, i, :], fox_o[i % 2][:], f32(y0_hi[:, i, :]), ALU.subtract).then_inc(fox_lo, 1)

    def act_fox(act):
        act.wait_ge(s5_bx_ready, 4)
        act.dma_start(levels_f[:], io["c_levels"]).then_inc(levels_in, 16)

        def exps(n):
            keys = fox_keys(n)
            act.wait_ge(att_nmax, n + 1)
            if n >= 3:
                act.wait_ge(att_t, n - 2)
            act.activation(prob[:, n % 3, 0:keys], bank[4 + n % 2][:, 0:keys], ACT.Exp, bias=att_m[:, n:n + 1],
                           scale=0.125, accum_out=att_l[:, n:n + 1]).then_inc(att_exp, 1)

        def copies(n):
            keys = fox_keys(n)
            act.wait_ge(att_t, n + 1)
            if n >= 2:
                act.wait_ge(att_o, n - 1)
            act.activation(probT[:, n % 2, 0:keys], fox_tr[n % 2][:, 0:keys], ACT.Copy).then_inc(att_tc, 1)

        for n in range(FOX_STEPS + 5):
            if n < FOX_STEPS:
                exps(n)
            if 0 <= n - 2 < FOX_STEPS:
                copies(n - 2)
            if n >= 12 and (n - 4) % 8 == 0:
                i = (n - 4) // 8 - 1
                act.wait_ge(att_o, 8 * (i + 1))
                act.activation(y0_hi[:, i, :], fox_o[i % 2][:], ACT.Copy).then_inc(fox_hi, 1)

    def pe_s5(pe):
        QFG, V = layers["hg_qfg"], layers["hg_v"]

        def outputs(t):
            j = 32 * (t % 4)
            out = bank[6 + (t // 4) % 2][j:j + 32, :]
            if t >= 8 and t % 4 == 0:
                pe.wait_ge(s5_y, t // 4 - 1)
            for n, (c, ready, count, product) in enumerate((
                    (0, s5_nprod, t + 1, ubuf[:]), (0, s5_prod, 3 * t + 1, gbuf[:]),
                    (1, s5_prod, 3 * t + 2, sq[:, 0, :]), (1, s5_prod, 3 * t + 3, sq[:, 1, :]))):
                pe.wait_ge(ready, count)
                mm = pe.matmul(out, s5_cx[:, c, t, :], product, start=n == 0, stop=n == 3)
            mm.then_inc(s5_ymm, 1)

        for u in range(16):
            L = QFG if u < 12 else V
            i = u - (0 if u < 12 else 12)
            if u == 3:
                pe.wait_ge(fox_lo, 4)
            if u < 12:
                project_unit(pe, L, i // 4, i % 4, xg_hi, xg_lo)
            else:
                pe_tokens_unit(pe, L, 0, i, xg_hi, xg_lo)
            t, j = u, 32 * (u % 4)
            if t >= 1:
                pe.wait_ge(s5_step, 6 * t - 2)
            if t == 0:
                pe.wait_ge(s5_bt_ready, 2)
                pe.wait_ge(s5_cx_ready, 4)
                pe.wait_ge(taken, layers["s5_in"].rbase + 4)
            for c in range(2):
                mm = pe.matmul(bank[4 + c][:], s5_bt[j:j + 32, c, t // 4, :], su[j:j + 32, t // 4, :], start=True, stop=True)
            mm.then_inc(s5_drive, 1)
            if t >= 1:
                outputs(t - 1)
        pe_merge_gate(pe, 0, 2, 0)
        outputs(15)

    def s5_state(t):
        sin, cos = rot[:, t % 2, 0, :], rot[:, t % 2, 1, :]
        return sin, cos, s5_g[t % 2][:, 0, :], s5_g[t % 2][:, 1, :]

    def pool_s5(pool):
        QFG, V = layers["hg_qfg"], layers["hg_v"]

        def split(u):
            split_lo_unit(pool, *((QFG, u // 4, u % 4) if u < 12 else (V, 0, u - 12) if u < 16 else (layers["merge01"], 0, u - 16)))
        split(0)
        split(1)
        for t in range(16):
            sin, cos, gr, gi = s5_state(t)
            split(t + 2)
            pool.wait_ge(s5_step, 6 * t + 5)
            if t:
                pool.wait_ge(s5_ymm, t)
            pool.tensor_tensor(gbuf[:], gr, cos, ALU.mult).then_inc(s5_prod, 1)
            pool.tensor_tensor(sq[:, 0, :], gr, sin, ALU.mult).then_inc(s5_prod, 1)
            pool.wait_ge(s5_step, 6 * t + 6)
            pool.tensor_tensor(sq[:, 1, :], gi, cos, ALU.mult).then_inc(s5_prod, 1)
        for i in range(2, layers["merge01"].n):
            split_lo_unit(pool, layers["merge01"], 0, i)

    def dve_s5(dve):
        QFG, V = layers["hg_qfg"], layers["hg_v"]

        def turns(t):
            tok = s5p[:, 6, t:t + 1]
            if t >= 1:
                dve.wait_ge(s5_rot, 4 * (t - 1) + 2)
            dve_chain(dve, dve.tensor_scalar(turn[:], iota[:], tok, ROUND, ALU.mult, ALU.add))
            dve_chain(dve, dve.tensor_scalar(turn[:], turn[:], ROUND, None, ALU.subtract))
            dve.scalar_tensor_tensor(turn[:], iota[:], tok, turn[:], ALU.mult, ALU.subtract).then_inc(s5_turn, 1)

        dve.wait_ge(iota_in, 16)
        turns(0)
        for t in range(16):
            if t < 12:
                dve.wait_ge(unit_used, QFG.base + t + 1)
                dve.tensor_tensor(hq[:, QFG_TILE[t], :], bank[t % 4][:], rstd[:], ALU.mult).then_inc(taken, 1)
            if t == 1:
                dve.wait_ge(levels_ready, 1)
            if t == 15:
                dve.wait_ge(hg_cum, 4 * HEADS)
                dve.wait_ge(s5_prod, 3 * t)
                dve.wait_ge(s5_nprod, t)
                for n in range(4):
                    dve.wait_ge(unit_used, V.base + 4)
                    dve.tensor_scalar(hv[:, n, :], bank[n][:], rcol[:, n:n + 1], None, ALU.mult).then_inc(taken, 1)
            sin, cos, gr, gi = s5_state(t)
            dr, di, m0, m1 = bank[4][:], bank[5][:], s5_m[:, 0, :], s5_m[:, 1, :]
            n0 = 6 * t
            dve.wait_ge(s5_rot, 4 * t + 4)
            if t >= 2:
                dve.wait_ge(s5_prod, 3 * t - 3)
                dve.wait_ge(s5_nprod, t - 1)
            dve.wait_ge(s5_drive, t + 1)
            dve.tensor_tensor(m0, dr, cos, ALU.mult).then_inc(s5_step, 1)
            dve.tensor_tensor(m1, di, sin, ALU.mult).then_inc(s5_step, 1)
            dve.tensor_tensor(gi, di, cos, ALU.mult).then_inc(s5_step, 1)
            dve.tensor_tensor(gr, dr, sin, ALU.mult).then_inc(s5_step, 1)
            dve.wait_ge(s5_step, n0 + 2)
            dve_chain(dve, dve.tensor_tensor(m0, m0, m1, ALU.add))
            dve.wait_ge(s5_step, n0 + 4)
            dve_chain(dve, dve.tensor_tensor(m1, gi, gr, ALU.subtract))
            mag = s5p[:, 3, t:t + 1].to_broadcast([P, T])
            dve.tensor_tensor_scan(gr, mag, m0, 0.0, ALU.mult, ALU.add).then_inc(s5_step, 1)
            dve.tensor_tensor_scan(gi, mag, m1, 0.0, ALU.mult, ALU.add).then_inc(s5_step, 1)
            if t < 15:
                turns(t + 1)
            if t >= 1:
                dve.wait_ge(s5_ymm, t)
            dve.wait_ge(s5_step, n0 + 6)
            dve.scalar_tensor_tensor(ubuf[:], gi, -1.0, sin, ALU.mult, ALU.mult).then_inc(s5_nprod, 1)
            if t % 4 == 0 and t:
                s5_result(dve, t // 4 - 1)
            if 5 <= t < 13:
                dve_hg_forget(dve, (t - 5) // 2, (t - 5) % 2)
        s5_result(dve, 3)
        dve.memset(hsc, 0.0).then_inc(hg_zero, 1)

    def s5_result(dve, i):
        dve.wait_ge(s5_ymm, 4 * i + 4)
        dve.scalar_tensor_tensor(su[:, i, :], su[:, i, :], col("s5_d_2", i), bank[6 + i % 2][:],
                                 ALU.mult, ALU.add).then_inc(s5_y, 1)

    def act_s5(act):
        QFG, V = layers["hg_qfg"], layers["hg_v"]
        act.dma_start(iota[:], io["c_iota"]).then_inc(iota_in, 16)
        act.wait_ge(levels_in, 16)
        act.activation(hm[:].rearrange("p l t -> p (l t)"), levels_f[:], ACT.Copy).then_inc(levels_ready, 1)
        act.preload_act_table(ACT.Sin)

        def rots(t):
            act.wait_ge(s5_turn, t + 1)
            if t >= 2:
                act.wait_ge(s5_prod, 3 * (t - 1))
                act.wait_ge(s5_nprod, t - 1)
            sin, cos = rot[:, t % 2, 0, :], rot[:, t % 2, 1, :]
            act.activation(sin, turn[:], ACT.Sin, scale=TURN).then_inc(s5_rot, 1)
            act.activation(cos, turn[:], ACT.Sin, scale=TURN / 2).then_inc(s5_rot, 1)
            act.wait_ge(s5_rot, 4 * t + 2)
            act.activation(cos, cos, ACT.Square).then_inc(s5_rot, 1)
            act.wait_ge(s5_rot, 4 * t + 3)
            act.activation(cos, cos, ACT.Copy, scale=-2.0, bias=1.0).then_inc(s5_rot, 1)

        rots(0)

        def work(b, i):
            u = 4 * b + i
            if u < 15:
                rots(u + 1)
            if u in (4, 6, 8, 10):
                act_hg_forget(act, (u - 4) // 2)
            elif u in (5, 7, 9, 11):
                act_hg_silu(act, (u - 5) // 2)
            elif u >= 12:
                act_hg_silu(act, 8 + u - 12)
            if 4 <= u < 14:
                act.preload_act_table(ACT.Sin)
        for b in range(3):
            act_bodies(act, QFG, work, only=b)
        act_bodies(act, V, lambda b, i: work(3, i), only=0)
        for i in range(4):
            act.wait_ge(s5_y, i + 1)
            act.activation(su[:, i, :], su[:, i, :], ACT.Gelu_apprx_tanh).then_inc(z_ready, 1)
        for i in range(4):
            act.wait_ge(z_ready, i + 1)
            act.activation(y1_hi[:, i, :], su[:, i, :], ACT.Copy).then_inc(z_hi_ready, 1)

    def dve_z(dve):
        for i in range(4):
            dve.wait_ge(z_hi_ready, i + 1)
            dve.tensor_tensor(y1_lo[:, i, :], su[:, i, :], f32(y1_hi[:, i, :]), ALU.subtract).then_inc(z_lo_ready, 1)

    GLU_UNIT, GLU_RESULT = 6, 8

    def triple(b, p):
        if b == 2:
            return layers["merge2"], 3 * p, 4 * p, 8 + p
        n = (p - 2) % 4 if b == 0 else 4 + p
        after_glu = n >= 2
        return layers["merge01"], 3 * n + 4 * after_glu, 4 * n + 4 * after_glu, n

    def merge_y(b):
        return ((y0_hi, y0_lo, fox_lo), (y1_hi, y1_lo, s5_lo), (y0_hi, y0_lo, hg_lo))[b]

    def pe_merge_gate(pe, b, p, i):
        L, u, r, _ = triple(b, p)
        pe.wait_ge(w_lo_ready, L.base + u + i + 1)
        pe.wait_ge(taken, L.rbase + r + i + 1 - RING)
        for k in range(KD):
            mm = three_passes(pe, bank[i][:], (u + i) % RING, k, xg_hi[:, k, :], xg_lo[:, k, :], k == 0, k == KD - 1)
        mm.then_inc(unit_used, 1)

    def pe_merge_branch(pe, b, p):
        L, u, r, _ = triple(b, p)
        y_hi, y_lo, ready = merge_y(b)
        pe.wait_ge(w_lo_ready, L.base + u + 3)
        pe.wait_ge(ready, 4)
        for i in range(2):
            pe.wait_ge(taken, L.rbase + r + 3 + i - RING)
            for k in range(4):
                mm = three_passes(pe, bank[2 + i][:], (u + 2) % RING, 4 * i + k, y_hi[:, k, :], y_lo[:, k, :], k == 0, k == 3)
        mm.then_inc(unit_used, 1)

    def dve_merge_gate(dve, b, p, i):
        L, u, r, _ = triple(b, p)
        if i == 0:
            dve.wait_ge(taken, L.rbase + r)
            if b:
                dve.wait_ge(merge_step, 2 * (4 * (b - 1) + p))
        dve.wait_ge(unit_used, L.base + u + i + 1)
        dve.tensor_tensor(gate_buf[i][:], bank[i][:], rstd[:], ALU.mult).then_inc(taken, 1)

    def dve_merge_branch(dve, b, p):
        L, u, r, n = triple(b, p)
        dve.wait_ge(unit_used, L.base + u + 3)
        for i in range(2):
            m = 2 * p + i
            dve.wait_ge(gate_tanh, 2 * n + i + 1)
            dst = merged[:, m, :] if b == 0 else gate_buf[i][:]
            dve.scalar_tensor_tensor(dst, gate_buf[i][:], 1.0, bank[2 + i][:], ALU.add, ALU.mult).then_inc(taken, 1)
            if b:
                dve.wait_ge(taken, L.rbase + r + 3 + i)
                dve.tensor_tensor(merged[:, m, :], merged[:, m, :], gate_buf[i][:], ALU.add).then_inc(merge_step, 1)

    def act_merge_split(act, b, p, i):
        L, u, r, _ = triple(b, p)
        split_hi(act, L, 0, u + i + AHEAD)

    def act_merge_gate(act, b, p, i):
        L, u, r, _ = triple(b, p)
        act.wait_ge(taken, L.rbase + r + i + 1)
        act.activation(gate_buf[i][:], gate_buf[i][:], ACT.Tanh, scale=0.5).then_inc(gate_tanh, 1)

    def pe_triple(pe, b, p):
        pe_merge_gate(pe, b, p, 0)
        pe_merge_gate(pe, b, p, 1)
        pe_merge_branch(pe, b, p)

    def dve_triple(dve, b, p):
        dve_merge_gate(dve, b, p, 0)
        dve_merge_gate(dve, b, p, 1)
        dve_merge_branch(dve, b, p)

    def act_triple(act, b, p):
        for i in range(3):
            act_merge_split(act, b, p, i)
            if i < 2:
                act_merge_gate(act, b, p, i)

    def pe_glu(pe):
        L = layers["merge01"]
        for i in range(4):
            u = GLU_UNIT + i
            pe.wait_ge(w_lo_ready, L.base + u + 1)
            pe.wait_ge(taken, L.rbase + GLU_RESULT + i + 1 - RING)
            for k in range(4):
                if i == 0:
                    pe.wait_ge(z_lo_ready, k + 1)
                mm = three_passes(pe, bank[i][:], u % RING, k, y1_hi[:, k, :], y1_lo[:, k, :], k == 0, k == 3)
            mm.then_inc(unit_used, 1)

    def dve_glu(dve):
        L = layers["merge01"]
        dve.wait_ge(taken, L.rbase + GLU_RESULT)
        for i in range(4):
            buf = gate_buf[i % 2][:]
            dve.wait_ge(unit_used, L.base + GLU_UNIT + i + 1)
            if i >= 2:
                dve.wait_ge(glu_out, i - 1)
            done(dve, dve.tensor_copy(buf, bank[i][:]), taken, L.rbase + GLU_RESULT + i + 1)
            dve.wait_ge(glu_sig, i + 1)
            dve.tensor_tensor(su[:, i, :], su[:, i, :], buf, ALU.mult).then_inc(glu_out, 1)
        for i in range(4):
            dve.wait_ge(s5_hi, i + 1)
            dve.tensor_tensor(y1_lo[:, i, :], su[:, i, :], f32(y1_hi[:, i, :]), ALU.subtract).then_inc(s5_lo, 1)

    def act_glu(act):
        L = layers["merge01"]
        for i in range(4):
            split_hi(act, L, 0, GLU_UNIT + i + AHEAD)
            act.wait_ge(taken, L.rbase + GLU_RESULT + i + 1)
            buf = gate_buf[i % 2][:]
            act.activation(buf, buf, ACT.Sigmoid, bias=col("s5_b_glu_2", i)).then_inc(glu_sig, 1)
        act.wait_ge(unit_used, L.base + GLU_UNIT + 4)
        for i in range(4):
            act.wait_ge(glu_out, i + 1)
            act.activation(y1_hi[:, i, :], su[:, i, :], ACT.Copy).then_inc(s5_hi, 1)

    m_hi = place("m_hi", [P, KD, T], F32R, at=work)
    m_lo = place("m_lo", [P, KD, T], F32R, at=work + 16 * KB)

    def act_load_mem(act):
        act.wait_ge(hg_lo, 4)
        for k in range(KD):
            act.dma_start(memx[:, k, :], io["memT"][k * P:(k + 1) * P, :]).then_inc(mem_in, 16)

    def act_mem_split(act):
        act.wait_ge(mem_in, 16 * KD)
        for k in range(KD):
            act.activation(msq[:, k, :], memx[:, k, :], ACT.Square).then_inc(mem_sq, 1)
            act.activation(mem_hi[:, k, :], memx[:, k, :], ACT.Copy, scale=col("norm_mem_2", k)).then_inc(mem_hi_ready, 1)

    def act_mem_std(act):
        act.wait_ge(mem_ss, 1)
        act.activation(rstd_m[:], bank[4][:, 0:NMEM], ACT.Sqrt, bias=eps[:], scale=1.0 / D).then_inc(mem_std, 1)
        act.wait_ge(mem_ss, 2)
        act.activation(rcol_m[:], bank[5][:, 0:2], ACT.Sqrt, bias=eps[:], scale=1.0 / D).then_inc(mem_std, 1)

    def dve_mem_split(dve):
        for k in range(KD):
            dve.wait_ge(mem_hi_ready, k + 1)
            dve.scalar_tensor_tensor(mem_lo[:, k, :], memx[:, k, :], col("norm_mem_2", k), f32(mem_hi[:, k, :]),
                                     ALU.mult, ALU.subtract).then_inc(mem_lo_ready, 1)

    def dve_mem_rstd(dve):
        dve.wait_ge(mem_std, 1)
        dve.reciprocal(rstd_m[:], rstd_m[:]).then_inc(mem_rstd, 1)
        dve.wait_ge(mem_std, 2)
        dve.reciprocal(rcol_m[:], rcol_m[:]).then_inc(mem_rstd, 1)
        dve.wait_ge(mem_rstd, 2)

    def pe_mem(pe):
        pe.wait_ge(mem_sq, KD)
        for k in range(KD):
            mm = pe.matmul(bank[4][:, 0:NMEM], ones[:], msq[:, k, :], start=k == 0, stop=k == KD - 1)
        mm.then_inc(mem_ss, 1)
        for t in range(2):
            for k in range(KD):
                mm = pe.matmul(bank[5][:, t:t + 1], msq[:, k, t * P:(t + 1) * P], ones[:, 0:1], start=k == 0, stop=k == KD - 1)
        mm.then_inc(mem_ss, 1)

    def pe_e(pe):
        K, V, O = layers["xk"], layers["xv"], layers["w_out"]
        pe_merge_branch(pe, 2, 0)
        pe_triple(pe, 2, 1)
        pe_triple(pe, 2, 2)
        pe_triple(pe, 2, 3)
        pe_mem(pe)
        pe_project(pe, K, mem_hi, mem_lo, (mem_lo_ready, 0), width=NMEM)
        for u in range(V.n):
            pe_tokens_unit(pe, V, u // 4, u % 4, mem_hi, mem_lo, 2)
            pe_key_square(pe, u)
        pe_project(pe, O, m_hi, m_lo, (m_lo_ready, 0))

    def dve_e(dve):
        K, V, O = layers["xk"], layers["xv"], layers["w_out"]
        dve_merge_branch(dve, 2, 0)
        dve_triple(dve, 2, 1)
        dve_triple(dve, 2, 2)
        dve_mem_split(dve)
        dve_triple(dve, 2, 3)
        dve_mem_rstd(dve)

        def k_tiles(b):
            for mm in range(4):
                m = b * 4 + mm
                dve.wait_ge(unit_used, b * 4 + (K.base + mm + 1))
                dve.tensor_tensor(kx[:, bass.ds(m, 1), :], bank[mm][:, 0:NMEM].unsqueeze(1), rstd_m[:].unsqueeze(1),
                                  ALU.mult).then_inc(taken, 1)
        dve_gain_kq(dve)
        each_body(dve, K.bodies, k_tiles)
        for m in range(KD):
            dve.wait_ge(m_hi_ready, m + 1)
            dve.scalar_tensor_tensor(m_lo[:, m, :], merged[:, m, :], 0.5, f32(m_hi[:, m, :]), ALU.mult, ALU.subtract).then_inc(m_lo_ready, 1)

        def v_tiles(b):
            for t in range(2):
                dve.wait_ge(unit_used, b * 4 + (V.base + 4))
                dve.tensor_scalar(vx[:, t, b * T:(b + 1) * T], bank[2 * b + t][:], rcol_m[:, t:t + 1], None, ALU.mult).then_inc(taken, 1)
        for b in range(V.bodies):
            v_tiles(b)
            for h in (2 * b, 2 * b + 1):
                dve_key_scale(dve, h)

    def act_e(act):
        K, V = layers["xk"], layers["xv"]
        act_load_mem(act)
        act_triple(act, 2, 1)
        act_mem_split(act)
        act_triple(act, 2, 2)
        act_triple(act, 2, 3)
        act_mem_std(act)
        for m in range(KD):
            act.wait_ge(merge_step, KD + m + 1)
            if m == 0:
                act.wait_ge(unit_used, layers["merge2"].base + 12)
            act.activation(m_hi[:, m, :], merged[:, m, :], ACT.Copy, scale=0.5).then_inc(m_hi_ready, 1)
        act_bodies(act, K)

        def squares(b, i):
            u = 4 * b + i
            act_head_square(act, "k", u)
            if u and u % 2 == 0:
                act_key_std(act, u // 2 - 1)
        for b in range(V.bodies):
            act_bodies(act, V, squares, only=b)
        act_key_std(act, 3)

    def dve_gain_kq(dve):
        q, k = (par[:, PARAMS[n]:PARAMS[n] + 2] for n in ("x_qnorm_2", "x_knorm_2"))
        dve_chain(dve, dve.tensor_tensor(gain_kq[:], q, k, ALU.mult))
        dve_chain(dve, dve.memset(eps256[:], 256 * EPS))

    def act_head_square(act, which, i):
        t, n, before = (kx, NMEM, 0) if which == "k" else (qx, T, 2 * X_HEADS)
        L = layers["xk" if which == "k" else "xq"]
        s = before + i
        act.wait_ge(taken, L.rbase + i + 1)
        if s >= 2:
            act.wait_ge(xn_ss, s - 1)
        act.activation(sq[:, i % 2, 0:n], t[:, i, :], ACT.Square).then_inc(xn_sq, 1)

    def key_norm(h):
        return bank[6 + h % 2][:, 0:NMEM], gate_buf[h % 2][:, 0:NMEM]

    def pe_key_square(pe, i):
        if i % 2 == 0 and i >= 4:
            pe.wait_ge(xn_std, i // 2 - 1)
        pe.wait_ge(xn_sq, i + 1)
        pe.matmul(key_norm(i // 2)[0], ones[:], sq[:, i % 2, 0:NMEM], start=i % 2 == 0, stop=i % 2 == 1).then_inc(xn_ss, 1)

    def act_key_std(act, h):
        total, rms = key_norm(h)
        act.wait_ge(xn_ss, 2 * h + 2)
        if h >= 2:
            act.wait_ge(xn_scaled, 2 * (h - 1))
        act.activation(rms, total, ACT.Sqrt, bias=eps[:], scale=1.0 / (2 * P)).then_inc(xn_std, 1)

    def dve_key_scale(dve, h):
        rms = key_norm(h)[1]
        dve.wait_ge(xn_std, h + 1)
        dve_chain(dve, dve.reciprocal(rms, rms))
        for i in range(2):
            m = 2 * h + i
            dve.scalar_tensor_tensor(kx[:, m, :], kx[:, m, :], gain_kq[:, i:i + 1], rms, ALU.mult, ALU.mult).then_inc(xn_scaled, 1)

    def query_cols(h):
        return slice(4 * h, 4 * h + 4)

    def pe_query_squares(pe, h):
        if h == 0:
            pe.wait_ge(xn_std, X_HEADS)
        pe.wait_ge(xn_sq, 2 * (X_HEADS + h + 1))
        for t in range(4):
            for i in range(2):
                mm = pe.matmul(bank[7][:, 4 * h + t:4 * h + t + 1], sq[:, i, t * P:(t + 1) * P], ones[:, 0:1],
                               start=i == 0, stop=i == 1)
                if t == 3:
                    mm.then_inc(xn_ss, 1)

    def act_query_std(act, h):
        act.wait_ge(xn_ss, 2 * (X_HEADS + h + 1))
        act.activation(xa_r[:, query_cols(h)], bank[7][:, query_cols(h)], ACT.Sqrt, bias=eps256[:]).then_inc(xn_std, 1)

    def dve_query_rms(dve, h):
        dve.wait_ge(xn_std, X_HEADS + h + 1)
        dve_chain(dve, dve.reciprocal(xa_r[:, query_cols(h)], xa_r[:, query_cols(h)]))

    X_HEADS = 4
    X_STEPS = 4 * X_HEADS
    X_SLOTS = X_STEPS + 6

    def cross_unit(n):
        return 4 + n // 2 if n % 2 == 0 and n < 8 else None

    def cross_norm(n):
        return n // 4 + 1 if n % 4 == 1 and n < 12 else None

    def cross_out(n):
        return (n - 5) // 4 if n >= 5 and (n - 5) % 4 == 0 else None

    def pe_cross(pe):
        Q, O = layers["xq"], layers["xo"]

        def scores(n):
            h, qi = n // 4, n % 4
            if n >= 2:
                pe.wait_ge(att_exp, FOX_STEPS + n - 1)
            if n == 0:
                pe.wait_ge(xn_scaled, 2 * X_HEADS)
            pe.wait_ge(taken, Q.rbase + 2 * h + 2)
            for i in range(2):
                mm = pe.matmul(bank[4 + n % 2][:, 0:NMEM], qx[:, 2 * h + i, qi * P:(qi + 1) * P], kx[:, 2 * h + i, :],
                               start=i == 0, stop=i == 1)
            mm.then_inc(att_s, 1)

        def transposes(n):
            pe.wait_ge(att_p, FOX_STEPS + n + 1)
            pe.wait_ge(att_tc, FOX_STEPS + n)
            for kb in range(2):
                mm = pe.transpose(bank[6][:, kb * P:(kb + 1) * P], xprob[:, n % 3, kb * P:(kb + 1) * P], ident[:])
            mm.then_inc(att_t, 1)

        def outputs(h):
            pe.wait_ge(att_tc, FOX_STEPS + 4 * h + 4)
            for i in range(2):
                m = 2 * h + i
                if h < 2:
                    pe.wait_ge(taken, Q.rbase + 4 + m + 1)
                else:
                    pe.wait_ge(xo_lo_ready, m - 3)
                for kb in range(2):
                    mm = pe.matmul(bank[m % 4][:], vx[:, kb, m * P:(m + 1) * P], xprobT[:, h % 2, kb, :],
                                   start=kb == 0, stop=kb == 1)
                mm.then_inc(att_o, 1)

        for u in range(4):
            project_unit(pe, Q, 0, u, xg_hi, xg_lo, (xg_lo_ready, split_count(8)))
            if u == 0:
                pe_norm_sum(pe, 8)
        pe_query_squares(pe, 0)
        for n in range(X_SLOTS):
            if cross_unit(n) is not None:
                project_unit(pe, Q, cross_unit(n) // 4, cross_unit(n) % 4, xg_hi, xg_lo)
            if n < X_STEPS:
                scores(n)
            if cross_norm(n - 1) is not None:
                pe_query_squares(pe, cross_norm(n - 1))
            if 0 <= n - 2 < X_STEPS:
                transposes(n - 2)
            if cross_out(n - 1) is not None:
                outputs(cross_out(n - 1))
        pe_project(pe, O, o_hi, o_lo, (xo_lo_ready, 0))

    def dve_cross(dve):
        Q = layers["xq"]

        def q_tile(u):
            dve.wait_ge(unit_used, Q.base + u + 1)
            dve.tensor_tensor(qx[:, u, :], bank[u % 4][:], rstd[:], ALU.mult).then_inc(taken, 1)

        def row_max(n):
            dve.wait_ge(att_s, FOX_STEPS + n + 1)
            dve_chain(dve, dve.reduce_max(xa_m[:, n:n + 1], bank[4 + n % 2][:, 0:NMEM], AX.X, negate=True))
            dve.tensor_scalar(xa_m[:, n:n + 1], xa_m[:, n:n + 1], xa_r[:, n:n + 1], None, ALU.mult).then_inc(att_nmax, 1)

        def scale(n):
            dve.wait_ge(att_exp, FOX_STEPS + n + 1)
            dve_chain(dve, dve.reciprocal(xa_l[:, n:n + 1], xa_l[:, n:n + 1]))
            dve.tensor_scalar(xprob[:, n % 3, :], xprob[:, n % 3, :], xa_l[:, n:n + 1], None, ALU.mult).then_inc(att_p, 1)

        for u in range(4):
            q_tile(u)
        dve_query_rms(dve, 0)
        for n in range(X_SLOTS + 1):
            if n < X_STEPS:
                row_max(n)
            if cross_unit(n) is not None:
                q_tile(cross_unit(n))
            if 0 <= n - 1 < X_STEPS:
                scale(n - 1)
            if cross_norm(n - 2) is not None:
                dve_query_rms(dve, cross_norm(n - 2))
            if cross_out(n - 2) is not None:
                for i in range(2):
                    m = 2 * cross_out(n - 2) + i
                    dve.wait_ge(xo_hi_ready, m + 1)
                    dve.tensor_tensor(o_lo[:, m, :], bank[m % 4][:], f32(o_hi[:, m, :]), ALU.subtract).then_inc(xo_lo_ready, 1)

    def act_cross(act):
        Q = layers["xq"]

        def exps(n):
            act.wait_ge(att_nmax, FOX_STEPS + n + 1)
            if n >= 3:
                act.wait_ge(att_t, FOX_STEPS + n - 2)
            act.activation(xprob[:, n % 3, :], bank[4 + n % 2][:, 0:NMEM], ACT.Exp, bias=xa_m[:, n:n + 1],
                           scale=xa_r[:, n:n + 1], accum_out=xa_l[:, n:n + 1]).then_inc(att_exp, 1)

        def copies(n):
            h, qi = n // 4, n % 4
            act.wait_ge(att_t, FOX_STEPS + n + 1)
            if h >= 2:
                act.wait_ge(att_o, FOX_STEPS + 2 * (h - 1))
            act.activation(xprobT[:, h % 2, :, qi * P:(qi + 1) * P], bank[6][:, 0:2 * P].rearrange("p (k t) -> p k t", t=P),
                           ACT.Copy).then_inc(att_tc, 1)

        def split(u):
            split_hi(act, Q, u // 4, u % 4 + AHEAD)
        for u in range(4):
            split(u)
            if u in (1, 2):
                act_head_square(act, "q", u - 1)
        act_query_std(act, 0)
        for n in range(X_SLOTS + 1):
            if cross_unit(n) is not None:
                split(cross_unit(n))
            if cross_norm(n) is not None:
                act_head_square(act, "q", 2 * cross_norm(n))
                act_head_square(act, "q", 2 * cross_norm(n) + 1)
            if n < X_STEPS:
                exps(n)
            if 0 <= n - 2 < X_STEPS:
                copies(n - 2)
            if cross_norm(n - 1) is not None:
                act_query_std(act, cross_norm(n - 1))
            if cross_out(n - 2) is not None:
                for i in range(2):
                    m = 2 * cross_out(n - 2) + i
                    act.wait_ge(att_o, FOX_STEPS + m + 1)
                    act.activation(o_hi[:, m, :], bank[m % 4][:], ACT.Copy).then_inc(xo_hi_ready, 1)

    HEADS = 4
    QFG_TILE = (4, 5, 6, 7, 0, 1, 2, 3, 8, 9, 10, 11)
    LEVELS = [64, 32, 16, 8, 4, 2, 1]
    STEPS = len(LEVELS) + 2
    KD_STEP, QE_STEP = len(LEVELS), len(LEVELS) + 1
    hsc, kdT = sq[:, 0, :], sq[:, 1, :]

    def chunks(ap):
        return ap.rearrange("p (n t) -> p n t", t=P)

    def hg_q(h):
        return hq[:, h, :]

    def hg_b(h):
        return hq[:, 4 + h, :]

    def hg_g(h):
        return hq[:, 8 + h, :]

    def hg_logf(h):
        return (ss, hf_odd)[h % 2][:]

    def act_hg_forget(act, h):
        act.wait_ge(taken, layers["hg_qfg"].rbase + h + 1)
        act.activation(hk[:, h, :], hg_b(h), ACT.Sigmoid, scale=-1.0).then_inc(hg_key, 1)
        buf = hg_logf(h)
        if h >= 2:
            act.wait_ge(hg_cum, 4 * (h - 1))
        act_chain(act, act.activation(buf, hg_b(h), ACT.Abs))
        act_chain(act, act.activation(buf, buf, ACT.Exp, scale=-1.0))
        act.activation(buf, buf, ACT.Ln, bias=1.0).then_inc(hg_ln, 1)

    def act_hg_silu(act, i):
        act.wait_ge(taken, layers["hg_qfg"].rbase + QFG_TILE.index(i) + 1)
        act.activation(hq[:, i, :], hq[:, i, :], ACT.Silu).then_inc(hg_silu, 1)

    def dve_hg_forget(dve, h, half):
        buf = hg_logf(h)
        if half == 0:
            dve.wait_ge(hg_ln, h + 1)
            dve_chain(dve, dve.scalar_tensor_tensor(buf, hg_b(h), 0.0, buf, ALU.min, ALU.subtract))
        for n in (2 * half, 2 * half + 1):
            c = slice(n * P, (n + 1) * P)
            dve.tensor_tensor_scan(hg_b(h)[:, c], ones[:], buf[:, c], 0.0, ALU.mult, ALU.add).then_inc(hg_cum, 1)

    def halves(ap, w):
        v = ap.rearrange("p (k two w) -> p k two w", two=2, w=w)
        return v[:, :, 0, :], v[:, :, 1, :]

    def hg_e(h, l):
        if l % 4 < 2:
            return he[:, l % 2, :]
        if h == 0:
            return merged[:, l % 4, :]
        return hg_q(h - 1) if l % 4 == 2 else hk[:, h - 1, :]

    def dve_hg_difference(dve, h, l):
        e, b = hg_e(h, l), hg_b(h)
        if h == 0 and l == 0:
            dve.wait_ge(hg_cum, 4 * HEADS)
        if l >= 4:
            dve.wait_ge(hg_score, (len(LEVELS) + 1) * h + l - 3)
        elif h:
            dve.wait_ge(hg_score, (len(LEVELS) + 1) * h)
            if l >= 2:
                dve.wait_ge(hg_fac, fac_count(h - 1, QE_STEP))
        if l < KD_STEP:
            w = LEVELS[l]
            b0, b1 = halves(b, w)
            e0, e1 = halves(e, w)
            ref = b0[:, :, w - 1:w].to_broadcast([P, T // (2 * w), w])
            dve.tensor_tensor(e0, ref, b0, ALU.subtract).then_inc(hg_diff, 1)
            dve.tensor_tensor(e1, b1, ref, ALU.subtract).then_inc(hg_diff, 1)
        else:
            last = chunks(b)[:, :, P - 1:P].to_broadcast([P, 4, P])
            dve.tensor_tensor(chunks(e), last, chunks(b), ALU.subtract).then_inc(hg_diff, 1)

    def diff_count(h, l):
        per = 2 * len(LEVELS) + 1
        return per * h + min(2 * (l + 1), per)

    def act_hg_exp(act, h, l):
        act.wait_ge(hg_diff, diff_count(h, l))
        if l == QE_STEP:
            if h:
                act.wait_ge(hg_state, 3 * h)
            act.activation(hdec[:], chunks(hg_b(h))[:, :, P - 1], ACT.Exp).then_inc(hg_dec, 1)
            act.wait_ge(hg_dec, h + 1)
            act.activation(hg_b(h), hg_b(h), ACT.Exp).then_inc(hg_exp, 1)
        else:
            act.activation(hg_e(h, l), hg_e(h, l), ACT.Exp).then_inc(hg_exp, 1)

    def dve_hg_factor(dve, h, l):
        e, k, q = hg_b(h) if l == QE_STEP else hg_e(h, l), hk[:, h, :], hg_q(h)
        dve.wait_ge(hg_exp, STEPS * h + l + 1)
        if h == 0 and l == 0:
            dve.wait_ge(hg_key, HEADS)
            dve.wait_ge(hg_silu, 2 * HEADS)
        if l < KD_STEP:
            w = LEVELS[l]
            (e0, e1), k0, q1 = halves(e, w), halves(k, w)[0], halves(q, w)[1]
            dve.tensor_tensor(e0, e0, k0, ALU.mult).then_inc(hg_fac, 1)
            dve.tensor_tensor(e1, e1, q1, ALU.mult).then_inc(hg_fac, 1)
        elif l == KD_STEP:
            dve.tensor_tensor(e, e, k, ALU.mult).then_inc(hg_fac, 1)
        else:
            dve.tensor_tensor(e, e, q, ALU.mult).then_inc(hg_fac, 1)

    def fac_count(h, l):
        n = len(LEVELS)
        return (2 * n + 2) * h + (2 * (l + 1) if l < n else 2 * n + l - n + 1)

    def pe_hg_scores(pe, h, l):
        n = len(LEVELS) + 1
        s = n * h + l
        if s >= 2:
            pe.wait_ge(hg_sel, s - 1)
        if l < len(LEVELS):
            pe.wait_ge(hg_fac, fac_count(h, l))
            a = b = hg_e(h, l)
        else:
            a, b = hk[:, h, :], hg_q(h)
        for c in range(4):
            cs = slice(c * P, (c + 1) * P)
            mm = pe.matmul(bank[6 + s % 2][:, cs], a[:, cs], b[:, cs], start=True, stop=True)
        mm.then_inc(hg_score, 1)

    def dve_hg_select(dve, h, l):
        s = (len(LEVELS) + 1) * h + l
        if s == 0:
            dve.wait_ge(levels_ready, 1)
            dve.wait_ge(hg_zero, 1)
        if h and l == 0:
            dve.wait_ge(hg_o, h)
        dve.wait_ge(hg_score, s + 1)
        if s:
            dve.wait_ge(hg_sel, s)
        dve.copy_predicated(chunks(hsc), hm[:, l, :].unsqueeze(1).to_broadcast([P, 4, P]),
                            chunks(bank[6 + s % 2][:])).then_inc(hg_sel, 1)

    def pe_hg_keys(pe, h):
        pe.wait_ge(hg_fac, fac_count(h, KD_STEP))
        if h:
            pe.wait_ge(hg_y, h)
        e = hg_e(h, KD_STEP)
        for c in range(4):
            cs = slice(c * P, (c + 1) * P)
            mm = pe.transpose(bank[4][:, cs], e[:, cs], ident[:])
        mm.then_inc(hg_kt, 1)

    def act_hg_keys(act, h):
        act.wait_ge(hg_kt, h + 1)
        if h:
            act.wait_ge(hg_update, h)
        act.activation(kdT, bank[4][:], ACT.Copy).then_inc(hg_ktc, 1)

    def pe_hg_update(pe, h):
        pe.wait_ge(hg_ktc, h + 1)
        if h:
            pe.wait_ge(hg_std, h)
        if h == 0:
            pe.wait_ge(taken, layers["hg_v"].rbase + 4)
        for n in range(3):
            mm = pe.matmul(bank[5][:, n * P:(n + 1) * P], kdT[:, n * P:(n + 1) * P], hv[:, n, h * P:(h + 1) * P],
                           start=True, stop=True)
        mm.then_inc(hg_update, 1)

    def dve_hg_state(dve, h):
        dve.wait_ge(hg_update, h + 1)
        if h:
            dve.wait_ge(hg_o, h)
        dve.wait_ge(hg_dec, h + 1)
        for n in range(3):
            u = bank[5][:, n * P:(n + 1) * P]
            if n == 0:
                dve.tensor_copy(hS[:, 0, :], u).then_inc(hg_state, 1)
            else:
                dve.wait_ge(hg_state, 3 * h + n)
                dve.scalar_tensor_tensor(hS[:, n, :], hS[:, n - 1, :], hdec[:, n:n + 1], u, ALU.mult, ALU.add).then_inc(hg_state, 1)

    def pe_hg_out(pe, h):
        pe.wait_ge(hg_sel, (len(LEVELS) + 1) * (h + 1))
        pe.wait_ge(hg_fac, fac_count(h, QE_STEP))
        pe.wait_ge(hg_state, 3 * h + 3)
        qe = hg_b(h)
        for n in range(4):
            cs = slice(n * P, (n + 1) * P)
            mm = pe.matmul(bank[4][:, cs], hv[:, n, h * P:(h + 1) * P], hsc[:, cs], start=True, stop=n == 0)
            if n:
                mm = pe.matmul(bank[4][:, cs], hS[:, n - 1, :], qe[:, cs], start=False, stop=True)
        mm.then_inc(hg_o, 1)

    def act_hg_square(act, h):
        act.wait_ge(hg_o, h + 1)
        if h:
            act.wait_ge(hg_y, h)
        act.activation(ss[:], bank[4][:], ACT.Square).then_inc(hg_osq, 1)

    def pe_hg_sum(pe, h):
        pe.wait_ge(hg_osq, h + 1)
        pe.matmul(bank[5][:], ones[:], ss[:], start=True, stop=True).then_inc(hg_oss, 1)

    def act_hg_std(act, h):
        act.wait_ge(hg_oss, h + 1)
        act.activation(ss[:], bank[5][:], ACT.Sqrt, bias=eps[:], scale=1.0 / P).then_inc(hg_std, 1)

    def dve_hg_y(dve, h):
        dve.wait_ge(hg_std, h + 1)
        dve_chain(dve, dve.reciprocal(ss[:], ss[:]))
        dve_chain(dve, dve.scalar_tensor_tensor(ss[:], bank[4][:], col("hg_onorm_2"), ss[:], ALU.mult, ALU.mult))
        dve.tensor_tensor(hg_g(h), hg_g(h), ss[:], ALU.mult).then_inc(hg_y, 1)

    def act_hg_split(act, h):
        act.wait_ge(hg_y, h + 1)
        if h == 0:
            L, u, _, _ = triple(0, 1)
            act.wait_ge(unit_used, L.base + u + 3)
        act.activation(y0_hi[:, h, :], hg_g(h), ACT.Copy).then_inc(hg_hi, 1)

    def dve_hg_split(dve, h):
        dve.wait_ge(hg_hi, h + 1)
        dve.tensor_tensor(y0_lo[:, h, :], hg_g(h), f32(y0_hi[:, h, :]), ALU.subtract).then_inc(hg_lo, 1)

    MERGE_UNITS = [(b, p, i) for b, p in ((0, 0), (0, 1), (1, 0), (1, 1), (1, 2), (1, 3)) for i in range(3)]
    SHARE = (5, 5, 4, 4)

    def share(h, place):
        at = sum(SHARE[:h])
        return MERGE_UNITS[at + place] if place < SHARE[h] else None

    def pe_share(pe, unit):
        if unit is not None:
            b, p, i = unit
            pe_merge_gate(pe, b, p, i) if i < 2 else pe_merge_branch(pe, b, p)

    def dve_share(dve, unit):
        if unit is not None:
            b, p, i = unit
            dve_merge_gate(dve, b, p, i) if i < 2 else dve_merge_branch(dve, b, p)

    def act_share_split(act, unit):
        if unit is not None:
            act_merge_split(act, *unit)

    def act_share_gate(act, unit):
        if unit is not None and unit[2] < 2:
            act_merge_gate(act, *unit)

    def pe_hg(pe):
        pe_merge_gate(pe, 0, 2, 1)
        pe_merge_branch(pe, 0, 2)
        pe_triple(pe, 0, 3)
        pe_glu(pe)
        for h in range(HEADS):
            pe_share(pe, share(h, 0))
            if h:
                pe_hg_out(pe, h - 1)
            pe_hg_scores(pe, h, 0)
            pe_hg_scores(pe, h, 1)
            pe_share(pe, share(h, 1))
            if h:
                pe_hg_sum(pe, h - 1)
            pe_hg_scores(pe, h, 2)
            pe_hg_scores(pe, h, 3)
            pe_share(pe, share(h, 2))
            pe_hg_scores(pe, h, 4)
            pe_hg_scores(pe, h, 5)
            pe_share(pe, share(h, 3))
            pe_hg_scores(pe, h, 6)
            pe_hg_scores(pe, h, KD_STEP)
            pe_hg_keys(pe, h)
            pe_share(pe, share(h, 4))
            pe_hg_update(pe, h)
        pe_merge_gate(pe, 2, 0, 0)
        pe_hg_out(pe, HEADS - 1)
        pe_hg_sum(pe, HEADS - 1)
        pe_merge_gate(pe, 2, 0, 1)

    def dve_hg(dve):
        dve_triple(dve, 0, 2)
        dve_triple(dve, 0, 3)
        dve_glu(dve)
        dve_hg_difference(dve, 0, 0)
        dve_hg_difference(dve, 0, 1)
        for h in range(HEADS):
            dve_hg_factor(dve, h, 0)
            dve_hg_factor(dve, h, 1)
            dve_hg_difference(dve, h, 2)
            dve_hg_difference(dve, h, 3)
            dve_share(dve, share(h, 0))
            dve_hg_factor(dve, h, 2)
            dve_hg_factor(dve, h, 3)
            dve_hg_select(dve, h, 0)
            dve_hg_select(dve, h, 1)
            dve_hg_difference(dve, h, 4)
            dve_hg_difference(dve, h, 5)
            dve_share(dve, share(h, 1))
            dve_hg_factor(dve, h, 4)
            dve_hg_factor(dve, h, 5)
            dve_hg_select(dve, h, 2)
            dve_hg_select(dve, h, 3)
            dve_hg_difference(dve, h, 6)
            dve_hg_difference(dve, h, KD_STEP)
            if h:
                dve_hg_y(dve, h - 1)
            dve_share(dve, share(h, 2))
            dve_hg_factor(dve, h, 6)
            dve_hg_factor(dve, h, KD_STEP)
            dve_hg_select(dve, h, 4)
            dve_hg_select(dve, h, 5)
            dve_share(dve, share(h, 3))
            dve_hg_factor(dve, h, QE_STEP)
            dve_hg_select(dve, h, 6)
            dve_hg_select(dve, h, KD_STEP)
            if h + 1 < HEADS:
                dve_hg_difference(dve, h + 1, 0)
                dve_hg_difference(dve, h + 1, 1)
            dve_share(dve, share(h, 4))
            dve_hg_state(dve, h)
        for i in range(HEADS - 1):
            dve_hg_split(dve, i)
        dve_merge_gate(dve, 2, 0, 0)
        dve_hg_y(dve, HEADS - 1)
        dve_hg_split(dve, HEADS - 1)
        dve_merge_gate(dve, 2, 0, 1)

    def act_hg(act):
        act_triple(act, 0, 2)
        act_triple(act, 0, 3)
        act_glu(act)
        act.preload_act_table(ACT.Exp)
        act_hg_exp(act, 0, 0)
        act_hg_exp(act, 0, 1)
        for h in range(HEADS):
            act_share_split(act, share(h, 0))
            act_hg_exp(act, h, 2)
            act_hg_exp(act, h, 3)
            act_share_gate(act, share(h, 0))
            if h:
                act_hg_square(act, h - 1)
            act_share_split(act, share(h, 1))
            act_hg_exp(act, h, 4)
            act_hg_exp(act, h, 5)
            if h:
                act_hg_std(act, h - 1)
            act_share_gate(act, share(h, 1))
            act_share_split(act, share(h, 2))
            act_hg_exp(act, h, 6)
            act_hg_exp(act, h, KD_STEP)
            act_hg_exp(act, h, QE_STEP)
            act_share_gate(act, share(h, 2))
            act_share_split(act, share(h, 3))
            act_share_gate(act, share(h, 3))
            act_hg_keys(act, h)
            if h + 1 < HEADS:
                act_hg_exp(act, h + 1, 0)
                act_hg_exp(act, h + 1, 1)
            act_share_split(act, share(h, 4))
            act_share_gate(act, share(h, 4))
        act_merge_split(act, 2, 0, 0)
        for i in range(HEADS - 1):
            act_hg_split(act, i)
        act_merge_gate(act, 2, 0, 0)
        act_hg_square(act, HEADS - 1)
        act_hg_std(act, HEADS - 1)
        act_merge_split(act, 2, 0, 1)
        act_hg_split(act, HEADS - 1)
        act_merge_gate(act, 2, 0, 1)
        act_merge_split(act, 2, 0, 2)

    @block.sync
    def _(sp):
        sp.dma_start(par[:], io["params"]).then_inc(par_in, 16)
        sp.dma_start(w_stage[:, 0, :], order[0].src(0, 0)).then_inc(w_loaded[0], 16)
        for k in range(KD):
            sp.dma_start(x[:, k, :], io["xT"][k * P:(k + 1) * P, :]).then_inc(x_in[k // 2], 16)
            if k == 3:
                sp.dma_start(w_stage[:, 1, :], order[0].src(0, 1)).then_inc(w_loaded[1], 16)
        for L in order:
            load_layer(sp, L)
            if L.name == "up0":
                sp.dma_start(ident[:], io["c_ident"]).then_inc(ident_in, 16)
                sp_rec(sp)
        L = order[-1]
        for k in range(KD):
            sp.wait_ge(taken, L.rbase + k + 1)
            sp.dma_start(io["outT"][k * P:(k + 1) * P, :], x[:, k, :]).then_inc(out_stored, 16)
        sp.wait_ge(out_stored, 16 * KD)

    @block.gpsimd
    def _(pool):
        pool.memset(ones[:], 1.0).then_inc(ones_set, 1)
        pool.memset(eps[:], EPS).then_inc(ones_set, 1)
        pool.memset(eps2[:], EPS * EPS).then_inc(ones_set, 1)
        pool.memset(gate_w[:], 0.0).then_inc(gate_w_zero, 1)
        for L in order:
            if L.name == "fox_v":
                pool_s5_weights(pool)
            if L.name == "rec_y":
                pool_rec(pool)
            elif L.name == "hg_qfg":
                pool_s5(pool)
            elif L.name not in ("hg_v", "merge01"):
                split_lo(pool, L)

    @block.scalar
    def _(act):
        act.wait_ge(par_in, 16)
        act_softplus(act)
        act.activation(s5v(0), parv("s5_log_dt_2"), ACT.Exp).then_inc(s5_act, 1)
        split_hi(act, order[0], 0, 0)
        for m in range(KD):
            act.wait_ge(x_in[m // 2], 32)
            act.activation(xg_hi[:, m, :], x[:, m, :], ACT.Copy, scale=col("ffn1_norm", m)).then_inc(xg_hi_ready, 1)
            if m % 4 == 3:
                split_hi(act, order[0], 0, 1 + m // 4)
        for m in range(KD):
            act_norm_square(act, 0, m, m % 2)
        act_ffn(act, 0)
        act_residual(act, layers["down0"], 1, gain_of("mix_norm", 0))
        act_s5_coefficients(act)
        act_rec(act)
        act_residual(act, layers["rec_out"], 2, gain_of("ffn2_norm", 0))
        act_ffn(act, 1)
        act_residual(act, layers["down1"], 3, gain_of("ffn1_norm", 1))
        act_ffn(act, 2)
        act_residual(act, layers["down2"], 4, gain_of("mix_norm", 1))
        act_norm_columns(act, 1)
        act_load_sgu(act)
        act_sgu(act)
        act_residual(act, layers["sg_out"], 5, gain_of("ffn2_norm", 1))
        act_ffn(act, 3)
        act_final(act, layers["down3"])
        act_load_mix(act)
        act_mix_a(act)
        act_fox(act)
        act_s5(act)
        act_hg(act)
        act_e(act)
        act_residual(act, layers["w_out"], 8, gain_of("norm_x_2"))
        act_cross(act)
        act_residual(act, layers["xo"], 9, gain_of("norm_ffn_2"))
        act_ffn(act, 4)
        act_residual(act, layers["down4"], None, None)

    @block.vector
    def _(dve):
        dve.wait_ge(par_in, 16)
        dve.memset(ss[:], 0.0).then_inc(ss_added, 1)
        for m in range(KD):
            dve.wait_ge(x_in[m // 2], 32)
            dve.wait_ge(xg_hi_ready, m + 1)
            dve.scalar_tensor_tensor(xg_lo[:, m, :], x[:, m, :], col("ffn1_norm", m), f32(xg_hi[:, m, :]),
                                     ALU.mult, ALU.subtract).then_inc(xg_lo_ready, 1)
        for m in range(KD):
            dve_norm_add(dve, 0, m, m % 2)
        dve_norm_rstd(dve, 0)
        dve_ffn(dve, 0)
        dve_softplus(dve)
        dve_s5_angles(dve)
        dve_residual(dve, layers["down0"], 0.5, 1, gain_of("mix_norm", 0))
        dve_rec(dve)
        dve_residual(dve, layers["rec_out"], 1.0, 2, gain_of("ffn2_norm", 0))
        dve_ffn(dve, 1)
        dve_s5_coefficients(dve)
        dve_residual(dve, layers["down1"], 0.5, 3, gain_of("ffn1_norm", 1))
        dve_ffn(dve, 2)
        dve_residual(dve, layers["down2"], 0.5, 4, gain_of("mix_norm", 1))
        dve_norm_columns(dve, 1)
        dve_sgu(dve)
        dve_residual(dve, layers["sg_out"], 1.0, 5, gain_of("ffn2_norm", 1))
        dve_ffn(dve, 3)
        dve_final(dve, layers["down3"])
        dve_mix_a(dve)
        dve_fox(dve)
        dve_s5(dve)
        dve_z(dve)
        dve_hg(dve)
        dve_e(dve)
        dve.wait_ge(final_step, KD)
        dve_residual(dve, layers["w_out"], 1.0, 8, gain_of("norm_x_2"))
        dve_cross(dve)
        dve_residual(dve, layers["xo"], 1.0, 9, gain_of("norm_ffn_2"))
        dve_ffn(dve, 4)
        dve_residual(dve, layers["down4"], 1.0, None, None)

    @block.tensor
    def _(pe):
        pe.wait_ge(ones_set, 1)
        pe_ffn(pe, 0, 0)
        pe_rec(pe, 1)
        pe_ffn(pe, 1, 2)
        pe_ffn(pe, 2, 3)
        pe_sgu(pe, 4)
        pe_ffn(pe, 3, 5)
        pe_mix_a(pe)
        pe_fox(pe)
        pe_s5(pe)
        pe_hg(pe)
        pe_e(pe)
        pe_cross(pe)
        pe_ffn(pe, 4, 9)

    ctx.close()


def columns(w, order=None):
    k, m = w.shape
    u = w.reshape(k // P, P, m // P, P).transpose(2, 1, 0, 3)
    if order is not None:
        u = u[order]
    return np.ascontiguousarray(u).reshape(m, k)


def token_blocks(w):
    k, m = w.shape
    u = w.reshape(k // P // 2, 2, P, m // T, T).transpose(3, 0, 2, 1, 4)
    return np.ascontiguousarray(u).reshape(-1, UNIT)


def features(v):
    return np.asarray(v).reshape(-1, P).T


def layout(a):
    a = {k: np.asarray(v) for k, v in a.items()}
    out = {"xT": np.ascontiguousarray(a["x"][0].T)}
    cols = []
    for name in PARAMS:
        v = a[name]
        if name in ("fox_qnorm_2", "fox_knorm_2"):
            v = np.tile(v.reshape(-1), 2)
        if name == "s5_log_dt_2":
            v = np.repeat(v.reshape(-1), 64)
        cols.append(features(v))
    out["params"] = np.ascontiguousarray(np.concatenate(cols, axis=1))
    ug = [h * KF + j for j in range(KF) for h in (1, 0)]
    ffn = [(a["ffn1_w_in"][0], a["ffn1_w_out"][0]), (a["ffn2_w_in"][0], a["ffn2_w_out"][0]),
           (a["ffn1_w_in"][1], a["ffn1_w_out"][1]), (a["ffn2_w_in"][1], a["ffn2_w_out"][1]),
           (a["w_gate_up_2"][0], a["w_down_2"][0])]
    for i, (up, down) in enumerate(ffn):
        out[f"w_up{i}"] = columns(up, ug)
        out[f"w_down{i}"] = columns(down)
    a_w = {"gate_a_w": a["rec_gate_a_w"][0], "gate_x_w": a["rec_gate_x_w"][0]}
    for name, w in a_w.items():
        out[name] = np.concatenate([w[s::2].transpose(1, 0, 2).reshape(64, 8 * 64) for s in range(2)])
    w = a["rec_w_in"][0]
    out["rec_r"], out["rec_y"] = columns(w[:, D:]), columns(w[:, :D])
    out["rec_out"] = columns(a["rec_w_out"][0])
    w = a["sg_w_in"][0]
    out["sg_v"], out["sg_u"] = token_blocks(w[:, D:]), columns(w[:, :D])
    out["sg_out"] = columns(a["sg_w_out"][0])
    out["sg_wsT"] = np.ascontiguousarray(a["sg_w_s"][0].transpose(2, 0, 1)).reshape(P, D)
    out["sg_bs"] = np.ascontiguousarray(a["sg_b_s"][0].reshape(1, D))
    w = a["w_in_2"][0]
    part = {}
    at = 0
    for name, n in (("fq", 512), ("fk", 512), ("fv", 512), ("ff", 8), ("su", 512), ("hq", 512), ("hf", 512), ("hi", 512),
                    ("hg", 512), ("gl", 3 * D)):
        part[name] = w[:, at:at + n]
        at += n
    out["fox_qk"] = columns(np.concatenate([part["fq"], part["fk"]], axis=1))
    out["fox_v"], out["hg_v"] = token_blocks(part["fv"]), token_blocks(part["hi"])
    out["ff_w"] = np.ascontiguousarray(part["ff"].reshape(KD, P, 8).transpose(1, 0, 2)).reshape(P, KD * 8)
    out["ff_b"] = a["fox_fbias_2"].reshape(8, 1)
    out["s5_in"] = columns(part["su"])
    out["hg_qfg"] = columns(np.concatenate([part["hf"], part["hq"], part["hg"]], axis=1))
    wb = a["w_branch_2"][0]
    merge = []
    for b in range(3):
        gate = columns(part["gl"][:, b * D:(b + 1) * D]).reshape(4, 2, P, UNIT)
        branch = columns(wb[b * 512:(b + 1) * 512]).reshape(4, 2, P, 512).transpose(0, 2, 1, 3).reshape(4, 1, P, UNIT)
        merge.append(np.concatenate([gate, branch], axis=1))
    glu = np.zeros((4, P, UNIT), np.float32)
    glu[:, :, :UNIT // 2] = columns(a["s5_w_glu_2"][0]).reshape(4, P, UNIT // 2)
    out["merge01"] = np.concatenate([t.reshape(-1, UNIT) for t in (merge[0][2:], glu, merge[0][:2], merge[1])])
    out["merge2"] = merge[2].reshape(-1, UNIT)
    for c in ("re", "im"):
        out[f"s5_b_{c}"] = np.ascontiguousarray(a[f"s5_b_{c}_2"][0].reshape(16, 2, 64, 16).transpose(1, 2, 0, 3)).reshape(P, 256)
        out[f"s5_c_{c}"] = np.ascontiguousarray(a[f"s5_c_{c}_2"][0].reshape(16, 2, 16, 64).transpose(1, 3, 0, 2)).reshape(P, 256)
    for name in ("xk", "xq", "xo", "w_out"):
        out[name] = columns(a[name + "_2"][0])
    out["xv"] = token_blocks(a["xv_2"][0])
    out["memT"] = np.ascontiguousarray(a["mem_2"][0].T)
    def rows(n, width, value):
        return np.repeat(np.eye(n, dtype=np.float32) * np.float32(value), width, axis=1)
    out["c_sel8"] = rows(8, P, 8.0)
    out["c_spread"] = rows(16, 64, 1.0)
    out["c_pack"] = np.zeros((P, 32), np.float32)
    out["c_pack"][np.arange(P), 16 + np.arange(P) // 64] = 1.0
    out["c_iota"] = np.tile(np.arange(T, dtype=np.float32), (P, 1))
    i = np.arange(P)
    out["c_ident"] = np.eye(P, dtype=np.float32)
    out["c_tri"] = (i[:, None] <= i[None, :]).astype(np.float32)
    out["c_causal"] = np.where(i[None, :] <= i[:, None], 0.0, -1e30).astype(np.float32)
    levels = [(i[:, None] // (2 * w) == i[None, :] // (2 * w)) & (i[:, None] % (2 * w) < w) & (i[None, :] % (2 * w) >= w)
              for w in (64, 32, 16, 8, 4, 2, 1)]
    out["c_levels"] = np.stack(levels + [i[:, None] == i[None, :]], axis=1).astype(np.float32).reshape(P, 8 * P)
    return out


def kernel(**inputs):
    import concourse.bacc as bacc
    from concourse.bass_utils import run_bass_kernel_spmd

    nc = bacc.Bacc("TRN2", target_bir_lowering=False, num_devices=1)
    arrays = layout(inputs)
    io = {k: nc.dram_tensor(k, list(v.shape), mybir.dt.from_np(v.dtype), kind="ExternalInput").ap()
          for k, v in arrays.items()}
    io["outT"] = nc.dram_tensor("outT", [D, T], F32, kind="ExternalOutput").ap()
    build(nc, io)
    r = run_bass_kernel_spmd(nc, [arrays], core_ids=[0])
    return np.ascontiguousarray(r.results[0]["outT"].T)[None]
```
